# Optimizing a Trainium2 kernel written in Bass

```python
import math
import jax, jax.numpy as jnp
from jax import lax
import numpy as np

D_MODEL = 1024
BATCH = 1
SEQ = 256
DEPTH = 2

PLE_DIM = 256
ROPE_THETA = 500000.0
NORM_EPS = 1e-6
Q_BLOCK = 128

DA_HEADS = 4
DA_DQK = 64
DA_DV = 2 * DA_DQK
DA_ROT = DA_DQK // 4

SSD_HEADS = 8
SSD_HEADDIM = 64
SSD_DINNER = SSD_HEADS * SSD_HEADDIM
SSD_GROUPS = 2
SSD_DSTATE = 128
SSD_CONV = 4
SSD_CHUNK = 128
SSD_CONV_DIM = SSD_DINNER + 2 * SSD_GROUPS * SSD_DSTATE

GLA_HEADS = 4
GLA_DK = 64
GLA_DV = 128
GLA_GATE_RANK = 16
GLA_GATE_NORMALIZER = 16.0
GLA_CHUNK = 64

DA_WIDTH = DA_HEADS * DA_DV
GLA_WIDTH = GLA_HEADS * GLA_DV
MIX_WIDTH = DA_WIDTH + SSD_DINNER + GLA_WIDTH
D_FF = -(-8 * D_MODEL // (3 * 256)) * 256

IN_SIZES = (
    DA_HEADS * 2 * DA_DQK,
    DA_HEADS * 2 * DA_DQK,
    DA_WIDTH,
    SSD_DINNER,
    SSD_CONV_DIM,
    SSD_HEADS,
    GLA_HEADS * GLA_DK,
    GLA_HEADS * GLA_DK,
    GLA_WIDTH,
    GLA_WIDTH,
    GLA_GATE_RANK,
)
IN_COLS = sum(IN_SIZES)
IN_SPLITS = tuple(int(v) for v in np.cumsum(IN_SIZES)[:-1])


def rms_norm(x, gain):
    xf = x.astype(jnp.float32)
    y = xf * lax.rsqrt(jnp.mean(xf * xf, axis=-1, keepdims=True) + NORM_EPS)
    return (y * gain.astype(jnp.float32)).astype(x.dtype)

def rope_tables(positions):
    inv_freq = ROPE_THETA ** (-jnp.arange(0, DA_ROT, 2, dtype=jnp.float32) / DA_ROT)
    ang = positions.astype(jnp.float32)[..., None] * inv_freq
    return jnp.cos(ang), jnp.sin(ang)

def partial_rope(x, cos, sin):
    half = DA_ROT // 2
    x1 = x[..., :half].astype(jnp.float32)
    x2 = x[..., half:DA_ROT].astype(jnp.float32)
    c = cos[:, :, None, :]
    s = sin[:, :, None, :]
    r1 = (x1 * c - x2 * s).astype(x.dtype)
    r2 = (x2 * c + x1 * s).astype(x.dtype)
    return jnp.concatenate([r1, r2, x[..., DA_ROT:]], axis=-1)

def diff_attention(q, k, v, positions, g_q, g_k, lq1, lk1, lq2, lk2, g_sub, lambda_init):
    B, S = q.shape[:2]
    q = rms_norm(q.reshape(B, S, DA_HEADS * 2, DA_DQK), g_q)
    k = rms_norm(k.reshape(B, S, DA_HEADS * 2, DA_DQK), g_k)
    v = v.reshape(B, S, DA_HEADS, DA_DV)
    cos, sin = rope_tables(positions)
    q = partial_rope(q, cos, sin).reshape(B, S, DA_HEADS, 2, DA_DQK)
    k = partial_rope(k, cos, sin).reshape(B, S, DA_HEADS, 2, DA_DQK)
    lam = (jnp.exp(jnp.sum(lq1.astype(jnp.float32) * lk1.astype(jnp.float32)))
           - jnp.exp(jnp.sum(lq2.astype(jnp.float32) * lk2.astype(jnp.float32)))
           + lambda_init)
    scale = DA_DQK ** -0.5
    n_blk = S // Q_BLOCK
    qb = q.reshape(B, n_blk, Q_BLOCK, DA_HEADS, 2, DA_DQK).transpose(1, 0, 2, 3, 4, 5)
    key_idx = jnp.arange(S)

    def one_block(args):
        qi, bi = args
        s = jnp.einsum('bqhcd,bkhcd->bhcqk', qi, k,
                       preferred_element_type=jnp.float32) * scale
        q_idx = bi * Q_BLOCK + jnp.arange(Q_BLOCK)
        causal = key_idx[None, :] <= q_idx[:, None]
        s = jnp.where(causal, s, -jnp.inf)
        pr = jax.nn.softmax(s, axis=-1)
        attn = pr[:, :, 0] - lam * pr[:, :, 1]
        return jnp.einsum('bhqk,bkhd->bqhd', attn.astype(v.dtype), v)

    out = lax.map(one_block, (qb, jnp.arange(n_blk)))
    out = out.transpose(1, 0, 2, 3, 4).reshape(B, S, DA_HEADS, DA_DV)
    out = rms_norm(out, g_sub) * (1.0 - lambda_init)
    return out.reshape(B, S, DA_WIDTH)

def ssd_mixer(z, xbc, dt_raw, conv_w, conv_b, dt_bias, a_log, d_skip, g_norm):
    B, S = z.shape[:2]
    G, R, P, N, L = SSD_GROUPS, SSD_HEADS // SSD_GROUPS, SSD_HEADDIM, SSD_DSTATE, SSD_CHUNK
    nc = S // L
    xbc = lax.conv_general_dilated(
        xbc, conv_w[:, None, :], window_strides=(1,), padding=[(SSD_CONV - 1, 0)],
        dimension_numbers=('NWC', 'WIO', 'NWC'), feature_group_count=SSD_CONV_DIM) + conv_b
    xbc = jax.nn.silu(xbc)
    xs, bs, cs = jnp.split(xbc, [SSD_DINNER, SSD_DINNER + G * N], axis=-1)
    dt = jax.nn.softplus(dt_raw.astype(jnp.float32) + dt_bias.astype(jnp.float32))
    a = -jnp.exp(a_log.astype(jnp.float32))
    xh = xs.astype(jnp.float32).reshape(B, nc, L, G, R, P)
    xdt = xh * dt.reshape(B, nc, L, G, R)[..., None]
    bm = bs.astype(jnp.float32).reshape(B, nc, L, G, N)
    cm = cs.astype(jnp.float32).reshape(B, nc, L, G, N)
    cum = jnp.cumsum((dt * a).reshape(B, nc, L, G, R), axis=2)
    seg = cum[:, :, :, None] - cum[:, :, None, :]
    causal = jnp.tril(jnp.ones((L, L), dtype=bool))[:, :, None, None]
    decay = jnp.exp(jnp.where(causal, seg, -jnp.inf))
    cb = jnp.einsum('bclgn,bcsgn->bclsg', cm, bm)
    y_diag = jnp.einsum('bclsgr,bcsgrp->bclgrp', cb[..., None] * decay, xdt)
    decay_to_end = jnp.exp(cum[:, :, -1:] - cum)
    states = jnp.einsum('bclgn,bclgrp->bcgrpn', bm, xdt * decay_to_end[..., None])
    chunk_decay = jnp.exp(cum[:, :, -1])

    def step(h, inp):
        st, dec = inp
        return dec[..., None, None] * h + st, h

    h0 = jnp.zeros((B, G, R, P, N), jnp.float32)
    _, prev = lax.scan(step, h0, (states.transpose(1, 0, 2, 3, 4, 5),
                                  chunk_decay.transpose(1, 0, 2, 3)))
    prev = prev.transpose(1, 0, 2, 3, 4, 5)
    y_off = jnp.einsum('bclgn,bcgrpn->bclgrp', cm, prev) * jnp.exp(cum)[..., None]
    y = y_diag + y_off + d_skip.astype(jnp.float32).reshape(G, R)[:, :, None] * xh
    y = y.reshape(B, S, SSD_DINNER) * jax.nn.silu(z.astype(jnp.float32))
    y = rms_norm(y.reshape(B, S, G, SSD_DINNER // G), g_norm.reshape(G, SSD_DINNER // G))
    return y.reshape(B, S, SSD_DINNER).astype(z.dtype)

def gla_mixer(q, k, v, g_out, gate_lr, w_gate2, b_gate, g_norm):
    B, S = q.shape[:2]
    H, DK, DV, L = GLA_HEADS, GLA_DK, GLA_DV, GLA_CHUNK
    nc = S // L
    gk = jax.nn.log_sigmoid((gate_lr @ w_gate2 + b_gate).astype(jnp.float32)) / GLA_GATE_NORMALIZER
    qf = q.astype(jnp.float32).reshape(B, nc, L, H, DK) * (DK ** -0.5)
    kf = k.astype(jnp.float32).reshape(B, nc, L, H, DK)
    vf = v.astype(jnp.float32).reshape(B, nc, L, H, DV)
    bcum = jnp.cumsum(gk.reshape(B, nc, L, H, DK), axis=2)
    q_dec = qf * jnp.exp(bcum)
    k_inv = kf * jnp.exp(-bcum)
    att = jnp.einsum('bclhd,bcshd->bchls', q_dec, k_inv)
    att = jnp.where(jnp.tril(jnp.ones((L, L), dtype=bool)), att, 0.0)
    o_intra = jnp.einsum('bchls,bcshv->bclhv', att, vf)
    k_end = kf * jnp.exp(bcum[:, :, -1:] - bcum)
    states = jnp.einsum('bclhd,bclhv->bchdv', k_end, vf)
    chunk_decay = jnp.exp(bcum[:, :, -1])

    def step(st_prev, inp):
        st, dec = inp
        return dec[..., None] * st_prev + st, st_prev

    s0 = jnp.zeros((B, H, DK, DV), jnp.float32)
    _, prev = lax.scan(step, s0, (states.transpose(1, 0, 2, 3, 4),
                                  chunk_decay.transpose(1, 0, 2, 3)))
    prev = prev.transpose(1, 0, 2, 3, 4)
    o_inter = jnp.einsum('bclhd,bchdv->bclhv', q_dec, prev)
    o = (o_intra + o_inter).reshape(B, S, H, DV)
    o = rms_norm(o, g_norm) * jax.nn.silu(g_out.astype(jnp.float32).reshape(B, S, H, DV))
    return o.reshape(B, S, GLA_WIDTH).astype(q.dtype)

def first_inputs(seed: int = 0) -> dict:
    key = jax.random.key(seed)
    ks = iter(jax.random.split(key, 48))

    def nrm(shape, scale):
        return jax.random.normal(next(ks), shape, jnp.float32) * scale

    def gain(shape):
        return 1.0 + nrm(shape, 0.02)

    x = nrm((BATCH, SEQ, D_MODEL), 1.0)
    p = nrm((DEPTH, BATCH, SEQ, PLE_DIM), 1.0)
    positions = jnp.broadcast_to(jnp.arange(SEQ, dtype=jnp.int32)[None, :], (BATCH, SEQ))
    dt0 = jnp.exp(jax.random.uniform(next(ks), (DEPTH, SSD_HEADS), jnp.float32)
                  * (math.log(0.1) - math.log(0.001)) + math.log(0.001))
    ssd_dt_bias = dt0 + jnp.log(-jnp.expm1(-dt0))
    ssd_a_log = jnp.log(jax.random.uniform(next(ks), (DEPTH, SSD_HEADS), jnp.float32,
                                           minval=1.0, maxval=16.0))
    return {
        'x': x,
        'p': p,
        'positions': positions,
        'attn_norm': gain((DEPTH, D_MODEL)),
        'w_in': nrm((DEPTH, D_MODEL, IN_COLS), D_MODEL ** -0.5),
        'da_q_norm': gain((DEPTH, DA_DQK)),
        'da_k_norm': gain((DEPTH, DA_DQK)),
        'da_lambda_q1': nrm((DEPTH, DA_DQK), 0.1),
        'da_lambda_k1': nrm((DEPTH, DA_DQK), 0.1),
        'da_lambda_q2': nrm((DEPTH, DA_DQK), 0.1),
        'da_lambda_k2': nrm((DEPTH, DA_DQK), 0.1),
        'da_sub_norm': gain((DEPTH, DA_DV)),
        'ssd_conv_w': nrm((DEPTH, SSD_CONV, SSD_CONV_DIM), SSD_CONV ** -0.5),
        'ssd_conv_b': nrm((DEPTH, SSD_CONV_DIM), 0.02),
        'ssd_dt_bias': ssd_dt_bias,
        'ssd_a_log': ssd_a_log,
        'ssd_d': 1.0 + nrm((DEPTH, SSD_HEADS), 0.1),
        'ssd_norm': gain((DEPTH, SSD_DINNER)),
        'gla_w_gate2': nrm((DEPTH, GLA_GATE_RANK, GLA_HEADS * GLA_DK), GLA_GATE_RANK ** -0.5),
        'gla_b_gate': nrm((DEPTH, GLA_HEADS * GLA_DK), 0.02),
        'gla_norm': gain((DEPTH, GLA_DV)),
        'w_out': nrm((DEPTH, MIX_WIDTH, D_MODEL), MIX_WIDTH ** -0.5),
        'ffn_norm': gain((DEPTH, D_MODEL)),
        'w_ffn_gate': nrm((DEPTH, D_MODEL, D_FF), D_MODEL ** -0.5),
        'w_ffn_up': nrm((DEPTH, D_MODEL, D_FF), D_MODEL ** -0.5),
        'w_ffn_down': nrm((DEPTH, D_FF, D_MODEL), D_FF ** -0.5),
        'ple_w_proj': nrm((DEPTH, PLE_DIM, D_MODEL), PLE_DIM ** -0.5),
        'ple_w_gate': nrm((DEPTH, D_MODEL, D_MODEL), D_MODEL ** -0.5),
    }

def first_block(x, p, positions, attn_norm, w_in, da_q_norm, da_k_norm, da_lambda_q1,
              da_lambda_k1, da_lambda_q2, da_lambda_k2, da_sub_norm, ssd_conv_w, ssd_conv_b,
              ssd_dt_bias, ssd_a_log, ssd_d, ssd_norm, gla_w_gate2, gla_b_gate, gla_norm,
              w_out, ffn_norm, w_ffn_gate, w_ffn_up, w_ffn_down, ple_w_proj, ple_w_gate):
    h = x
    for i in range(DEPTH):
        lambda_init = 0.8 - 0.6 * math.exp(-0.3 * i)
        a = rms_norm(h, attn_norm[i])
        proj = a @ w_in[i]
        (da_q, da_k, da_v, ssd_z, ssd_xbc, ssd_dt,
         gla_q, gla_k, gla_v, gla_g, gla_lr) = jnp.split(proj, IN_SPLITS, axis=-1)
        y_da = diff_attention(da_q, da_k, da_v, positions, da_q_norm[i], da_k_norm[i],
                              da_lambda_q1[i], da_lambda_k1[i], da_lambda_q2[i],
                              da_lambda_k2[i], da_sub_norm[i], lambda_init)
        y_ssd = ssd_mixer(ssd_z, ssd_xbc, ssd_dt, ssd_conv_w[i], ssd_conv_b[i],
                          ssd_dt_bias[i], ssd_a_log[i], ssd_d[i], ssd_norm[i])
        y_gla = gla_mixer(gla_q, gla_k, gla_v, gla_g, gla_lr, gla_w_gate2[i],
                          gla_b_gate[i], gla_norm[i])
        mix = jnp.concatenate([y_da, y_ssd.astype(y_da.dtype), y_gla.astype(y_da.dtype)], axis=-1)
        h = h + mix @ w_out[i]
        f = rms_norm(h, ffn_norm[i])
        h = h + (jax.nn.silu(f @ w_ffn_gate[i]) * (f @ w_ffn_up[i])) @ w_ffn_down[i]
        h = h + jax.nn.sigmoid(h @ ple_w_gate[i]) * (p[i] @ ple_w_proj[i])
    return h


GRID_W = 64
CTX_LEN = 256
N_MIXERS = 2
EXPAND = 2
D_INNER = EXPAND * D_MODEL
HG_HEAD_DIM = 128
HG_HEADS = D_INNER // HG_HEAD_DIM
HG_CHUNK = 32
N_HG_LAYERS = (DEPTH + 1) // 2
MLA_NOPE_DIM = 128
MLA_ROPE_DIM = 64
MLA_V_DIM = 128
MLA_HEADS = D_INNER // MLA_V_DIM
MLA_Q_RANK = D_MODEL // 4
MLA_KV_RANK = D_MODEL // 8
MLA_SCALE = (MLA_NOPE_DIM + MLA_ROPE_DIM) ** -0.5
N_MLA_LAYERS = DEPTH // 2
ROPE_THETA_2 = 10000.0
ROPE_AXIS_DIM = MLA_ROPE_DIM // 2


def _rmsnorm(x, g):
    xf = x.astype(jnp.float32)
    y = xf * lax.rsqrt(jnp.mean(xf * xf, axis=-1, keepdims=True) + NORM_EPS)
    return (y * g.astype(jnp.float32)).astype(x.dtype)

def _axial_rope(n_tokens):
    rows = n_tokens // GRID_W
    row = jnp.repeat(jnp.arange(rows, dtype=jnp.float32), GRID_W)
    col = jnp.tile(jnp.arange(GRID_W, dtype=jnp.float32), rows)
    inv = ROPE_THETA_2 ** (-jnp.arange(0, ROPE_AXIS_DIM, 2, dtype=jnp.float32) / ROPE_AXIS_DIM)
    ang = jnp.concatenate([row[:, None] * inv, col[:, None] * inv], axis=-1)
    return jnp.cos(ang), jnp.sin(ang)

def _apply_rope(x, cos, sin):
    half = x.shape[-1] // 2
    x1 = x[..., :half].astype(jnp.float32)
    x2 = x[..., half:].astype(jnp.float32)
    return jnp.concatenate([x1 * cos - x2 * sin, x1 * sin + x2 * cos], axis=-1).astype(x.dtype)

def _hgrn2_scan(q, k, v, log_f, s0):
    B, L, H, _ = q.shape
    DV = v.shape[-1]
    n = L // HG_CHUNK

    def chunks(t):
        return jnp.moveaxis(t.astype(jnp.float32).reshape(B, n, HG_CHUNK, H, t.shape[-1]), 1, 0)

    tri = jnp.tril(jnp.ones((HG_CHUNK, HG_CHUNK), dtype=bool))[None, :, :, None, None]

    def step(S, xs):
        qc, kc, vc, lfc = xs
        b = jnp.cumsum(lfc, axis=1)
        b_last = b[:, -1]
        o_inter = jnp.einsum('bthk,bhkv->bthv', qc * jnp.exp(b), S)
        decay = jnp.exp(jnp.where(tri, b[:, :, None] - b[:, None, :], -jnp.inf))
        scores = jnp.einsum('bthk,btshk,bshk->bhts', qc, decay, kc)
        o_intra = jnp.einsum('bhts,bshv->bthv', scores, vc)
        S_new = jnp.exp(b_last)[..., None] * S + jnp.einsum(
            'bshk,bshv->bhkv', kc * jnp.exp(b_last[:, None] - b), vc)
        return S_new, o_inter + o_intra

    S, o = lax.scan(step, s0, (chunks(q), chunks(k), chunks(v), chunks(log_f)))
    return jnp.moveaxis(o, 0, 1).reshape(B, L, H, DV), S

def _hgrn2_bidir(q, v, gates, init_states):
    (k_f, lf_f), (k_b, lf_b) = gates
    rev = lambda t: jnp.flip(t, axis=1)
    o_f, s_f = _hgrn2_scan(q, k_f, v, lf_f, init_states[0])
    o_b, s_b = _hgrn2_scan(rev(q), rev(k_b), rev(v), rev(lf_b), init_states[1])
    return o_f + rev(o_b), (s_f, s_b)

def _hgrn2_mixer(h_lat, h_ctx, w_in, lb, o_gain, w_out):
    def project(h):
        B, L, _ = h.shape
        heads = lambda t: t.reshape(B, L, HG_HEADS, HG_HEAD_DIM)
        q, i_in, f_fw, f_bw, z = jnp.split(h @ w_in, 5, axis=-1)
        gates = []
        for d, g in enumerate((f_fw, f_bw)):
            lbd = lb[d]
            gf = g.astype(jnp.float32)
            log_f = jnp.logaddexp(jnp.log(lbd), jnp.log1p(-lbd) + jax.nn.log_sigmoid(gf))
            k = (1.0 - lbd) * jax.nn.sigmoid(-gf)
            gates.append((heads(k), heads(log_f)))
        return heads(jax.nn.silu(q)), heads(i_in), gates, z

    def readout(o, z):
        B, L = o.shape[:2]
        o = _rmsnorm(o, o_gain).reshape(B, L, D_INNER).astype(z.dtype)
        return (o * jax.nn.silu(z)) @ w_out

    Bsz = h_lat.shape[0]
    s0 = jnp.zeros((Bsz, HG_HEADS, HG_HEAD_DIM, HG_HEAD_DIM), jnp.float32)
    q_c, v_c, gates_c, z_c = project(h_ctx)
    o_c, ctx_states = _hgrn2_bidir(q_c, v_c, gates_c, (s0, s0))
    q_l, v_l, gates_l, z_l = project(h_lat)
    o_l, _ = _hgrn2_bidir(q_l, v_l, gates_l, ctx_states)
    return readout(o_l, z_l), readout(o_c, z_c)

def _attend(q_nope, q_pe, k_nope, k_pe, v):
    s = (jnp.einsum('bqhd,bkhd->bhqk', q_nope, k_nope, preferred_element_type=jnp.float32)
         + jnp.einsum('bqhr,bkr->bhqk', q_pe, k_pe, preferred_element_type=jnp.float32))
    p = jax.nn.softmax(s * MLA_SCALE, axis=-1)
    return jnp.einsum('bhqk,bkhd->bqhd', p.astype(v.dtype), v)

def _blocked_attend(q_nope, q_pe, k_nope, k_pe, v):
    B, L, H, _ = q_nope.shape
    n = L // Q_BLOCK
    blk = lambda t: jnp.moveaxis(t.reshape(B, n, Q_BLOCK, H, t.shape[-1]), 1, 0)
    o = lax.map(lambda qs: _attend(qs[0], qs[1], k_nope, k_pe, v), (blk(q_nope), blk(q_pe)))
    return jnp.moveaxis(o, 0, 1).reshape(B, L, H, v.shape[-1])

def _mla_mixer(h_lat, h_ctx, w_in, qa_norm, w_qb, kva_norm, w_kvb, w_out, cos, sin, need_ctx):
    splits = [MLA_Q_RANK, MLA_Q_RANK + MLA_KV_RANK, MLA_Q_RANK + MLA_KV_RANK + MLA_ROPE_DIM]

    def queries(q_a):
        B, L, _ = q_a.shape
        q = (_rmsnorm(q_a, qa_norm) @ w_qb).reshape(B, L, MLA_HEADS, MLA_NOPE_DIM + MLA_ROPE_DIM)
        return q[..., :MLA_NOPE_DIM], q[..., MLA_NOPE_DIM:]

    def keys_values(kv_a):
        B, L, _ = kv_a.shape
        kv = (_rmsnorm(kv_a, kva_norm) @ w_kvb).reshape(B, L, MLA_HEADS, MLA_NOPE_DIM + MLA_V_DIM)
        return kv[..., :MLA_NOPE_DIM], kv[..., MLA_NOPE_DIM:]

    def readout(o, z):
        B, L = o.shape[:2]
        return (o.reshape(B, L, D_INNER) * jax.nn.silu(z)) @ w_out

    q_a, kv_a, k_pe, z = jnp.split(h_lat @ w_in, splits, axis=-1)
    q_nope, q_pe = queries(q_a)
    q_pe = _apply_rope(q_pe, cos[None, :, None, :], sin[None, :, None, :])
    k_pe = _apply_rope(k_pe, cos[None], sin[None])
    k_nope, v = keys_values(kv_a)

    if need_ctx:
        qc_a, kvc_a, kc_pe, z_c = jnp.split(h_ctx @ w_in, splits, axis=-1)
    else:
        kvc_a, kc_pe = jnp.split(h_ctx @ w_in[:, splits[0]:splits[2]], [MLA_KV_RANK], axis=-1)
    kc_nope, v_c = keys_values(kvc_a)

    o_lat = _blocked_attend(q_nope, q_pe,
                            jnp.concatenate([kc_nope, k_nope], axis=1),
                            jnp.concatenate([kc_pe, k_pe], axis=1),
                            jnp.concatenate([v_c, v], axis=1))
    y_lat = readout(o_lat, z)
    y_ctx = None
    if need_ctx:
        qc_nope, qc_pe = queries(qc_a)
        y_ctx = readout(_attend(qc_nope, qc_pe, kc_nope, kc_pe, v_c), z_c)
    return y_lat, y_ctx

def second_inputs(seed: int = 0) -> dict:
    key = jax.random.key(seed)
    ks = jax.random.split(key, 20)
    f32 = jnp.float32

    def w(k, shape, fan_in):
        return jax.random.normal(k, shape, f32) * fan_in ** -0.5

    def gain(k, shape):
        return 1.0 + 0.1 * jax.random.normal(k, shape, f32)

    mla_in = MLA_Q_RANK + MLA_KV_RANK + MLA_ROPE_DIM + D_INNER
    return {
        "x": jax.random.normal(ks[0], (BATCH, SEQ, D_MODEL), f32),
        "c": jax.random.normal(ks[1], (BATCH, D_MODEL), f32),
        "ctx": jax.random.normal(ks[2], (BATCH, CTX_LEN, D_MODEL), f32),
        "c_ctx": jax.random.normal(ks[3], (D_MODEL,), f32),
        "ada_w": w(ks[4], (DEPTH, D_MODEL, 3 * D_MODEL), D_MODEL),
        "ada_b": 0.02 * jax.random.normal(ks[5], (DEPTH, 3 * D_MODEL), f32),
        "norm_pre": gain(ks[6], (DEPTH, D_MODEL)),
        "norm_post": gain(ks[7], (DEPTH, D_MODEL)),
        "hg_w_in": w(ks[8], (N_HG_LAYERS, D_MODEL, 5 * D_INNER), D_MODEL),
        "hg_lb_logits": jax.random.normal(ks[9], (N_HG_LAYERS, 2, D_INNER), f32),
        "hg_o_norm": gain(ks[10], (N_HG_LAYERS, HG_HEAD_DIM)),
        "hg_w_out": w(ks[11], (N_HG_LAYERS, D_INNER, D_MODEL), D_INNER),
        "mla_w_in": w(ks[12], (N_MLA_LAYERS, D_MODEL, mla_in), D_MODEL),
        "mla_qa_norm": gain(ks[13], (N_MLA_LAYERS, MLA_Q_RANK)),
        "mla_w_qb": w(ks[14], (N_MLA_LAYERS, MLA_Q_RANK, MLA_HEADS * (MLA_NOPE_DIM + MLA_ROPE_DIM)), MLA_Q_RANK),
        "mla_kva_norm": gain(ks[15], (N_MLA_LAYERS, MLA_KV_RANK)),
        "mla_w_kvb": w(ks[16], (N_MLA_LAYERS, MLA_KV_RANK, MLA_HEADS * (MLA_NOPE_DIM + MLA_V_DIM)), MLA_KV_RANK),
        "mla_w_out": w(ks[17], (N_MLA_LAYERS, D_INNER, D_MODEL), D_INNER),
    }

def second_block(x, c, ctx, c_ctx, ada_w, ada_b, norm_pre, norm_post,
              hg_w_in, hg_lb_logits, hg_o_norm, hg_w_out,
              mla_w_in, mla_qa_norm, mla_w_qb, mla_kva_norm, mla_w_kvb, mla_w_out):
    cos, sin = _axial_rope(x.shape[1])
    p = jax.nn.softmax(hg_lb_logits.astype(jnp.float32), axis=0)
    lower_bounds = jnp.cumsum(p, axis=0) - p[0:1]
    silu_c = jax.nn.silu(c)
    silu_cc = jax.nn.silu(c_ctx)
    x_lat, x_ctx = x, ctx
    for i in range(DEPTH):
        need_ctx = i < DEPTH - 1
        j = i // N_MIXERS
        mod_lat = (silu_c @ ada_w[i] + ada_b[i])[:, None, :]
        mod_ctx = silu_cc @ ada_w[i] + ada_b[i]
        sh_l, sc_l, gt_l = jnp.split(mod_lat, 3, axis=-1)
        sh_c, sc_c, gt_c = jnp.split(mod_ctx, 3, axis=-1)
        h_lat = _rmsnorm(x_lat, norm_pre[i]) * (1.0 + sc_l) + sh_l
        h_ctx = _rmsnorm(x_ctx, norm_pre[i]) * (1.0 + sc_c) + sh_c
        if i % N_MIXERS == 0:
            y_lat, y_ctx = _hgrn2_mixer(h_lat, h_ctx, hg_w_in[j], lower_bounds[j],
                                        hg_o_norm[j], hg_w_out[j])
        else:
            y_lat, y_ctx = _mla_mixer(h_lat, h_ctx, mla_w_in[j], mla_qa_norm[j], mla_w_qb[j],
                                      mla_kva_norm[j], mla_w_kvb[j], mla_w_out[j],
                                      cos, sin, need_ctx)
        x_lat = x_lat + gt_l * _rmsnorm(y_lat, norm_post[i])
        if need_ctx:
            x_ctx = x_ctx + gt_c * _rmsnorm(y_ctx, norm_post[i])
    return x_lat


def setup_inputs(seed=0):
    out = dict(first_inputs(seed))
    for name, value in second_inputs(seed + 1).items():
        if name != "x":
            out[name + "_2"] = value
    return out


def reference(
    x, p, positions, attn_norm, w_in, da_q_norm, da_k_norm, da_lambda_q1, da_lambda_k1,
    da_lambda_q2, da_lambda_k2, da_sub_norm, ssd_conv_w, ssd_conv_b, ssd_dt_bias, ssd_a_log,
    ssd_d, ssd_norm, gla_w_gate2, gla_b_gate, gla_norm, w_out, ffn_norm, w_ffn_gate, w_ffn_up,
    w_ffn_down, ple_w_proj, ple_w_gate, c_2, ctx_2, c_ctx_2, ada_w_2, ada_b_2, norm_pre_2,
    norm_post_2, hg_w_in_2, hg_lb_logits_2, hg_o_norm_2, hg_w_out_2, mla_w_in_2, mla_qa_norm_2,
    mla_w_qb_2, mla_kva_norm_2, mla_w_kvb_2, mla_w_out_2,
):
    x = first_block(
        x, p, positions, attn_norm, w_in, da_q_norm, da_k_norm, da_lambda_q1, da_lambda_k1,
        da_lambda_q2, da_lambda_k2, da_sub_norm, ssd_conv_w, ssd_conv_b, ssd_dt_bias, ssd_a_log,
        ssd_d, ssd_norm, gla_w_gate2, gla_b_gate, gla_norm, w_out, ffn_norm, w_ffn_gate,
        w_ffn_up, w_ffn_down, ple_w_proj, ple_w_gate,
    )
    return second_block(
        x, c_2, ctx_2, c_ctx_2, ada_w_2, ada_b_2, norm_pre_2, norm_post_2, hg_w_in_2,
        hg_lb_logits_2, hg_o_norm_2, hg_w_out_2, mla_w_in_2, mla_qa_norm_2, mla_w_qb_2,
        mla_kva_norm_2, mla_w_kvb_2, mla_w_out_2,
    )


_drawn_inputs = setup_inputs


def setup_inputs(seed=0):
    import zlib

    import numpy as np

    out = dict(_drawn_inputs(seed))
    spreads = {}
    factors = {'da_q_norm': 5.827,
     'da_k_norm': 5.687,
     'da_lambda_q1': 3.985,
     'da_lambda_k2': 3.571,
     'da_sub_norm': 5.723,
     'ssd_conv_b': 2.929,
     'ssd_norm': 4.286,
     'gla_b_gate': 8.0,
     'gla_norm': 7.376,
     'ffn_norm': 3.332,
     'mla_qa_norm_2': 28.653,
     'ada_b_2': 8.0,
     'norm_pre_2': 3.695,
     'norm_post_2': 7.349,
     'hg_o_norm_2': 8.0,
     'mla_kva_norm_2': 8.0}
    for name, (base, spread) in spreads.items():
        noise = np.random.default_rng([zlib.crc32(name.encode()), seed]).standard_normal(out[name].shape)
        drawn = base * np.exp(spread * noise) if base else spread * noise
        out[name] = __import__('jax').numpy.asarray(drawn.astype(out[name].dtype))
    for name, factor in factors.items():
        out[name] = (out[name] * factor).astype(out[name].dtype)
    return out
```

```python
import math
from contextlib import ExitStack

import numpy as np
import concourse.bass as bass
from concourse import mybir

P = 128
D = 1024
S = 256
CTX = 256
DEPTH = 2
EPS = 1e-6
NT = S // P
KC = D // P
PLE = 256
DA_H, DQK, DV = 4, 64, 128
HC = DA_H * 2
ROT = DQK // 4
SSD_H, SSD_P, SSD_N = 8, 64, 128
GLA_H, GLA_K, GLA_V, GLA_R = 4, 64, 128, 16
FF = -(-8 * D // (3 * 256)) * 256
FC = FF // P
MIX = 1536
MC = MIX // P
DI = 2 * D
NH = DI // P
PE_D = 64
QR, KVR = D // 4, D // 8
MLA_SCALE = (128 + 64) ** -0.5
C_DAQ, C_DAK, C_DAV, C_Z, C_XBC, C_DT = 0, 512, 1024, 1536, 2048, 3072
C_GQ, C_GV, C_GG, C_LR = 3080, 3592, 4104, 4616
NLEV = 7

CONST_COLS = dict(ident=128, upper=128, chunk_upper=128, causal=256, ones=128, inv_freq=8,
                  ax_cos=NT * 32, ax_sin=NT * 32)


def const_slices():
    at, where = 0, {}
    for name, n in CONST_COLS.items():
        where[name] = (at, at + n)
        at += n
    return where, at


def constants():
    where, width = const_slices()
    c = np.zeros((P, width), np.float32)

    def put(name, value):
        a, b = where[name]
        c[:, a:b] = value

    k, q = np.arange(P)[:, None], np.arange(P)[None, :]
    put("ident", k == q)
    put("upper", k <= q)
    put("chunk_upper", (k <= q) & (k // 64 == q // 64))
    put("causal", np.concatenate([np.zeros((P, P)), np.where(q <= k, 0.0, -1e30)], axis=1))
    put("ones", 1.0)
    put("inv_freq", np.float32(500000.0) ** (-np.arange(0, ROT, 2, dtype=np.float32) / np.float32(ROT)))
    init = [0.8 - 0.6 * math.exp(-0.3 * i) for i in range(DEPTH)]
    lam = np.array([[[v, 1.0 - v]] * P for v in init], np.float32)
    tok = np.arange(S)
    inv = np.float32(10000.0) ** (-np.arange(0, 32, 2, dtype=np.float32) / np.float32(32))
    ang = np.concatenate([(tok // 64).astype(np.float32)[:, None] * inv,
                          (tok % 64).astype(np.float32)[:, None] * inv], axis=1)
    fold = lambda t: t.reshape(NT, P, 32).transpose(1, 0, 2).reshape(P, NT * 32)
    put("ax_cos", fold(np.cos(ang)))
    put("ax_sin", fold(np.sin(ang)))
    m = np.zeros((P, NLEV + 1, P), np.float32)
    for lev in range(NLEV):
        h = 64 >> lev
        m[:, lev] = (k // (2 * h) == q // (2 * h)) & (k // h != q // h)
    m[:, NLEV] = k == q
    return c, m.reshape(P, -1), lam


class Turns:

    def __init__(self, area, filled, free, order):
        self.area, self.filled, self.free = area, filled, free
        self.at = {name: k for k, name in enumerate(order)}
        self.n = len(order)
        assert self.n % 2 == 0 and len(self.at) == self.n

    def buf(self, name):
        p = self.at[name] % 2
        return self.area[:, p * 1024:(p + 1) * 1024]

    def wait_free(self, eng, name, i=0):
        k = self.at[name]
        eng.wait_ge(self.free[k % 2], i * (self.n // 2) + k // 2 + 1)

    def wait_filled(self, eng, name, i=0):
        eng.wait_ge(self.filled, i * self.n + self.at[name] + 1)

    def done(self, ins):
        ins.then_inc(self.filled, 1)

    def release(self, ins, name):
        ins.then_inc(self.free[self.at[name] % 2], 1)


class Ring:

    def __init__(self, slots, ready, free, pieces):
        self.slots, self.ready, self.free = slots, ready, free
        self.names = [p[0] for p in pieces]
        self.at = {n: k for k, n in enumerate(self.names)}
        self.n, self.r = len(pieces), len(ready)
        assert self.n % self.r == 0
        self.dmas = [p[1] for p in pieces]
        self.total = [sum(self.dmas[s::self.r]) for s in range(self.r)]

    def slot(self, name):
        return self.slots[:, self.at[name] % self.r, :]

    def wait_free(self, eng, name, i=0):
        eng.wait_ge(self.free, i * self.n + self.at[name] + 1)

    def loaded(self, dma, name):
        dma.then_inc(self.ready[self.at[name] % self.r], 16)

    def wait_ready(self, eng, name, i=0):
        k = self.at[name]
        s = k % self.r
        eng.wait_ge(self.ready[s], i * (16 * self.total[s]) + 16 * sum(self.dmas[s:k + 1:self.r]))

    def used(self, ins):
        ins.then_inc(self.free, 1)


def program(nc, d, out):
    f32, i32 = mybir.dt.float32, mybir.dt.int32
    ALU, ACT, AX = mybir.AluOpType, mybir.ActivationFunctionType, mybir.AxisListType
    V, A, T, G = nc.vector, nc.scalar, nc.tensor, nc.gpsimd
    ctx = ExitStack()
    with ctx:
        def sb(name, cols, dt=f32):
            return ctx.enter_context(nc.sbuf_tensor(name, [P, cols], dt))

        sems = {}

        def sem(name):
            if name not in sems:
                sems[name] = ctx.enter_context(nc.semaphore(name))
            return sems[name]

        where, n_const = const_slices()
        cst = sb("cst", n_const)
        C = {n: cst[:, a:b] for n, (a, b) in where.items()}
        ident, upper, ones = C["ident"], C["upper"], C["ones"]
        h = sb("h", NT * D)
        h3 = h[:].rearrange("p (t n) -> p t n", t=NT)
        ring = sb("ring", 4 * 4096)
        ring3 = ring[:].rearrange("p (s n) -> p s n", s=4)
        prm = sb("prm", 1712)
        prm2 = sb("prm2", 340)
        work = sb("work", 31800)
        pg = ctx.enter_context(nc.psum_tensor("pg", [P, 2048], f32))
        pm = ctx.enter_context(nc.psum_tensor("pm", [P, 2048], f32))

        class Bump:
            def __init__(self, tile):
                self.tile, self.at = tile, 0

            def take(self, n):
                self.at += n
                assert self.at <= self.tile.shape[1], self.at
                return self.tile[:, self.at - n:self.at]

        bp = Bump(prm)
        p_qkg, p_lam, p_sub = bp.take(2 * DQK), bp.take(4 * DQK), bp.take(DV)
        p_ssdn, p_glan = bp.take(512), bp.take(GLA_V)
        p_dtb, p_alog, p_dskip = bp.take(8), bp.take(8), bp.take(8)
        p_attn, p_ffn = bp.take(KC), bp.take(KC)
        p_convw, p_convb, p_bgate = bp.take(32), bp.take(8), bp.take(2)
        p_wg2, p_li, p_wsm = bp.take(256), bp.take(2), bp.take(KC * 24)
        convw3 = p_convw.rearrange("p (j c) -> p j c", j=4)
        wsm3 = p_wsm.rearrange("p (c n) -> p c n", c=KC)

        b2 = Bump(prm2)
        scc, p_adab, mods = b2.take(2 * KC), b2.take(24), b2.take(DEPTH * 48)
        p_pre, p_post, p_qan, p_kvan = b2.take(DEPTH * KC), b2.take(DEPTH * KC), b2.take(QR // P), b2.take(1)
        g1, gtp = b2.take(2 * KC), b2.take(2 * KC)
        st_a, st_b, st_c, st_m = b2.take(8), b2.take(8), b2.take(8), b2.take(8)
        tot_f, tot_b = b2.take(8), b2.take(8)
        scc3 = scc.rearrange("p (c s) -> p c s", s=2)
        mods4 = mods.rearrange("p (i c s) -> p i c s", i=DEPTH, s=2)

        q3 = lambda ap, a: ap.rearrange("p (a b) -> p a b", a=a)
        w = Bump(work)
        xn, aT = w.take(2048), w.take(2048)
        gu = w.take(FC * S)
        qk, big, sc, at0T = gu[:, 0:2048], gu[:, 2048:4096], gu[:, 4096:5120], gu[:, 5120:5632]
        mixT = w.take(MC * S)
        qT, kTz = mixT[:, 0:1024], mixT[:, 1024:3072]
        dav, sz, sg, gqk, gv = (w.take(1024) for _ in range(5))
        xbc = w.take(8 * 259)
        xc, mix = w.take(2048), w.take(NT * MIX)
        xde, st, bmT = w.take(512), w.take(512), w.take(256)
        gxa = w.take(1024)
        gx, gax, kendT = gxa[:, 0:512], gxa[:, 512:1024], gxa[:, 0:768]
        geb, gei, gqd, gqA, gqB, gkA, gkB = (w.take(512) for _ in range(7))
        pT = w.take(NT * PLE)
        kinvz, gatT, cbm, Sz = xn[:, 0:1024], xn[:, 1024:2048], aT[:, 0:512], aT[:, 512:2048]
        attn = qk[:, 0:1536]
        xh, xdt = xbc[:, 0:1024], xbc[:, 1024:2048]
        at1T = gqk
        ptok, junk = mix[:, 0:512], big
        gqA_to_gkB = work[:, w.at - 2560:w.at - 512]
        qk_jt = qk.rearrange("p (t j n) -> p t j n", t=NT, j=2)
        pp, psig = mix[:, 0:2048], mix[:, 2048:3072]
        sgate = dav
        ss, rstd = w.take(2), w.take(2)
        n_a, n_b, n_c = w.take(32), w.take(32), w.take(32)
        mx, dsum, wgt = w.take(16), w.take(16), w.take(16)
        lam, lamp = w.take(4), sc[:, 768:896]
        dtx, dtl, dta, cum = w.take(16), w.take(16), w.take(16), w.take(16)
        dte, ecum, aneg = w.take(8), w.take(8), w.take(8)
        lrT = sc[:, 512:768]
        cosr, sinr, rtmp = w.take(NT * 8), w.take(NT * 8), sc[:, 0:512]
        posf = w.take(2 * NT)

        xn3, aT3, mixT3, gu3 = q3(xn, NT), q3(aT, KC), q3(mixT, MC), q3(gu, FC)
        mix3, dav3, gv3, sz3, sg3 = (q3(t, NT) for t in (mix, dav, gv, sz, sg))
        qk5 = qk.rearrange("p (t j c e) -> p t j c e", t=NT, j=2, c=HC)
        qT3, kTz4 = q3(qT, 4), kTz.rearrange("p (c r n) -> p c r n", c=4, r=2)
        xbc3, xc3 = q3(xbc, 8), q3(xc, 8)
        gqk3 = q3(gqk, 4)
        Sz5 = Sz.rearrange("p (c a r v) -> p c a r v", c=3, a=2, r=2)
        posi = sb("posi", NT, i32)

        class Event:

            def __init__(self, name, n=1, start=0):
                self.sem, self.n, self.start = sem(name), n, start

            def wait(self, eng, i, k=None):
                eng.wait_ge(self.sem, i * self.n + ((self.n if k is None else k) + self.start))

            def set(self, ins):
                ins.then_inc(self.sem, 1)

        layer_pieces = ([(n, 1) for n in ("daq", "dak", "xbc0", "xbc1", "gqk", "dav", "gv", "z", "gg")]
                        + [(f"ada{a}", 1) for a in range(8)]
                        + [(f"wo{j}", 1) for j in range(MC // 4)]
                        + [(f"gu{j}", 2) for j in range(FC // 2)]
                        + [(f"dn{j}", 1) for j in range(-(-FC // 4))]
                        + [("plep", 1), ("pleg0", 1), ("pleg1", 1)])
        W = Ring(ring3, [sem(f"weights_ready{s}") for s in range(4)], sem("weights_slot_free"), layer_pieces)
        GEMM = Turns(pg, sem("gemm_filled"), [sem("gemm_free0"), sem("gemm_free1")],
                     ["daq", "dak", "xbc0", "xbc1", "gqk", "dav", "gv", "z", "gg", "wo_t0", "wo_t1"]
                     + [f"gu{j}" for j in range(FC // 2)] + ["dn_t0", "dn_t1", "pp_t0", "pp_t1", "pleg0", "pleg1"])
        M = Turns(pm, sem("mixer_psum_filled"), [sem("mixer_psum_free0"), sem("mixer_psum_free1")],
                  ["norm0a", "norm0b", "small", "qT", "kT", "gate", "mod0", "xsT", "bcum", "cb", "modT0", "mod1", "state", "score0",
                   "cumb0", "modT1", "mod2", "score1", "cumb1", "modT2", "mod3", "score2", "modT3", "kendT", "gla_att", "gla_st0", "gla_st1", "attT0", "attT1", "pv",
                   "ydiag", "yoff", "gla_out", "mix0", "mix1", "mix2", "norm1a", "norm1b", "hT_a", "hT_b"])
        loaded_pos = sem("positions_loaded")
        loaded_const, loaded_h = sem("const_loaded"), sem("h_loaded")
        loaded_attn, loaded_prm, loaded_p = sem("attn_norm_loaded"), sem("params_loaded"), sem("p_loaded")
        N_PRM = 24
        tables_done = sem("rope_tables_done")
        sin_in, sin_out = sem("sin_arguments"), sem("sin_done")
        e_ss, e_xn, e_aT, e_h = Event("squares_summed", 2), Event("rows_normed", 2), Event("aT_ready", 3), Event("h_updated", 3, 1)
        e_zero0, e_zero1, e_win = Event("mixer_zeros"), Event("gla_zeros"), Event("w_in_done")
        e_qkin, e_qk, e_xbcin, e_conv, e_xs = Event("qk_in", 2), Event("qk_roped"), Event("xbc_in", 2), Event("conv_done"), Event("conv_silu")
        e_small, e_gqk, e_dav, e_gv, e_sz, e_sg = (Event(n) for n in ("small_in", "gqk_in", "dav_in", "gv_in", "silu_z", "silu_g"))
        e_qT, e_kT = Event("qT_in"), Event("kT_in")
        e_abs, e_ln, e_dta = Event("gate_arguments"), Event("softplus_logs"), Event("dta_ready")
        e_bc, e_gexp, e_gops = Event("gla_cumsums"), Event("gla_exps"), Event("gla_operands")
        e_xh, e_dtx, e_dte, e_xde, e_st = Event("bmT_in"), Event("ssd_decay_arguments"), Event("ssd_decay_exps"), Event("xde_ready"), Event("ssd_state_in")
        e_ux, e_seg, e_segx, e_mt = Event("dta_triangles", 2), Event("segments", 2), Event("segment_exps", 2), Event("ssd_maps", 2)
        e_cbm = Event("cb_masked")
        e_sub, e_sexp, e_attn = Event("scores_shifted", 3), Event("scores_exp", 3), Event("attn_ready", 3)
        e_kendT, e_gat, e_S = Event("kendT_in"), Event("gla_att_masked"), Event("gla_states")
        e_atT, e_mixed, e_mixT = Event("attT_in", 2), Event("mixer_out", 3), Event("mixT_in", 3)
        e_sgate, e_gu = Event("gate_silu", FC // 2), Event("gu_ready", FC // 2)
        e_pp, e_psig, e_pused = Event("p_proj_in", 2), Event("ple_sigmoid", 2), Event("ple_sigmoid_used", 2, 1)
        e_mrow = Event("modulation_rows", 4)
        steps_apart = sem("steps_apart")
        loaded_c, silu_c = sem("c_loaded"), sem("silu_c_done")
        out_done = sem("out_stored")

        ctx.enter_context(nc.allow_non_contiguous_dma(reason="vectors of parameters, one feature per partition"))
        block = ctx.enter_context(nc.Block())
        cols = lambda name, i: d[name][i].rearrange("(c p) -> p c", p=P)

        def rows(name, i):
            return d[name][i].rearrange("(o n) -> o n", o=1).to_broadcast([P, d[name].shape[1]])

        TOK = CTX + S
        TT = TOK // P
        GH = 2
        NG = NH // GH
        J = GH * TT
        w2 = Bump(work)
        hT = w2.take(KC * TOK)
        hT3 = q3(hT, KC)
        oT = w2.take(NH * TOK)
        oT3 = q3(oT, NH)
        raw = w2.take(2 * 5 * 1024)
        raw3 = raw.rearrange("p (b k n) -> p b k n", b=2, k=5)
        gate_sets = (w2.take(6 * 1024), ring[:, 5 * 2048:5 * 2048 + 6 * 1024])
        maps = w2.take(1024)
        states = w2.take(3 * 2 * GH * P)
        states5 = states.rearrange("p (c d a v) -> p c d a v", c=3, d=2, a=GH)
        hmask = w2.take(1024 // 4).bitcast(mybir.dt.uint8)
        gate_tots = ((tot_f, tot_b), (p_lam[:, 32:40], p_lam[:, 40:48]))

        def gate_set(b):
            return [gate_sets[b][:, k * 1024:(k + 1) * 1024] for k in range(6)]

        def kend_transposed(b):
            return gate_sets[b][:, 0:12 * P]

        x2n, xctx = raw[:, 0:4096], raw[:, 4096:6144]
        x2n3, xctx3 = q3(x2n, TT), q3(xctx, NT)
        y2 = raw[:, 0:4096]
        y23 = q3(y2, TT)
        gtb = raw[:, 6144:8192]
        junk2 = raw[:, 6144:10240]
        hring = ring[:, 0:5 * 2048].rearrange("p (s n) -> p s n", s=5)

        w3 = Bump(work)
        w3.take(KC * TOK)
        qnT = q3(hT, NH)
        zT = w3.take(NH * S)
        zT3 = q3(zT, NH)
        knT = w3.take(NH * TOK)
        knT3 = q3(knT, NH)
        vv = w3.take(TT * DI)
        vv3 = q3(vv, TT)
        qpe = w3.take(NT * NH * PE_D)
        qpeT = w3.take(NH // 2 * S)
        kpeT2 = w3.take(2 * TOK)
        kvaT, qaT = w3.take(TOK), w3.take(2 * S)
        gtb2 = w3.take(D)
        qkv = vv[:, 2048:2048 + 2 * 448]
        kvc = vv[:, 4096:4096 + 2 * 192]
        kpe = vv[:, 5120:5120 + TT * P]
        rt = vv[:, 6144:8192]
        x3n, xctx_m = knT[:, 0:4096], vv[:, 0:2048]
        hq_tmp = qpeT
        n_a2, n_b2, n_c2 = p_lam[:, 0:8], p_lam[:, 8:16], p_lam[:, 16:24]
        pr_ = qpe
        prT = work[:, 29696:29696 + 1024]
        y3 = knT[:, 0:2048]

        hg_pieces = [(n, 1) for n in ("gf", "gb", "q", "v", "z")]
        HW = Ring(hring, [sem(f"hg_weights_ready{s}") for s in range(5)], sem("hg_slot_free"), hg_pieces)
        PAIR = [f"{n}{b}" for b in range(2) for n in HW.names]
        HGEMM = Turns(pg, sem("hg_gemm_filled"), [sem("hg_gemm_free0"), sem("hg_gemm_free1")], PAIR)
        HPRE = Turns(pm, sem("hg_pre_filled"), [sem("hg_pre_free0"), sem("hg_pre_free1")], ["n0", "n1", "n2", "n3", "diag", "unused"])
        HM = Turns(pm, sem("hg_psum_filled"), [sem("hg_psum_free0"), sem("hg_psum_free1")],
                   [f"lev{v}" for v in range(NLEV)] + ["keF", "keB", "stF", "stB", "diag", "o", "oT"])
        m_pieces = ([(f"hgo{k}", 1) for k in range(4)] + [("qkv", 1)] + [(f"z{k}", 1) for k in range(4)]
                    + [("qb0", 1), ("qb1", 1), ("kvb", 1)] + [(f"mo{k}", 1) for k in range(4)])
        MW = Ring(ring3, [sem(f"mla_weights_ready{s}") for s in range(4)], sem("mla_slot_free"), m_pieces)
        MGEMM = Turns(pg, sem("mla_gemm_filled"), [sem("mla_gemm_free0"), sem("mla_gemm_free1")],
                      ["y0a", "y0b", "y1a", "y1b", "qkv_l", "qkv_c"] + [f"z{k}" for k in range(4)]
                      + ["qn0", "qn1", "qp0", "qn2", "qn3", "qp1"] + [f"kn{k}" for k in range(8)] + [f"v{k}" for k in range(8)]
                      + ["out_t0", "out_t1"])
        heads_order = ["s0"]
        for k in range(NH):
            heads_order += ([f"s{k + 1}"] if k + 1 < NH else []) + [f"pT{k}", f"o{k}"]
        MM = Turns(pm, sem("mla_psum_filled"), [sem("mla_psum_free0"), sem("mla_psum_free1")],
                   ["gt0", "gt1", "n0", "n1", "n2", "n3", "gt2", "qaT", "kvpe", "qpeT0", "qpeT1", "pad"] + heads_order)
        all_turns = [HGEMM, HPRE, HM, MGEMM, MM]

        loaded_s2, loaded_ctx, loaded_on, loaded_mask, loaded_ctx2 = sem("second_params_loaded"), sem("ctx_loaded"), sem("second_gains_loaded"), sem("masks_loaded"), sem("ctx_loaded_again")
        s2_sq, s2_xn, s2_hT, s2_g = sem("hg_squares"), sem("hg_rows_normed"), sem("hg_input_ready"), sem("hg_done")
        h_q, h_g, h_v, h_z = Event("hg_q_in"), Event("hg_gates_in", 2), Event("hg_v_in"), Event("hg_z_in")
        h_abs, h_ln, h_karg, h_k = Event("hg_abs", 2), Event("hg_logs"), Event("hg_k_arguments"), Event("hg_k_ready")
        h_d, h_x, h_ops = Event("hg_differences", NLEV), Event("hg_exps", NLEV), Event("hg_operands", NLEV)
        h_iarg, h_iexp, h_iops, h_keT = Event("hg_state_arguments"), Event("hg_state_exps"), Event("hg_state_operands"), Event("hg_kendT_in", 2)
        h_S, h_map, h_og, h_oT = Event("hg_states"), Event("hg_maps"), Event("hg_out_normed"), Event("hg_oT_in")
        h_free, h_ks = Event("hg_raw_used", 1, 1), Event("hg_k_summed")
        m_gt, m_gtb, m_y, m_ysq = sem("post_gains"), sem("post_gains_in"), sem("y_in"), sem("y_squares")
        m_x, m_xn, m_hT, m_sq = sem("ctx_updated"), sem("mla_rows_normed"), sem("mla_input_ready"), sem("mla_squares")
        m_qkv, m_qn, m_z = sem("qkv_in"), sem("latents_normed"), sem("mla_z_in")
        m_aT, m_kT = sem("qaT_in"), sem("kva_kpe_in")
        m_qp, m_qpr, m_qpT, m_kn, m_vv = sem("qpe_in"), sem("qpe_roped"), sem("qpeT_in"), sem("heads_in"), sem("mla_v_in")
        m_mx, m_p, m_pn, m_pT, m_o = sem("score_max"), sem("score_exp"), sem("probs_ready"), sem("probsT_in"), sem("mla_out")
        m_yf, m_yfs, m_fin = sem("y_final_in"), sem("y_final_squares"), sem("out_ready")

        hg_w = d["hg_w_in_2"][0].rearrange("(c p) (k g n) -> k g p c n", p=P, k=5, g=NG)
        hg_order = {"q": 0, "v": 1, "gf": 2, "gb": 3, "z": 4}
        tok = lambda ap: ap.rearrange("(t p) n -> p t n", p=P)

        def pairs_loop(eng, body):
            with eng.Fori(0, NG // 2 - 1) as n:
                body(n, True)
            body(NG // 2 - 1, False)

        def second_sp(sp):
            for r in (HW, MW):
                sp.sem_inc(r.free, r.r)
            for t in all_turns:
                for f in t.free:
                    sp.sem_inc(f, 1)
            sp.wait_ge(W.free, W.r + DEPTH * W.n)
            with sp.Fori(0, NG) as g:
                for name in HW.names:
                    HW.wait_free(sp, name, g)
                    sp.sem_inc(steps_apart, 1)
                    HW.loaded(sp.dma_start(HW.slot(name).rearrange("p (c n) -> p c n", c=KC), hg_w[hg_order[name], g]), name)
            sp.wait_ge(HW.free, HW.r + NG * HW.n)

            def piece(name, dst, src):
                MW.wait_free(sp, name)
                MW.loaded(sp.dma_start(dst, src), name)

            c8 = lambda s, n: s[:, 0:KC * n].rearrange("p (c n) -> p c n", c=KC)
            for n in range(2):
                if n == 1:
                    h_oT.wait(sp, NG - 1)
                for k in range(2):
                    name = f"hgo{2 * n + k}"
                    piece(name, c8(MW.slot(name), 512),
                          d["hg_w_out_2"][0, k * D:(k + 1) * D, n * 512:(n + 1) * 512].rearrange("(c p) n -> p c n", p=P))
            win = d["mla_w_in_2"][0].rearrange("(c p) n -> p c n", p=P)
            piece("qkv", c8(MW.slot("qkv"), 448), win[:, :, 0:448])
            for k in range(4):
                piece(f"z{k}", c8(MW.slot(f"z{k}"), 512), win[:, :, 448 + 512 * k:448 + 512 * (k + 1)])
            wqb = d["mla_w_qb_2"][0].rearrange("(c p) n -> p c n", p=P)
            for k in range(2):
                piece(f"qb{k}", MW.slot(f"qb{k}")[:, 0:2 * 1536].rearrange("p (c n) -> p c n", c=2), wqb[:, :, 1536 * k:1536 * (k + 1)])
            piece("kvb", MW.slot("kvb"), d["mla_w_kvb_2"][0])
            wo = d["mla_w_out_2"][0].rearrange("(c p) n -> p c n", p=P)
            for k in range(4):
                piece(f"mo{k}", MW.slot(f"mo{k}").rearrange("p (c n) -> p c n", c=4), wo[:, 4 * k:4 * k + 4, :])
            sp.wait_ge(m_fin, 1)
            sp.dma_start(tok(out[0]), h3).then_inc(out_done, 16)
            sp.wait_ge(out_done, 16)

        def second_pool_early(pool):
            for i in range(DEPTH):
                pool.dma_start(p_pre[:, i * KC:(i + 1) * KC], cols("norm_pre_2", i)).then_inc(loaded_s2, 16)
                pool.dma_start(p_post[:, i * KC:(i + 1) * KC], cols("norm_post_2", i)).then_inc(loaded_s2, 16)
            pool.dma_start(p_qan, cols("mla_qa_norm_2", 0)).then_inc(loaded_s2, 16)
            pool.dma_start(p_kvan, cols("mla_kva_norm_2", 0)).then_inc(loaded_s2, 16)

        def second_pool(pool):
            pool.wait_ge(e_h.sem, 3 * DEPTH + 1)
            pool.dma_start(xctx3, tok(d["ctx_2"][0])).then_inc(loaded_ctx, 16)
            pool.dma_start(p_sub, rows("hg_o_norm_2", 0)).then_inc(loaded_on, 16)
            pool.dma_start(oT[:, 0:(NLEV + 1) * P], d["hmask"]).then_inc(loaded_mask, 16)
            h_free.wait(pool, NG - 1)
            pool.dma_start(q3(xctx_m, NT), tok(d["ctx_2"][0])).then_inc(loaded_ctx2, 16)

        def second_act(act):
            act.wait_ge(e_h.sem, 3 * DEPTH + 1)
            act.wait_ge(loaded_ctx, 16)

            def stream_squares(xc_, jk, sig):
                for t in range(TT):
                    src = (xc_[:, t, :] if t < NT else h3[:, t - NT, :])
                    A.activation(jk[:, t * D:(t + 1) * D], src, ACT.Square, accum_out=st_a[:, t:t + 1])
                act.drain().then_inc(sig, 1)

            stream_squares(xctx3, junk2, s2_sq)

            EVAC = {"q": (0, ACT.Silu, h_q), "gf": (1, ACT.Copy, h_g), "gb": (2, ACT.Copy, h_g), "v": (3, ACT.Copy, h_v), "z": (4, ACT.Silu, h_z)}

            def evac(n, b, name):
                k, func, event = EVAC[name]
                HGEMM.wait_filled(act, f"{name}{b}", n)
                HGEMM.release(A.activation(raw3[:, b, k, :], HGEMM.buf(f"{name}{b}"), func), f"{name}{b}")
                event.set(act.drain())

            def gate_exp(n, b, k):
                h_abs.wait(act, n * 2 + b, k + 1)
                d_ = gate_set(b)[2 + k]
                A.activation(d_, d_, ACT.Exp, scale=-1.0)

            def gate_ln(n, b):
                act.drain()
                for d_ in gate_set(b)[2:4]:
                    A.activation(d_, d_, ACT.Ln, bias=1.0)
                h_ln.set(act.drain())

            def k_exp(n, b):
                h_karg.wait(act, n * 2 + b)
                for k in (1, 2):
                    A.activation(raw3[:, b, k, :], raw3[:, b, k, :], ACT.Exp)
                h_k.set(act.drain())

            def level_exps(n, b, lev):
                h_d.wait(act, n * 2 + b, lev + 1)
                _, _, dF, dB, EQ, EK = gate_set(b)
                v4 = lambda ap: ap.rearrange("p (n h m) -> p n h m", h=2, m=64 >> lev)
                A.activation(v4(EQ)[:, :, 0, :], v4(dB)[:, :, 0, :], ACT.Exp, scale=-1.0)
                A.activation(v4(EQ)[:, :, 1, :], v4(dF)[:, :, 1, :], ACT.Exp)
                A.activation(v4(EK)[:, :, 0, :], v4(dF)[:, :, 0, :], ACT.Exp, scale=-1.0)
                A.activation(v4(EK)[:, :, 1, :], v4(dB)[:, :, 1, :], ACT.Exp)
                h_x.set(act.drain())

            def group(n, b, nxt):
                g = n * 2 + b
                bF, cB, dF, dB, EQ, EK = gate_set(b)
                tF, tB = gate_tots[b]
                hkendT = kend_transposed(b)
                for lev in range(NLEV):
                    if lev > 0:
                        HM.wait_filled(act, f"lev{lev - 1}", g)
                        level_exps(n, b, lev)
                    if nxt and lev == 1:
                        h_free.wait(act, g, 0)
                        evac(*nxt, "gf")
                    if nxt and lev == 2:
                        gate_exp(*nxt, 0)
                    if nxt and lev == 3:
                        evac(*nxt, "gb")
                    if nxt and lev == 4:
                        gate_exp(*nxt, 1)
                        gate_ln(*nxt)
                    if nxt and lev == 5:
                        evac(*nxt, "q")
                    if nxt and lev == 6:
                        k_exp(*nxt)
                h_iarg.wait(act, g)
                for dst, src in ((EQ, EQ), (EK, cB), (dF, bF), (dB, dB), (tF, tF), (tB, tB)):
                    A.activation(dst, src, ACT.Exp)
                h_iexp.set(act.drain())
                if nxt:
                    evac(*nxt, "v")
                for k, name in enumerate(("keF", "keB")):
                    HM.wait_filled(act, name, g)
                    HM.release(A.copy(hkendT[:, k * 768:(k + 1) * 768], HM.buf(name)[:, 0:768]), name)
                    h_keT.set(act.drain())
                if nxt:
                    HM.wait_filled(act, "diag", g)
                    level_exps(*nxt, 0)
                    evac(*nxt, "z")
                HM.wait_filled(act, "oT", g)
                dst = oT.rearrange("p (g n) -> p g n", g=NG)
                dst = dst[:, g, :] if isinstance(n, int) else dst[:, bass.ds(g, 1), :].rearrange("p a n -> p (a n)")
                HM.release(A.copy(dst, HM.buf("oT")), "oT")
                h_oT.set(act.drain())

            evac(0, 0, "gf")
            gate_exp(0, 0, 0)
            evac(0, 0, "gb")
            gate_exp(0, 0, 1)
            gate_ln(0, 0)
            evac(0, 0, "q")
            k_exp(0, 0)
            evac(0, 0, "v")
            HPRE.wait_filled(act, "diag")
            level_exps(0, 0, 0)
            evac(0, 0, "z")

            def body(n, more):
                group(n, 0, (n, 1))
                group(n, 1, (n + 1, 0) if more else None)

            pairs_loop(act, body)

            act.wait_ge(m_gt, 1)
            for s in range(2):
                MM.wait_filled(act, f"gt{s}")
                MM.release(A.copy(gtb[:, s * D:(s + 1) * D], MM.buf(f"gt{s}")), f"gt{s}")
                act.drain().then_inc(m_gtb, 1)
            for n in range(2):
                for k, c in enumerate("ab"):
                    name = f"y{n}{c}"
                    MGEMM.wait_filled(act, name)
                    MGEMM.release(A.copy(y23[:, 2 * k:2 * k + 2, n * 512:(n + 1) * 512], q3(MGEMM.buf(name), 2)), name)
            act.drain()
            for t in range(TT):
                A.activation(oT[:, t * D:(t + 1) * D], y23[:, t, :], ACT.Square, accum_out=st_a[:, t:t + 1])
            act.drain().then_inc(m_ysq, 1)

            act.wait_ge(m_x, 1)
            stream_squares(q3(xctx_m, NT), vv[:, 2048:6144], m_sq)
            MM.wait_filled(act, "gt2")
            MM.release(A.copy(gtb2, MM.buf("gt2")), "gt2")
            for name, dst in (("qkv_l", q3(qkv, NT)), ("qkv_c", q3(kvc, NT))):
                MGEMM.wait_filled(act, name)
                MGEMM.release(A.copy(dst, q3(MGEMM.buf(name), NT)[:, :, 0:dst.shape[2]]), name)
                act.drain().then_inc(m_qkv, 1)
            for k in range(4):
                MGEMM.wait_filled(act, f"z{k}")
                MGEMM.release(A.activation(zT[:, k * 1024:(k + 1) * 1024], MGEMM.buf(f"z{k}"), ACT.Silu), f"z{k}")
            act.drain().then_inc(m_z, 1)
            MM.wait_filled(act, "kvpe")
            b = MM.buf("kvpe")
            for r in range(2):
                pr = slice(r * 64, r * 64 + 64)
                last = A.copy(kpeT2[pr, r * TOK:(r + 1) * TOK], b[pr, 512:1024])
            MM.release(A.activation(kvaT, b[:, 0:512], ACT.Copy, scale=p_kvan), "kvpe")
            act.drain().then_inc(m_kT, 1)
            for k in range(2):
                for c in range(2):
                    name = f"qn{2 * k + c}"
                    MGEMM.wait_filled(act, name)
                    MGEMM.release(A.copy(hT[:, (2 * k + c) * 1024:(2 * k + c + 1) * 1024], MGEMM.buf(name)), name)
                name = f"qp{k}"
                MGEMM.wait_filled(act, name)
                MGEMM.release(A.copy(q3(qpe, NT)[:, :, k * 512:(k + 1) * 512], q3(MGEMM.buf(name), NT)), name)
                act.drain().then_inc(m_qp, 1)
            for k in range(8):
                MGEMM.wait_filled(act, f"kn{k}")
                MGEMM.release(A.copy(knT[:, k * 1024:(k + 1) * 1024], MGEMM.buf(f"kn{k}")), f"kn{k}")
            act.drain().then_inc(m_kn, 1)
            for k in range(8):
                MGEMM.wait_filled(act, f"v{k}")
                MGEMM.release(A.copy(vv3[:, k // 2, (k % 2) * 1024:(k % 2 + 1) * 1024], MGEMM.buf(f"v{k}")), f"v{k}")
            act.drain().then_inc(m_vv, 1)
            for k in range(2):
                MM.wait_filled(act, f"qpeT{k}")
                MM.release(A.copy(qpeT[:, k * 1024:(k + 1) * 1024], MM.buf(f"qpeT{k}")), f"qpeT{k}")
            act.drain().then_inc(m_qpT, 1)

            def probs(k):
                act.wait_ge(m_mx, k + 1)
                for t in range(NT):
                    last = A.activation(pr_[:, (k % 2) * 1024 + t * 512:(k % 2) * 1024 + (t + 1) * 512], MM.buf(f"s{k}")[:, t * 512:(t + 1) * 512], ACT.Exp,
                                        bias=st_b[:, (k % 2) * 2 + t:(k % 2) * 2 + t + 1], scale=MLA_SCALE, accum_out=st_c[:, (k % 2) * 2 + t:(k % 2) * 2 + t + 1])
                MM.release(act.drain(), f"s{k}")
                act.drain().then_inc(m_p, 1)

            probs(0)
            for k in range(NH):
                if k + 1 < NH:
                    probs(k + 1)
                MM.wait_filled(act, f"pT{k}")
                MM.release(A.copy(prT, MM.buf(f"pT{k}")), f"pT{k}")
                act.drain().then_inc(m_pT, 1)
            for t in range(NT):
                MGEMM.wait_filled(act, f"out_t{t}")
                A.activation(vv[:, t * D:(t + 1) * D], MGEMM.buf(f"out_t{t}"), ACT.Square, accum_out=st_a[:, t:t + 1])
                act.drain().then_inc(m_yfs, 1)

        def second_pe(pe):
            def mm(out_, lhsT, rhs, first=True, last=True):
                return T.matmul(out_, lhsT, rhs, start=first, stop=last)

            def tr(out_, in_):
                return T.transpose(out_, in_, ident)

            def stream_transposes(turns, src):
                for a, name in enumerate(("n0", "n1", "n2", "n3")):
                    s, f = a // 2, a % 2
                    turns.wait_free(pe, name)
                    for c in range(4):
                        for t in range(NT):
                            last = tr(turns.buf(name)[:, c * S + t * P:c * S + (t + 1) * P], src[:, 2 * s + t, (4 * f + c) * P:(4 * f + c + 1) * P])
                    turns.done(last)

            pe.wait_ge(s2_xn, 1)
            stream_transposes(HPRE, x2n3)
            pe.wait_ge(s2_hT, 1)

            def project(n, b, unit):
                name, half = HW.names[unit // 2], unit % 2
                g = n * 2 + b
                if half == 0:
                    HW.wait_ready(pe, name, g)
                    HGEMM.wait_free(pe, f"{name}{b}", n)
                wt = HW.slot(name).rearrange("p (c n) -> p c n", c=KC)
                o_ = HGEMM.buf(f"{name}{b}")
                if name in ("v", "z"):
                    for j in (2 * half, 2 * half + 1):
                        for c in range(KC):
                            last = mm(o_[:, j * 256:(j + 1) * 256], hT3[:, c, j * P:(j + 1) * P], wt[:, c, :], c == 0, c == KC - 1)
                else:
                    a = half
                    for c in range(KC):
                        last = mm(o_[:, a * 512:(a + 1) * 512], wt[:, c, a * P:(a + 1) * P], hT3[:, c, :], c == 0, c == KC - 1)
                if half:
                    HGEMM.done(last)
                    HW.used(pe.drain())

            def level(n, b, lev):
                g = n * 2 + b
                name = f"lev{lev}"
                EQ, EK = gate_set(b)[4:6]
                h_ops.wait(pe, g, lev + 1)
                HM.wait_free(pe, name, g)
                for j in range(J):
                    cs = slice(j * P, (j + 1) * P)
                    last = mm(HM.buf(name)[:, cs], EK[:, cs], EQ[:, cs])
                HM.done(last)

            def diagonal(n, b, turns, turn):
                h_ks.wait(pe, n * 2 + b)
                h_q.wait(pe, n * 2 + b)
                turns.wait_free(pe, "diag", turn)
                ks = gate_set(b)[5]
                for j in range(J):
                    cs = slice(j * P, (j + 1) * P)
                    last = mm(turns.buf("diag")[:, cs], ks[:, cs], raw3[:, b, 0, cs])
                turns.done(last)

            def out_head(n, hd):
                k, c = hd // KC, hd % KC
                name = f"hgo{2 * n + k}"
                if hd == 0:
                    for ab in "ab":
                        MGEMM.wait_free(pe, f"y{n}{ab}")
                if c == 0:
                    MW.wait_ready(pe, name)
                wt = MW.slot(name).rearrange("p (c n) -> p c n", c=KC)
                for t in range(TT):
                    y_ = f"y{n}{'ab'[t // 2]}"
                    last = mm(MGEMM.buf(y_)[:, (t % 2) * 512:(t % 2 + 1) * 512], oT3[:, hd, t * P:(t + 1) * P], wt[:, c, :], hd == 0, hd == NH - 1)
                    if hd == NH - 1 and t % 2:
                        MGEMM.done(last)
                if c == KC - 1:
                    MW.used(pe.drain())

            FWD, BWD = (0, 1, 2), (1, 0, 3)

            def group(n, b, nxt):
                g = n * 2 + b
                dF, dB, EQ, EK = gate_set(b)[2:6]
                hkendT = kend_transposed(b)
                heads_out = iter(range(NH - GH))

                def between(unit, heads):
                    if nxt:
                        project(*nxt, unit)
                    else:
                        for _ in range(heads):
                            out_head(0, next(heads_out))

                if not nxt:
                    h_z.wait(pe, NG - 1)
                    h_oT.wait(pe, NG - 2)
                for lev in range(NLEV):
                    between(lev, 1)
                    level(n, b, lev)
                between(NLEV, 2)
                between(NLEV + 1, 2)
                v4 = raw3[:, b, 3, :].rearrange("p (t a v) -> p t a v", t=TT, a=GH)
                h_iops.wait(pe, g)
                for name, src, tiles in (("keF", EQ, FWD), ("keB", EK, BWD)):
                    HM.wait_free(pe, name, g)
                    for c, t in enumerate(tiles):
                        for a in range(GH):
                            last = tr(HM.buf(name)[:, (c * GH + a) * P:(c * GH + a + 1) * P], src[:, (a * TT + t) * P:(a * TT + t + 1) * P])
                    HM.done(last)
                h_v.wait(pe, g)
                for k, (name, tiles) in enumerate((("stF", FWD), ("stB", BWD))):
                    h_keT.wait(pe, g, k + 1)
                    HM.wait_free(pe, name, g)
                    for c, t in enumerate(tiles):
                        for a in range(GH):
                            at = (c * GH + a) * P
                            last = mm(HM.buf(name)[:, at:at + P], hkendT[:, k * 768 + at:k * 768 + at + P], v4[:, t, a, :])
                    HM.done(last)
                if nxt:
                    diagonal(*nxt, HM, g)
                else:
                    HM.wait_free(pe, "diag", g)
                    HM.done(tr(HM.buf("diag")[:, 0:P], ident))
                h_map.wait(pe, g)
                h_S.wait(pe, g)
                HM.wait_free(pe, "o", g)
                for t in range(TT):
                    for a in range(GH):
                        o_ = HM.buf("o")[:, (t * GH + a) * P:(t * GH + a + 1) * P]
                        cs = slice((a * TT + t) * P, (a * TT + t + 1) * P)
                        parts = [(maps[:, cs], v4[:, t, a, :])]
                        if t > 0:
                            parts.append((dF[:, cs], states5[:, t - 1, 0, a, :]))
                        if t != 1:
                            parts.append((dB[:, cs], states5[:, {0: 0, 3: 1, 2: 2}[t], 1, a, :]))
                        for k, (l_, r_) in enumerate(parts):
                            last = mm(o_, l_, r_, k == 0, k == len(parts) - 1)
                HM.done(last)
                between(NLEV + 2, 3)
                h_og.wait(pe, g)
                HM.wait_free(pe, "oT", g)
                for a in range(GH):
                    for t in range(TT):
                        last = tr(HM.buf("oT")[:, (a * TT + t) * P:(a * TT + t + 1) * P], EQ[:, (t * GH + a) * P:(t * GH + a + 1) * P])
                HM.done(last)

            for unit in range(2 * HW.n - 4):
                project(0, 0, unit)
            diagonal(0, 0, HPRE, 0)
            for unit in range(2 * HW.n - 4, 2 * HW.n):
                project(0, 0, unit)

            def body(n, more):
                group(n, 0, (n, 1))
                group(n, 1, (n + 1, 0) if more else None)

            pairs_loop(pe, body)

            pe.wait_ge(m_gt, 1)
            dg = maps

            def spread(name):
                MM.wait_free(pe, name)
                for c in range(2):
                    last = mm(MM.buf(name)[:, c * 512:(c + 1) * 512], ones, dg[:, c * 512:(c + 1) * 512])
                MM.done(last)

            spread("gt0")
            pe.wait_ge(m_gt, 2)
            spread("gt1")
            h_oT.wait(pe, NG - 1)
            for hd in range(NH - GH, NH):
                out_head(0, hd)
            for hd in range(NH):
                out_head(1, hd)

            pe.wait_ge(m_xn, 1)
            stream_transposes(MM, q3(x3n, TT))
            pe.wait_ge(m_gt, 3)
            spread("gt2")
            pe.wait_ge(m_hT, 1)
            MW.wait_ready(pe, "qkv")
            wt = MW.slot("qkv")[:, 0:KC * 448].rearrange("p (c n) -> p c n", c=KC)
            for name, t0, lo in (("qkv_l", NT, 0), ("qkv_c", 0, QR)):
                MGEMM.wait_free(pe, name)
                for t in range(NT):
                    for c in range(KC):
                        last = mm(MGEMM.buf(name)[:, t * 512:t * 512 + 448 - lo], hT3[:, c, (t0 + t) * P:(t0 + t + 1) * P], wt[:, c, lo:448],
                                  c == 0, c == KC - 1)
                MGEMM.done(last)
            MW.used(pe.drain())
            for k in range(4):
                name = f"z{k}"
                MW.wait_ready(pe, name)
                MGEMM.wait_free(pe, name)
                wt = MW.slot(name).rearrange("p (c n) -> p c n", c=KC)
                for f in range(4):
                    for c in range(KC):
                        last = mm(MGEMM.buf(name)[:, f * S:(f + 1) * S], wt[:, c, f * P:(f + 1) * P], hT3[:, c, CTX:TOK], c == 0, c == KC - 1)
                MGEMM.done(last)
                MW.used(pe.drain())
            pe.wait_ge(m_qn, 1)
            MM.wait_free(pe, "qaT")
            for c in range(2):
                for t in range(NT):
                    last = tr(MM.buf("qaT")[:, c * S + t * P:c * S + (t + 1) * P], q3(qkv, NT)[:, t, c * P:(c + 1) * P])
            MM.done(last)
            MM.wait_free(pe, "kvpe")
            b = MM.buf("kvpe")
            for t in range(TT):
                src = q3(kvc, NT)[:, t, 0:KVR] if t < NT else q3(qkv, NT)[:, t - NT, QR:QR + KVR]
                tr(b[:, t * P:(t + 1) * P], src)
            for t in range(TT):
                last = tr(b[:, 512 + t * P:512 + (t + 1) * P], q3(kpe, TT)[:, t, :])
            MM.done(last)
            pe.wait_ge(m_aT, 1)
            qa3 = q3(qaT, 2)
            for k in range(2):
                MW.wait_ready(pe, f"qb{k}")
                wt = MW.slot(f"qb{k}")[:, 0:3072].rearrange("p (c h n) -> p c h n", c=2, h=8)
                for q4 in range(2):
                    name = f"qn{2 * k + q4}"
                    MGEMM.wait_free(pe, name)
                    for a in range(4):
                        for c in range(2):
                            last = mm(MGEMM.buf(name)[:, a * S:(a + 1) * S], wt[:, c, 4 * q4 + a, 0:P], qa3[:, c, :], c == 0, c == 1)
                    MGEMM.done(last)
                name = f"qp{k}"
                MGEMM.wait_free(pe, name)
                for t in range(NT):
                    for c in range(2):
                        last = mm(MGEMM.buf(name)[:, t * 512:(t + 1) * 512], qa3[:, c, t * P:(t + 1) * P], wt[:, c, :, P:P + PE_D], c == 0, c == 1)
                MGEMM.done(last)
                MW.used(pe.drain())
            pe.wait_ge(m_kT, 1)
            MW.wait_ready(pe, "kvb")
            wt = MW.slot("kvb").rearrange("p (h n) -> p h n", h=NH)
            for k in range(8):
                MGEMM.wait_free(pe, f"kn{k}")
                for a in range(2):
                    last = mm(MGEMM.buf(f"kn{k}")[:, a * 512:(a + 1) * 512], wt[:, 2 * k + a, 0:P], kvaT)
                MGEMM.done(last)
            for k in range(8):
                MGEMM.wait_free(pe, f"v{k}")
                for a in range(2):
                    h0 = (k % 2) * 8 + a * 4
                    last = mm(MGEMM.buf(f"v{k}")[:, a * 512:(a + 1) * 512], kvaT[:, (k // 2) * P:(k // 2 + 1) * P], wt[:, h0:h0 + 4, P:2 * P])
                MGEMM.done(last)
            MW.used(pe.drain())
            pe.wait_ge(m_qpr, 1)
            for k in range(2):
                MM.wait_free(pe, f"qpeT{k}")
                for c in range(4):
                    for t in range(NT):
                        last = tr(MM.buf(f"qpeT{k}")[:, c * S + t * P:c * S + (t + 1) * P], q3(qpe, NT)[:, t, (4 * k + c) * P:(4 * k + c + 1) * P])
                MM.done(last)
            MM.wait_free(pe, "pad")
            MM.done(tr(MM.buf("pad")[:, 0:P], ident))
            pe.wait_ge(m_qpT, 1)
            pe.wait_ge(m_kn, 1)

            def scores(k):
                MM.wait_free(pe, f"s{k}")
                for t in range(NT):
                    o_ = MM.buf(f"s{k}")[:, t * 512:(t + 1) * 512]
                    mm(o_, qnT[:, k, t * P:(t + 1) * P], knT3[:, k, :], True, False)
                    last = mm(o_, qpeT[:, (k // 2) * S + t * P:(k // 2) * S + (t + 1) * P], kpeT2[:, (k % 2) * TOK:(k % 2 + 1) * TOK], False, True)
                MM.done(last)

            scores(0)
            pe.wait_ge(m_vv, 1)
            for k in range(NH):
                if k + 1 < NH:
                    scores(k + 1)
                pe.wait_ge(m_pn, k + 1)
                MM.wait_free(pe, f"pT{k}")
                p3 = pr_[:, (k % 2) * 1024:(k % 2 + 1) * 1024].rearrange("p (t n) -> p t n", t=NT)
                for c in range(TT):
                    for t in range(NT):
                        last = tr(MM.buf(f"pT{k}")[:, c * S + t * P:c * S + (t + 1) * P], p3[:, t, c * P:(c + 1) * P])
                MM.done(last)
                pe.wait_ge(m_pT, k + 1)
                MM.wait_free(pe, f"o{k}")
                for c in range(TT):
                    last = mm(MM.buf(f"o{k}")[:, 0:S], vv3[:, c, k * P:(k + 1) * P], prT[:, c * S:(c + 1) * S], c == 0, c == TT - 1)
                MM.done(last)
            pe.wait_ge(m_o, NH)
            for t in range(NT):
                MGEMM.wait_free(pe, f"out_t{t}")
            for k in range(4):
                MW.wait_ready(pe, f"mo{k}")
                wt = MW.slot(f"mo{k}").rearrange("p (c n) -> p c n", c=4)
                for c in range(4):
                    hd = 4 * k + c
                    for t in range(NT):
                        for e in range(2):
                            last = mm(MGEMM.buf(f"out_t{t}")[:, e * 512:(e + 1) * 512], zT3[:, hd, t * P:(t + 1) * P], wt[:, c, e * 512:(e + 1) * 512],
                                      hd == 0, hd == NH - 1)
                        if hd == NH - 1:
                            MGEMM.done(last)
                MW.used(pe.drain())

        def second_dve(dve):
            dve.wait_ge(loaded_s2, 16 * (2 * DEPTH + 2))
            dve.wait_ge(loaded_ctx, 16)
            ctx_lat = (1, 0)

            def mod_gains(i):
                V.tensor_scalar(g1, mods4[:, i, 8:16, :].rearrange("p c s -> p (c s)"), 1.0, None, ALU.add)
                dve.drain()
                V.tensor_tensor(g1.rearrange("p (c s) -> p c s", s=2), g1.rearrange("p (c s) -> p c s", s=2),
                                bc(p_pre[:, i * KC:(i + 1) * KC], [KC, 2], 2), ALU.mult)
                V.tensor_tensor(gtp.rearrange("p (c s) -> p c s", s=2), mods4[:, i, 16:24, :],
                                bc(p_post[:, i * KC:(i + 1) * KC], [KC, 2], 2), ALU.mult)
                dve.drain()

            def stream_norm(xc_, dst, sq, sig):
                dve.wait_ge(sq, 1)
                V.tensor_scalar(st_b[:, 0:TT], st_a[:, 0:TT], 1.0 / D, EPS, ALU.mult, ALU.add)
                dve.drain()
                rsqrt(dve, st_c[:, 0:TT], st_b[:, 0:TT], st_m[:, 0:TT])
                for t in range(TT):
                    src = xc_[:, t, :] if t < NT else h3[:, t - NT, :]
                    V.tensor_scalar(dst[:, t, :], src, st_c[:, t:t + 1], None, ALU.mult)
                dve.drain().then_inc(sig, 1)

            def stream_in(turns, i, sig):
                for a, name in enumerate(("n0", "n1", "n2", "n3")):
                    s, f = a // 2, a % 2
                    m_ = ctx_lat[s]
                    turns.wait_filled(dve, name)
                    for c in range(4):
                        k = 4 * f + c
                        last = V.tensor_scalar(hT3[:, k, s * S:(s + 1) * S], turns.buf(name)[:, c * S:(c + 1) * S],
                                               g1[:, 2 * k + m_:2 * k + m_ + 1], mods4[:, i, k, m_:m_ + 1], ALU.mult, ALU.add)
                    turns.release(last, name)
                dve.drain().then_inc(sig, 1)

            mod_gains(0)
            stream_norm(xctx3, x2n3, s2_sq, s2_xn)
            stream_in(HPRE, 0, s2_hT)
            dve.wait_ge(loaded_mask, 16)
            dve.wait_ge(loaded_on, 16)
            V.tensor_copy(hmask, oT[:, 0:(NLEV + 1) * P])
            dve.drain()
            mask3 = hmask.rearrange("p (l n) -> p l n", l=NLEV + 1)
            maps3 = q3(maps, J)

            j3 = lambda ap: q3(ap, J)

            def gate_abs(n, b, k):
                h_g.wait(dve, n * 2 + b, k + 1)
                V.tensor_scalar(gate_set(b)[2 + k].bitcast(i32), raw3[:, b, 1 + k, :].bitcast(i32), 0x7FFFFFFF, None, ALU.bitwise_and)
                h_abs.set(dve.drain())

            def gate_logs(n, b):
                h_ln.wait(dve, n * 2 + b)
                for k in range(2):
                    V.scalar_tensor_tensor(gate_set(b)[4 + k], raw3[:, b, 1 + k, :], 0.0, gate_set(b)[2 + k], ALU.min, ALU.subtract)
                dve.drain()

            def k_arguments(n, b):
                for k in range(2):
                    V.tensor_tensor(raw3[:, b, 1 + k, :], gate_set(b)[4 + k], raw3[:, b, 1 + k, :], ALU.subtract)
                h_karg.set(dve.drain())

            def running_decays(b):
                bF, cB, _, _, EQ, EK = gate_set(b)
                for src, dst in ((EQ, bF), (EK, cB)):
                    for j in range(J):
                        cs = slice(j * P, (j + 1) * P)
                        V.tensor_tensor_scan(dst[:, cs], ones, src[:, cs], 0.0, ALU.mult, ALU.add)
                dve.drain()
                V.tensor_copy(gate_tots[b][0], j3(bF)[:, :, P - 1])
                V.tensor_copy(gate_tots[b][1], j3(cB)[:, :, P - 1])
                dve.drain()
                V.tensor_tensor(cB, cB, EK, ALU.subtract)
                dve.drain()

            def k_sum(n, b):
                h_k.wait(dve, n * 2 + b)
                V.tensor_tensor(gate_set(b)[5], raw3[:, b, 1, :], raw3[:, b, 2, :], ALU.add)
                h_ks.set(dve.drain())

            def differences(b, lev):
                bF, cB, dF, dB, _, _ = gate_set(b)
                m = 64 >> lev
                v4 = lambda ap: ap.rearrange("p (n h m) -> p n h m", h=2, m=m)
                v3 = lambda ap: ap.rearrange("p (n k) -> p n k", k=2 * m)
                nb = 1024 // (2 * m)
                V.tensor_tensor(v3(dF), v3(bF), v4(bF)[:, :, 0, m - 1:m].to_broadcast([P, nb, 2 * m]), ALU.subtract)
                V.tensor_tensor(v3(dB), v3(cB), v4(cB)[:, :, 1, 0:1].to_broadcast([P, nb, 2 * m]), ALU.subtract)
                h_d.set(dve.drain())

            def keep(lev, turns, name, turn):
                turns.wait_filled(dve, name, turn)
                dve.sem_inc(steps_apart, 1)
                turns.release(V.copy_predicated(maps3, bc(mask3[:, lev, :], [J, P], 1), j3(turns.buf(name))), name)

            def group(n, b, nxt):
                g = n * 2 + b
                q_, kf, kb, v_, z_ = (raw3[:, b, k, :] for k in range(5))
                bF, cB, dF, dB, EQ, EK = gate_set(b)
                tF, tB = gate_tots[b]
                h_q.wait(dve, g)
                for lev in range(NLEV):
                    v4 = lambda ap: ap.rearrange("p (n h m) -> p n h m", h=2, m=64 >> lev)
                    h_x.wait(dve, g, lev + 1)
                    V.tensor_tensor(EQ, EQ, q_, ALU.mult)
                    V.tensor_tensor(v4(EK)[:, :, 0, :], v4(EK)[:, :, 0, :], v4(kf)[:, :, 0, :], ALU.mult)
                    V.tensor_tensor(v4(EK)[:, :, 1, :], v4(EK)[:, :, 1, :], v4(kb)[:, :, 1, :], ALU.mult)
                    h_ops.set(dve.drain())
                    if lev + 1 < NLEV:
                        differences(b, lev + 1)
                    keep(lev, HM, f"lev{lev}", g)
                    if nxt and lev == 1:
                        gate_abs(*nxt, 0)
                    if nxt and lev == 3:
                        gate_abs(*nxt, 1)
                    if nxt and lev == 4:
                        gate_logs(*nxt)
                    if nxt and lev == 5:
                        k_arguments(*nxt)
                h_map.set(dve.drain())
                V.tensor_tensor(j3(EQ), bc(tF, [J, P], 2), j3(bF), ALU.subtract)
                V.tensor_tensor(j3(dB), bc(tB, [J, P], 2), j3(cB), ALU.subtract)
                h_iarg.set(dve.drain())
                if nxt:
                    running_decays(nxt[1])
                h_iexp.wait(dve, g)
                V.tensor_tensor(EQ, EQ, kf, ALU.mult)
                V.tensor_tensor(EK, EK, kb, ALU.mult)
                h_iops.set(dve.drain())
                V.tensor_tensor(dF, dF, q_, ALU.mult)
                V.tensor_tensor(dB, dB, q_, ALU.mult)
                if nxt:
                    k_sum(*nxt)
                    differences(nxt[1], 0)
                for k, (name, tiles, tot) in enumerate((("stF", (0, 1, 2), tF), ("stB", (1, 0, 3), tB))):
                    HM.wait_filled(dve, name, g)
                    src = HM.buf(name)[:, 0:768].rearrange("p (c a v) -> p c a v", c=3, a=GH)
                    V.tensor_copy(states5[:, 0, k, :, :], src[:, 0])
                    dve.drain()
                    for c in (1, 2):
                        for a in range(GH):
                            j = a * TT + tiles[c]
                            last = V.scalar_tensor_tensor(states5[:, c, k, a, :], states5[:, c - 1, k, a, :], tot[:, j:j + 1], src[:, c, a, :],
                                                          ALU.mult, ALU.add)
                        if c == 1:
                            dve.drain()
                    HM.release(last, name)
                h_S.set(dve.drain())
                HM.wait_filled(dve, "o", g)
                HM.release(V.tensor_copy(EQ, HM.buf("o")), "o")
                if nxt:
                    keep(NLEV, HM, "diag", g)
                else:
                    HM.wait_filled(dve, "diag", g)
                    HM.release(dve.drain(), "diag")
                dve.drain()
                V.tensor_tensor(EK, EQ, EQ, ALU.mult)
                dve.drain()
                V.tensor_reduce(st_a[:, 0:J], j3(EK), AX.X, ALU.add)
                dve.drain()
                V.tensor_scalar(st_b[:, 0:J], st_a[:, 0:J], 1.0 / P, EPS, ALU.mult, ALU.add)
                dve.drain()
                rsqrt(dve, st_c[:, 0:J], st_b[:, 0:J], st_m[:, 0:J])
                V.tensor_tensor(j3(EQ), j3(EQ), bc(st_c, [J, P], 2), ALU.mult)
                dve.drain()
                V.tensor_tensor(j3(EQ), j3(EQ), bc(p_sub, [J, P], 1), ALU.mult)
                dve.drain()
                h_z.wait(dve, g)
                V.tensor_tensor(EQ, EQ, z_, ALU.mult)
                h_og.set(dve.drain())
                h_free.set(dve.drain())

            gate_abs(0, 0, 0)
            gate_abs(0, 0, 1)
            gate_logs(0, 0)
            k_arguments(0, 0)
            running_decays(0)
            k_sum(0, 0)
            differences(0, 0)
            keep(NLEV, HPRE, "diag", 0)

            def body(n, more):
                group(n, 0, (n, 1))
                group(n, 1, (n + 1, 0) if more else None)

            pairs_loop(dve, body)

            mod_gains_post = gtp.rearrange("p (c s) -> p c s", s=2)

            def diag(s, count):
                V.tensor_tensor(q3(maps, KC), bc(ident, [KC, P], 1), bc(mod_gains_post[:, :, s], [KC, P], 2), ALU.mult)
                dve.drain().then_inc(m_gt, 1)

            diag(ctx_lat[0], 1)
            dve.wait_ge(m_gtb, 1)
            diag(ctx_lat[1], 2)
            dve.wait_ge(m_gtb, 2)
            dve.wait_ge(m_ysq, 1)

            def post(y_t, rstd_col, gain, x_t):
                V.scalar_tensor_tensor(y_t, y_t, rstd_col, gain, ALU.mult, ALU.mult)
                dve.drain()
                V.tensor_tensor(x_t, x_t, y_t, ALU.add)

            dve.wait_ge(loaded_ctx2, 16)
            V.tensor_scalar(st_b[:, 0:TT], st_a[:, 0:TT], 1.0 / D, EPS, ALU.mult, ALU.add)
            dve.drain()
            rsqrt(dve, st_c[:, 0:TT], st_b[:, 0:TT], st_m[:, 0:TT])
            for t in range(TT):
                s = t // NT
                post(y23[:, t, :], st_c[:, t:t + 1], gtb[:, s * D:(s + 1) * D], q3(xctx_m, NT)[:, t, :] if s == 0 else h3[:, t - NT, :])
            dve.drain().then_inc(m_x, 1)

            mod_gains(1)
            diag(ctx_lat[1], 3)
            stream_norm(q3(xctx_m, NT), q3(x3n, TT), m_sq, m_xn)
            stream_in(MM, 1, m_hT)
            dve.wait_ge(m_qkv, 2)
            q_l, kv_c = q3(qkv, NT), q3(kvc, NT)
            parts = [(q_l[:, t, 0:QR], QR) for t in range(NT)] + [(kv_c[:, t, 0:KVR], KVR) for t in range(NT)] + [(q_l[:, t, QR:QR + KVR], KVR) for t in range(NT)]
            for k, (x, n) in enumerate(parts):
                V.tensor_tensor(rt[:, k * 256:k * 256 + n], x, x, ALU.mult)
            dve.drain()
            for k, (x, n) in enumerate(parts):
                V.tensor_reduce(n_a2[:, k:k + 1], rt[:, k * 256:k * 256 + n], AX.X, ALU.add)
            dve.drain()
            for k0, k1, n in ((0, 2, QR), (2, 6, KVR)):
                V.tensor_scalar(n_b2[:, k0:k1], n_a2[:, k0:k1], 1.0 / n, EPS, ALU.mult, ALU.add)
            dve.drain()
            rsqrt(dve, n_c2[:, 0:6], n_b2[:, 0:6], n_a2[:, 0:6])
            for k, (x, n) in enumerate(parts):
                V.tensor_scalar(x, x, n_c2[:, k:k + 1], None, ALU.mult)
            kpe4 = kpe.rearrange("p (t r e) -> p t r e", t=TT, r=2)
            cos3, sin3 = q3(C["ax_cos"], NT), q3(C["ax_sin"], NT)
            for r in range(2):
                V.tensor_copy(kpe4[:, 0:NT, r, :], kv_c[:, :, KVR:KVR + PE_D])
            x1, x2 = q_l[:, :, QR + KVR:QR + KVR + 32], q_l[:, :, QR + KVR + 32:QR + KVR + 64]
            r4 = [q3(rt[:, 1536 + k * 64:1536 + (k + 1) * 64], NT) for k in range(4)]
            for dst, x, cs in ((r4[0], x1, cos3), (r4[1], x2, sin3), (r4[2], x1, sin3), (r4[3], x2, cos3)):
                V.tensor_tensor(dst, x, cs, ALU.mult)
            dve.drain()
            for r in range(2):
                V.tensor_tensor(kpe4[:, NT:TT, r, 0:32], r4[0], r4[1], ALU.subtract)
                V.tensor_tensor(kpe4[:, NT:TT, r, 32:64], r4[2], r4[3], ALU.add)
            MM.wait_filled(dve, "gt2")
            V.memset(kpeT2, 0.0)
            dve.drain().then_inc(m_qn, 1)
            MM.wait_filled(dve, "qaT")
            for c in range(2):
                last = V.tensor_scalar(qaT[:, c * S:(c + 1) * S], MM.buf("qaT")[:, c * S:(c + 1) * S], p_qan[:, c:c + 1], None, ALU.mult)
            MM.release(last, "qaT")
            dve.drain().then_inc(m_aT, 1)
            dve.wait_ge(m_qp, 2)
            for t in range(NT):
                x = qpe[:, t * 1024:(t + 1) * 1024].rearrange("p (a e) -> p a e", a=NH)
                x1, x2 = x[:, :, 0:32], x[:, :, 32:64]
                cs, sn = (bc(v[:, t, :], [NH, 32], 1) for v in (cos3, sin3))
                r4 = [q3(hq_tmp[:, k * 512:(k + 1) * 512], NH) for k in range(4)]
                for dst, x_, c_ in ((r4[0], x1, cs), (r4[1], x2, sn), (r4[2], x1, sn), (r4[3], x2, cs)):
                    V.tensor_tensor(dst, x_, c_, ALU.mult)
                dve.drain()
                V.tensor_tensor(x1, r4[0], r4[1], ALU.subtract)
                V.tensor_tensor(x2, r4[2], r4[3], ALU.add)
                dve.drain()
            dve.drain().then_inc(m_qpr, 1)
            MM.wait_filled(dve, "pad")
            MM.release(dve.drain(), "pad")

            def score_max(k):
                MM.wait_filled(dve, f"s{k}")
                cs = slice((k % 2) * 2, (k % 2) * 2 + 2)
                V.tensor_reduce(st_m[:, cs], q3(MM.buf(f"s{k}"), NT), AX.X, ALU.max)
                dve.drain()
                V.tensor_scalar(st_b[:, cs], st_m[:, cs], -MLA_SCALE, None, ALU.mult)
                dve.drain().then_inc(m_mx, 1)

            dve.wait_ge(m_z, 1)
            score_max(0)
            for k in range(NH):
                if k + 1 < NH:
                    score_max(k + 1)
                dve.wait_ge(m_p, k + 1)
                cs = slice((k % 2) * 2, (k % 2) * 2 + 2)
                V.reciprocal(st_a[:, cs], st_c[:, cs])
                dve.drain()
                for t in range(NT):
                    x = pr_[:, (k % 2) * 1024 + t * 512:(k % 2) * 1024 + (t + 1) * 512]
                    V.tensor_scalar(x, x, st_a[:, (k % 2) * 2 + t:(k % 2) * 2 + t + 1], None, ALU.mult)
                dve.drain().then_inc(m_pn, 1)
                MM.wait_filled(dve, f"o{k}")
                MM.release(V.tensor_tensor(zT3[:, k, :], zT3[:, k, :], MM.buf(f"o{k}")[:, 0:S], ALU.mult), f"o{k}")
                dve.drain().then_inc(m_o, 1)
            for t in range(NT):
                dve.wait_ge(m_yfs, t + 1)
                V.tensor_scalar(st_b[:, t:t + 1], st_a[:, t:t + 1], 1.0 / D, EPS, ALU.mult, ALU.add)
                dve.drain()
                rsqrt(dve, st_c[:, t:t + 1], st_b[:, t:t + 1], st_m[:, t:t + 1])
                y_t = y3[:, t * D:(t + 1) * D]
                V.scalar_tensor_tensor(y_t, MGEMM.buf(f"out_t{t}"), st_c[:, t:t + 1], gtb2, ALU.mult, ALU.mult)
                dve.drain()
                V.tensor_tensor(h3[:, t, :], h3[:, t, :], y_t, ALU.add)
            dve.drain().then_inc(m_fin, 1)


        @block.sync
        def _(sp):
            for s in (W.free,):
                sp.sem_inc(s, W.r)
            for s in GEMM.free + M.free:
                sp.sem_inc(s, 1)
            for e in (e_h, e_pused, h_free):
                sp.sem_inc(e.sem, e.start)
            sp.dma_start(cst[:], d["cst"]).then_inc(loaded_const, 16)
            sp.dma_start(h3, d["x"][0].rearrange("(t p) n -> p t n", p=P)).then_inc(loaded_h, 16)

            def piece(name, i, *parts):
                W.wait_free(sp, name, i)
                for dst, src in parts:
                    W.loaded(sp.dma_start(dst(W.slot(name)), src), name)

            whole8 = lambda s: s.rearrange("p (c n) -> p c n", c=KC)
            whole4 = lambda s: s.rearrange("p (c n) -> p c n", c=4)
            with sp.Fori(0, DEPTH) as i:
                win = d["w_in"][i].rearrange("(c p) n -> p c n", p=P)
                for name, at in (("daq", C_DAQ), ("dak", C_DAK), ("xbc0", C_XBC), ("xbc1", C_XBC + 512), ("gqk", C_GQ),
                                 ("dav", C_DAV), ("gv", C_GV), ("z", C_Z), ("gg", C_GG)):
                    piece(name, i, (whole8, win[:, :, at:at + 512]))
                wa = d["ada_w_2"][i].rearrange("(c p) n -> p c n", p=P)
                for a in range(8):
                    piece(f"ada{a}", i, (lambda s: s[:, 0:KC * 384].rearrange("p (c n) -> p c n", c=KC), wa[:, :, 384 * a:384 * a + 384]))
                wo = d["w_out"][i].rearrange("(c p) n -> p c n", p=P)
                for j in range(MC // 4):
                    piece(f"wo{j}", i, (whole4, wo[:, 4 * j:4 * j + 4, :]))
                wg = d["w_ffn_gate"][i].rearrange("(c p) n -> p c n", p=P)
                wu = d["w_ffn_up"][i].rearrange("(c p) n -> p c n", p=P)
                for j in range(FC // 2):
                    piece(f"gu{j}", i, (lambda s: whole8(s)[:, :, 0:256], wg[:, :, 256 * j:256 * j + 256]),
                          (lambda s: whole8(s)[:, :, 256:512], wu[:, :, 256 * j:256 * j + 256]))
                wd = d["w_ffn_down"][i].rearrange("(c p) n -> p c n", p=P)
                for j in range(-(-FC // 4)):
                    n = min(4, FC - 4 * j)
                    piece(f"dn{j}", i, (lambda s, n=n: whole4(s)[:, 0:n, :], wd[:, 4 * j:4 * j + n, :]))
                wp = d["ple_w_proj"][i].rearrange("(c p) n -> p c n", p=P)
                piece("plep", i, (lambda s: whole4(s)[:, 0:2, :], wp))
                wpg = d["ple_w_gate"][i].rearrange("(c p) n -> p c n", p=P)
                for n in range(2):
                    piece(f"pleg{n}", i, (whole8, wpg[:, :, 512 * n:512 * n + 512]))
            second_sp(sp)

        @block.gpsimd
        def _(pool):
            pool.dma_start(posi[:], d["positions"][0].rearrange("(t p) -> p t", p=P)).then_inc(loaded_pos, 16)
            pool.dma_start(scc3[:, :, 0], d["c_2"][0].rearrange("(c p) -> p c", p=P)).then_inc(loaded_c, 16)
            pool.dma_start(scc3[:, :, 1], d["c_ctx_2"].rearrange("(c p) -> p c", p=P)).then_inc(loaded_c, 16)
            second_pool_early(pool)
            with pool.Fori(0, DEPTH) as i:
                e_h.wait(pool, i, 0)
                pool.dma_start(p_attn, cols("attn_norm", i)).then_inc(loaded_attn, 16)
                G.memset(gqA_to_gkB, 0.0)
                G.memset(kTz, 0.0)
                e_zero0.set(G.memset(xbc3[:, :, 0:3], 0.0))
                pool.dma_start(q3(ptok, NT), d["p"][i, 0].rearrange("(t p) n -> p t n", p=P)).then_inc(loaded_p, 16)
                small_loads = [
                    (wsm3[:, :, 0:8], d["w_in"][i].rearrange("(c p) n -> p c n", p=P)[:, :, C_DT:C_DT + 8]),
                    (wsm3[:, :, 8:24], d["w_in"][i].rearrange("(c p) n -> p c n", p=P)[:, :, C_LR:C_LR + 16]),
                    (p_convb, cols("ssd_conv_b", i)),
                    (p_qkg[:, 0:DQK], rows("da_q_norm", i)), (p_qkg[:, DQK:], rows("da_k_norm", i)),
                    (p_bgate, cols("gla_b_gate", i)), (p_wg2[0:GLA_R, :], d["gla_w_gate2"][i]),
                    (p_dtb, rows("ssd_dt_bias", i)), (p_alog, rows("ssd_a_log", i)),
                    (p_lam[:, 0:64], rows("da_lambda_q1", i)), (p_lam[:, 64:128], rows("da_lambda_k1", i)),
                    (p_lam[:, 128:192], rows("da_lambda_q2", i)), (p_lam[:, 192:256], rows("da_lambda_k2", i)),
                    (p_dskip, rows("ssd_d", i)), (p_ssdn, rows("ssd_norm", i)), (p_glan, rows("gla_norm", i)),
                    (p_sub, rows("da_sub_norm", i)),
                    (p_ffn, cols("ffn_norm", i)), (p_li, d["lam"][i]),
                    (p_adab, d["ada_b_2"][i].rearrange("(c p) -> p c", p=P)),
                ]
                for j in range(4):
                    small_loads.insert(3 + j, (convw3[:, j, :], d["ssd_conv_w"][i, j].rearrange("(c p) -> p c", p=P)))
                for dst, src in small_loads:
                    pool.dma_start(dst, src).then_inc(loaded_prm, 16)
                assert len(small_loads) == N_PRM
                e_win.wait(pool, i)
                pool.sem_inc(steps_apart, 1)
                G.memset(kinvz, 0.0)
                e_zero1.set(G.memset(Sz, 0.0))
            second_pool(pool)

        @block.scalar
        def _(act):
            act.wait_ge(sin_in, 1)
            A.activation(sinr, sinr, ACT.Sin)
            A.activation(cosr, cosr, ACT.Sin).then_inc(sin_out, 1)
            act.wait_ge(loaded_c, 32)
            A.activation(scc, scc, ACT.Silu).then_inc(silu_c, 1)
            act.wait_ge(loaded_h, 16)
            with act.Fori(0, DEPTH) as i:
                def squares(k, turn):
                    e_h.wait(act, i, turn)
                    for t in range(NT):
                        A.activation(junk[:, t * D:(t + 1) * D], h3[:, t, :], ACT.Square, accum_out=ss[:, t:t + 1])
                    e_ss.set(act.drain())

                def gemm_copy(name, dst, event, func=ACT.Copy):
                    GEMM.wait_filled(act, name, i)
                    GEMM.release(A.activation(dst, GEMM.buf(name).rearrange("p (t n) -> p t n", t=dst.shape[1]), func), name)
                    event.set(act.drain())

                squares(0, 0)
                gemm_copy("daq", qk_jt[:, :, 0, :], e_qkin)
                gemm_copy("dak", qk_jt[:, :, 1, :], e_qkin)
                gemm_copy("xbc0", xbc3[:, 0:4, 3:], e_xbcin)
                gemm_copy("xbc1", xbc3[:, 4:8, 3:], e_xbcin)
                M.wait_filled(act, "small", i)
                b = M.buf("small")
                A.copy(dtx, b[:, 0:16])
                A.copy(lrT[0:GLA_R, :], b[0:GLA_R, 256:512])
                M.release(A.copy(pT, b[:, 512:1024]), "small")
                e_small.set(act.drain())
                gemm_copy("gqk", gqk3, e_gqk)
                gemm_copy("dav", dav3, e_dav)
                gemm_copy("gv", gv3, e_gv)
                gemm_copy("z", sz3, e_sz, ACT.Silu)
                gemm_copy("gg", sg3, e_sg, ACT.Silu)
                e_conv.wait(act, i)
                e_xs.set(A.activation(xc, xc, ACT.Silu))
                M.wait_filled(act, "qT", i)
                M.release(A.copy(qT, M.buf("qT")), "qT")
                e_qT.set(act.drain())
                M.wait_filled(act, "kT", i)
                e_zero0.wait(act, i)
                kTb = M.buf("kT").rearrange("p (c n) -> p c n", c=4)
                A.copy(kTz4[0:64, :, 0, :], kTb[0:64])
                M.release(A.copy(kTz4[64:128, :, 1, :], kTb[64:128]), "kT")
                e_kT.set(act.drain())
                def modulation_rows(k):
                    M.wait_filled(act, f"mod{k}", i)
                    src = M.buf(f"mod{k}").rearrange("p (b n) -> p b n", b=2)[0:2, :, 0:384]
                    M.release(A.copy(mix[0:2, k * 768:(k + 1) * 768].rearrange("p (b n) -> p b n", b=2), src), f"mod{k}")
                    e_mrow.set(act.drain())

                e_abs.wait(act, i)
                A.activation(gax, gax, ACT.Exp, scale=-1.0)
                A.activation(dtl, dtl, ACT.Exp, scale=-1.0)
                A.activation(aneg, p_alog, ACT.Exp)
                A.activation(lam[:, 2:4], lam[:, 0:2], ACT.Exp)
                act.drain()
                A.activation(gax, gax, ACT.Ln, bias=1.0)
                A.activation(dtl, dtl, ACT.Ln, bias=1.0)
                e_ln.set(act.drain())
                modulation_rows(0)
                e_bc.wait(act, i)
                A.activation(geb, gax, ACT.Exp)
                A.activation(gx, gax, ACT.Exp, scale=-1.0)
                A.activation(gei, gei, ACT.Exp)
                e_gexp.set(act.drain())
                e_dtx.wait(act, i)
                A.activation(dte, dte, ACT.Exp)
                A.activation(ecum, cum[:, 8:16], ACT.Exp)
                e_dte.set(act.drain())
                modulation_rows(1)
                M.wait_filled(act, "state", i)
                M.release(A.copy(st, M.buf("state")[:, 0:512]), "state")
                e_st.set(act.drain())

                def score_exp(r):
                    e_sub.wait(act, i, r + 1)
                    e_sexp.set(A.activation(sc, sc, ACT.Exp, scale=DQK ** -0.5))

                def segment_exp(t):
                    e_seg.wait(act, i, t + 1)
                    seg = big[:, t * 1024:(t + 1) * 1024]
                    e_segx.set(A.activation(seg, seg, ACT.Exp))

                score_exp(0)
                segment_exp(0)
                modulation_rows(2)
                score_exp(1)
                segment_exp(1)
                modulation_rows(3)
                score_exp(2)
                M.wait_filled(act, "kendT", i)
                M.release(A.copy(kendT, M.buf("kendT")[:, 0:768]), "kendT")
                e_kendT.set(act.drain())
                M.wait_filled(act, "attT0", i)
                M.release(A.copy(at0T, M.buf("attT0")[:, 0:512]), "attT0")
                e_atT.set(act.drain())
                M.wait_filled(act, "attT1", i)
                M.release(A.copy(at1T, M.buf("attT1")), "attT1")
                e_atT.set(act.drain())
                for k in range(3):
                    M.wait_filled(act, f"mix{k}", i)
                    M.release(A.copy(mixT[:, k * 1024:(k + 1) * 1024], M.buf(f"mix{k}")), f"mix{k}")
                    e_mixT.set(act.drain())
                squares(1, 1)
                for j in range(FC // 2):
                    GEMM.wait_filled(act, f"gu{j}", i)
                    e_sgate.set(A.activation(sgate[:, (j % 2) * 512:(j % 2) * 512 + 512], GEMM.buf(f"gu{j}")[:, 0:512], ACT.Silu))
                for t in range(NT):
                    GEMM.wait_filled(act, f"pp_t{t}", i)
                    GEMM.release(A.copy(pp[:, t * 1024:(t + 1) * 1024], GEMM.buf(f"pp_t{t}")), f"pp_t{t}")
                    e_pp.set(act.drain())
                for n in range(2):
                    GEMM.wait_filled(act, f"pleg{n}", i)
                    e_pused.wait(act, i, n)
                    GEMM.release(A.activation(psig, GEMM.buf(f"pleg{n}"), ACT.Sigmoid), f"pleg{n}")
                    e_psig.set(act.drain())
            second_act(act)

        @block.tensor
        def _(pe):
            pe.wait_ge(loaded_const, 16)
            pe.wait_ge(loaded_h, 16)
            pe.wait_ge(silu_c, 1)
            with pe.Fori(0, DEPTH) as i:
                def mm(out_, lhsT, rhs, first=True, last=True):
                    return T.matmul(out_, lhsT, rhs, start=first, stop=last)

                def tr(out_, in_):
                    return T.transpose(out_, in_, ident)

                def norm_transposes(names, src):
                    for a, name in enumerate(names):
                        M.wait_free(pe, name, i)
                        for c in range(4):
                            for t in range(NT):
                                last = tr(M.buf(name)[:, c * S + t * P:c * S + (t + 1) * P],
                                          src[:, t, (4 * a + c) * P:(4 * a + c + 1) * P])
                        M.done(last)

                def weights_used():
                    W.used(pe.drain())

                def tokens_by_columns(name):
                    W.wait_ready(pe, name, i)
                    GEMM.wait_free(pe, name, i)
                    wt = W.slot(name).rearrange("p (c n) -> p c n", c=KC)
                    for t in range(NT):
                        for c in range(KC):
                            last = mm(GEMM.buf(name)[:, t * 512:(t + 1) * 512], aT3[:, c, t * P:(t + 1) * P], wt[:, c, :],
                                      c == 0, c == KC - 1)
                    GEMM.done(last)
                    weights_used()

                def columns_by_tokens(name):
                    W.wait_ready(pe, name, i)
                    GEMM.wait_free(pe, name, i)
                    wt = W.slot(name).rearrange("p (c n) -> p c n", c=KC)
                    for f in range(4):
                        for c in range(KC):
                            last = mm(GEMM.buf(name)[:, f * S:(f + 1) * S], wt[:, c, f * P:(f + 1) * P], aT3[:, c, :],
                                      c == 0, c == KC - 1)
                    GEMM.done(last)
                    weights_used()

                def rows_to_width(turns, pieces, lhs):
                    for name in turns:
                        GEMM.wait_free(pe, name, i)
                    n_rows = sum(n for _, n in pieces)
                    k = 0
                    for name, n in pieces:
                        W.wait_ready(pe, name, i)
                        wt = W.slot(name).rearrange("p (c n) -> p c n", c=4)
                        for c in range(n):
                            for t in range(NT):
                                for b in range(2):
                                    last = mm(GEMM.buf(turns[t])[:, b * 512:(b + 1) * 512], lhs[:, k, t * P:(t + 1) * P],
                                              wt[:, c, b * 512:(b + 1) * 512], k == 0, k == n_rows - 1)
                                if k == n_rows - 1:
                                    GEMM.done(last)
                            k += 1
                        weights_used()

                e_xn.wait(pe, i, 1)
                norm_transposes(("norm0a", "norm0b"), xn3)
                e_aT.wait(pe, i, 1)
                tokens_by_columns("daq")
                tokens_by_columns("dak")
                columns_by_tokens("xbc0")
                columns_by_tokens("xbc1")
                M.wait_free(pe, "small", i)
                pe.wait_ge(loaded_prm, 16 * N_PRM * i + 16 * N_PRM)
                pe.wait_ge(loaded_p, 16 * i + 16)
                b = M.buf("small")
                for t in range(NT):
                    for c in range(KC):
                        mm(b[:, t * 8:t * 8 + 8], aT3[:, c, t * P:(t + 1) * P], wsm3[:, c, 0:8], c == 0, c == KC - 1)
                for c in range(KC):
                    mm(b[0:GLA_R, 256:512], wsm3[:, c, 8:24], aT3[:, c, :], c == 0, c == KC - 1)
                for c in range(2):
                    for t in range(NT):
                        last = tr(b[:, 512 + c * S + t * P:512 + c * S + (t + 1) * P], q3(ptok, NT)[:, t, c * P:(c + 1) * P])
                M.done(last)
                columns_by_tokens("gqk")
                tokens_by_columns("dav")
                tokens_by_columns("gv")
                tokens_by_columns("z")
                tokens_by_columns("gg")
                e_win.set(pe.drain())

                e_qk.wait(pe, i)
                for name, j in (("qT", 0), ("kT", 1)):
                    M.wait_free(pe, name, i)
                    for c in range(4):
                        for t in range(NT):
                            last = tr(M.buf(name)[:, c * S + t * P:c * S + (t + 1) * P], qk_jt[:, t, j, c * P:(c + 1) * P])
                    M.done(last)
                M.wait_free(pe, "gate", i)
                e_small.wait(pe, i)
                for c in range(2):
                    last = mm(M.buf("gate")[:, c * S:(c + 1) * S], p_wg2[0:GLA_R, c * P:(c + 1) * P], lrT[0:GLA_R, :])
                M.done(last)
                def modulation(k):
                    M.wait_free(pe, f"mod{k}", i)
                    for a in (2 * k, 2 * k + 1):
                        W.wait_ready(pe, f"ada{a}", i)
                        wt = W.slot(f"ada{a}")[:, 0:KC * 384].rearrange("p (c n) -> p c n", c=KC)
                        for c in range(KC):
                            last = mm(M.buf(f"mod{k}")[0:2, (a % 2) * 512:(a % 2) * 512 + 384], scc3[:, c, :], wt[:, c, :], c == 0, c == KC - 1)
                        if a % 2:
                            M.done(last)
                        weights_used()

                def modulation_columns(k):
                    e_mrow.wait(pe, i, k + 1)
                    M.wait_free(pe, f"modT{k}", i)
                    for c in range(6):
                        last = mm(M.buf(f"modT{k}")[:, 2 * c:2 * c + 2], mix[0:2, k * 768 + c * P:k * 768 + (c + 1) * P], ident[0:2, 0:2])
                    M.done(last)

                modulation(0)
                e_xs.wait(pe, i)
                M.wait_free(pe, "xsT", i)
                for t in range(NT):
                    for c in range(4):
                        last = tr(M.buf("xsT")[:, t * 512 + c * P:t * 512 + (c + 1) * P], xc3[:, c, t * P:(t + 1) * P])
                M.done(last)
                e_dta.wait(pe, i)
                M.wait_free(pe, "bcum", i)
                b = M.buf("bcum")
                for g in range(2):
                    tr(b[:, g * P:(g + 1) * P], xc3[:, 4 + g, 0:P])
                for t in range(NT):
                    mm(b[:, 512 + t * 8:520 + t * 8], upper, dta[:, t * 8:t * 8 + 8])
                M.done(mm(b[:, 528:536], ones, dta[:, 0:8]))
                M.wait_free(pe, "cb", i)
                for t in range(NT):
                    for g in range(2):
                        last = mm(M.buf("cb")[:, (2 * t + g) * P:(2 * t + g + 1) * P], xc3[:, 4 + g, t * P:(t + 1) * P],
                                  xc3[:, 6 + g, t * P:(t + 1) * P])
                M.done(last)
                modulation_columns(0)
                modulation(1)
                e_xde.wait(pe, i)
                M.wait_free(pe, "state", i)
                for g in range(2):
                    last = mm(M.buf("state")[:, g * 256:(g + 1) * 256], bmT[:, g * P:(g + 1) * P], xde[:, g * 256:(g + 1) * 256])
                M.done(last)
                e_qT.wait(pe, i)
                e_kT.wait(pe, i)

                def scores(name, maps, t):
                    M.wait_free(pe, name, i)
                    keys = (t + 1) * P
                    for k, m_ in enumerate(maps):
                        last = mm(M.buf(name)[:, k * keys:(k + 1) * keys], qT3[:, m_ // 2, t * P:(t + 1) * P],
                                  kTz4[:, m_ // 2, m_ % 2, 0:keys])
                    M.done(last)

                def running_rows(t):
                    e_ux.wait(pe, i, t + 1)
                    M.wait_free(pe, f"cumb{t}", i)
                    for b_ in range(2):
                        last = mm(M.buf(f"cumb{t}")[:, b_ * 512:(b_ + 1) * 512], ones, big[:, t * 1024 + b_ * 512:t * 1024 + (b_ + 1) * 512])
                    M.done(last)

                scores("score0", range(HC), 0)
                running_rows(0)
                modulation_columns(1)
                modulation(2)
                scores("score1", range(0, HC // 2), 1)
                running_rows(1)
                modulation_columns(2)
                modulation(3)
                scores("score2", range(HC // 2, HC), 1)
                modulation_columns(3)
                e_gops.wait(pe, i)
                M.wait_free(pe, "kendT", i)
                for c, (src, t) in enumerate(((gkA, 0), (gkB, 0), (gkA, 1))):
                    for f in range(2):
                        last = tr(M.buf("kendT")[:, c * 256 + f * P:c * 256 + (f + 1) * P], src[:, f * S + t * P:f * S + (t + 1) * P])
                M.done(last)
                M.wait_free(pe, "gla_att", i)
                for t in range(NT):
                    for hd in range(GLA_H):
                        last = mm(M.buf("gla_att")[:, (t * 4 + hd) * P:(t * 4 + hd + 1) * P],
                                  kinvz[:, hd * S + t * P:hd * S + (t + 1) * P], gqd[:, (hd // 2) * S + t * P:(hd // 2) * S + (t + 1) * P])
                M.done(last)
                e_kendT.wait(pe, i)
                e_gv.wait(pe, i)
                for name, chunks in (("gla_st0", (0, 1)), ("gla_st1", (2,))):
                    M.wait_free(pe, name, i)
                    for k, c in enumerate(chunks):
                        for f in range(2):
                            last = mm(M.buf(name)[:, k * 512 + f * 256:k * 512 + (f + 1) * 256], kendT[:, c * 256 + f * P:c * 256 + (f + 1) * P],
                                      gv3[:, c // 2, f * 256:(f + 1) * 256])
                    M.done(last)
                e_attn.wait(pe, i, 1)
                M.wait_free(pe, "attT0", i)
                for hd in range(DA_H):
                    last = tr(M.buf("attT0")[:, hd * P:(hd + 1) * P], attn[:, hd * P:(hd + 1) * P])
                M.done(last)
                e_attn.wait(pe, i, 3)
                M.wait_free(pe, "attT1", i)
                for hd in range(DA_H):
                    for kt in range(NT):
                        last = tr(M.buf("attT1")[:, kt * 512 + hd * P:kt * 512 + (hd + 1) * P],
                                  attn[:, 512 + hd * 256 + kt * P:512 + hd * 256 + (kt + 1) * P])
                M.done(last)
                e_atT.wait(pe, i)
                e_dav.wait(pe, i)
                M.wait_free(pe, "pv", i)
                b = M.buf("pv")
                for hd in range(DA_H):
                    mm(b[:, hd * DV:(hd + 1) * DV], at0T[:, hd * P:(hd + 1) * P], dav3[:, 0, hd * DV:(hd + 1) * DV])
                for hd in range(DA_H):
                    for kt in range(NT):
                        last = mm(b[:, 512 + hd * DV:512 + (hd + 1) * DV], at1T[:, kt * 512 + hd * P:kt * 512 + (hd + 1) * P],
                                  dav3[:, kt, hd * DV:(hd + 1) * DV], kt == 0, kt == NT - 1)
                M.done(last)
                e_mt.wait(pe, i)
                M.wait_free(pe, "ydiag", i)
                for t in range(NT):
                    for hd in range(SSD_H):
                        last = mm(M.buf("ydiag")[:, t * 512 + hd * 64:t * 512 + (hd + 1) * 64], big[:, t * 1024 + hd * P:t * 1024 + (hd + 1) * P],
                                  xdt[:, t * 512 + hd * 64:t * 512 + (hd + 1) * 64])
                M.done(last)
                e_st.wait(pe, i)
                M.wait_free(pe, "yoff", i)
                for g in range(2):
                    last = mm(M.buf("yoff")[:, g * 256:(g + 1) * 256], xc3[:, 6 + g, P:2 * P], st[:, g * 256:(g + 1) * 256])
                M.done(last)
                e_gat.wait(pe, i)
                e_S.wait(pe, i)
                M.wait_free(pe, "gla_out", i)
                for t in range(NT):
                    for hd in range(GLA_H):
                        o_ = M.buf("gla_out")[:, t * 512 + hd * P:t * 512 + (hd + 1) * P]
                        at = (hd // 2) * S + t * P
                        mm(o_, gatT[:, (t * 4 + hd) * P:(t * 4 + hd + 1) * P], gv3[:, t, hd * P:(hd + 1) * P], True, False)
                        if t > 0:
                            mm(o_, gqA[:, at:at + P], Sz5[:, 2 * t - 1, hd // 2, hd % 2, :], False, False)
                        last = mm(o_, gqB[:, at:at + P], Sz5[:, 2 * t, hd // 2, hd % 2, :], False, True)
                M.done(last)
                for k in range(3):
                    e_mixed.wait(pe, i, k + 1)
                    M.wait_free(pe, f"mix{k}", i)
                    for c in range(4):
                        for t in range(NT):
                            last = tr(M.buf(f"mix{k}")[:, c * S + t * P:c * S + (t + 1) * P], mix3[:, t, k * 512 + c * P:k * 512 + (c + 1) * P])
                    M.done(last)
                e_mixT.wait(pe, i)
                rows_to_width(("wo_t0", "wo_t1"), [(f"wo{j}", 4) for j in range(MC // 4)], mixT3)

                e_xn.wait(pe, i, 2)
                norm_transposes(("norm1a", "norm1b"), xn3)
                e_aT.wait(pe, i, 2)
                for j in range(FC // 2):
                    columns_by_tokens(f"gu{j}")
                e_gu.wait(pe, i)
                rows_to_width(("dn_t0", "dn_t1"), [(f"dn{j}", min(4, FC - 4 * j)) for j in range(-(-FC // 4))], gu3)

                W.wait_ready(pe, "plep", i)
                wt = W.slot("plep").rearrange("p (c n) -> p c n", c=4)
                for t in range(NT):
                    GEMM.wait_free(pe, f"pp_t{t}", i)
                    for b_ in range(2):
                        for c in range(2):
                            last = mm(GEMM.buf(f"pp_t{t}")[:, b_ * 512:(b_ + 1) * 512], pT[:, c * S + t * P:c * S + (t + 1) * P],
                                      wt[:, c, b_ * 512:(b_ + 1) * 512], c == 0, c == 1)
                    GEMM.done(last)
                weights_used()
                e_h.wait(pe, i, 2)
                norm_transposes(("hT_a", "hT_b"), h3)
                e_aT.wait(pe, i, 3)
                tokens_by_columns("pleg0")
                tokens_by_columns("pleg1")
            second_pe(pe)

        def bc(ap, shape, *axes):
            for a in axes:
                ap = ap.unsqueeze(a)
            return ap.to_broadcast([P, *shape])

        def rsqrt(dve, y, x, tmp):
            V.tensor_scalar(tmp.bitcast(i32), x.bitcast(i32), 1, None, ALU.logical_shift_right)
            dve.drain()
            V.tensor_scalar(y.bitcast(i32), tmp.bitcast(i32), -1.0, float(0x5F3759DF), ALU.mult, ALU.add)
            dve.drain()
            for _ in range(3):
                V.tensor_tensor(tmp, y, y, ALU.mult)
                dve.drain()
                V.scalar_tensor_tensor(tmp, tmp, -0.5, x, ALU.mult, ALU.mult)
                dve.drain()
                V.scalar_tensor_tensor(y, tmp, 1.5, y, ALU.add, ALU.mult)
                dve.drain()

        def group_rstd(dve, y, sq, groups, width, x=None):
            V.tensor_reduce(n_a[:, 0:groups], sq.rearrange("p (g e) -> p g e", g=groups), AX.X, ALU.add)
            dve.drain()
            V.tensor_scalar(n_b[:, 0:groups], n_a[:, 0:groups], 1.0 / width, EPS, ALU.mult, ALU.add)
            dve.drain()
            rsqrt(dve, y, n_b[:, 0:groups], n_a[:, 0:groups])

        @block.vector
        def _(dve):
            dve.wait_ge(loaded_const, 16)
            dve.wait_ge(loaded_pos, 16)
            V.tensor_copy(posf[:, 0:NT], posi[:])
            dve.drain()
            ang, turns_ = rtmp[:, 0:16], rtmp[:, 16:32]
            for t in range(NT):
                V.tensor_scalar(ang[:, t * 8:t * 8 + 8], C["inv_freq"], posf[:, t:t + 1], None, ALU.mult)
            dve.drain()
            big_ = 1.5 * 2.0 ** 23
            V.tensor_scalar(turns_, ang, 1.0 / (2 * math.pi), big_, ALU.mult, ALU.add)
            dve.drain()
            V.tensor_scalar(turns_, turns_, big_, None, ALU.subtract)
            dve.drain()
            c1 = 6.28125
            c2 = round((2 * math.pi - c1) * 2.0 ** 20) / 2.0 ** 20
            c3 = 2 * math.pi - c1 - c2
            for c_ in (c1, c2, c3):
                V.scalar_tensor_tensor(ang, turns_, -c_, ang, ALU.mult, ALU.add)
                dve.drain()
            lim = 3.1415925
            V.tensor_scalar(sinr, ang, lim, -lim, ALU.min, ALU.max)
            V.tensor_scalar(ang, ang, math.pi / 2, None, ALU.add)
            dve.drain()
            V.tensor_scalar(turns_, ang, math.pi, -2 * math.pi, ALU.is_gt, ALU.mult)
            dve.drain()
            V.tensor_tensor(ang, ang, turns_, ALU.add)
            dve.drain()
            V.tensor_scalar(cosr, ang, lim, -lim, ALU.min, ALU.max).then_inc(sin_in, 1)
            dve.wait_ge(sin_out, 1)
            dve.wait_ge(loaded_h, 16)

            with dve.Fori(0, DEPTH) as i:
                def release(ins, name):
                    M.release(ins, name)

                def norm_rows(turn):
                    e_ss.wait(dve, i, turn)
                    V.tensor_scalar(n_b[:, 0:NT], ss, 1.0 / D, EPS, ALU.mult, ALU.add)
                    dve.drain()
                    rsqrt(dve, rstd, n_b[:, 0:NT], n_a[:, 0:NT])
                    for t in range(NT):
                        V.tensor_scalar(xn3[:, t, :], h3[:, t, :], rstd[:, t:t + 1], None, ALU.mult)
                    e_xn.set(dve.drain())

                def columns_in(names, gain):
                    for a, name in enumerate(names):
                        M.wait_filled(dve, name, i)
                        for c in range(4):
                            src = M.buf(name)[:, c * S:(c + 1) * S]
                            k = 4 * a + c
                            if gain is None:
                                last = V.tensor_copy(aT3[:, k, :], src)
                            else:
                                last = V.tensor_scalar(aT3[:, k, :], src, gain[:, k:k + 1], None, ALU.mult)
                        release(last, name)
                    e_aT.set(dve.drain())

                norm_rows(1)
                dve.wait_ge(loaded_attn, 16 * i + 16)
                columns_in(("norm0a", "norm0b"), p_attn)

                e_qkin.wait(dve, i)
                dve.wait_ge(loaded_prm, 16 * N_PRM * i + 16 * N_PRM)
                V.tensor_tensor(big, qk, qk, ALU.mult)
                dve.drain()
                group_rstd(dve, n_c, big, 32, DQK)
                V.tensor_tensor(q3(qk, 32), q3(qk, 32), bc(n_c, [32, DQK], 2), ALU.mult)
                dve.drain()
                for t in range(NT):
                    V.tensor_tensor(qk5[:, t], qk5[:, t], bc(q3(p_qkg, 2), [2, HC, DQK], 2), ALU.mult)
                dve.drain()
                for t in range(NT):
                    x = qk5[:, t].rearrange("p j c e -> p (j c) e")
                    x1, x2 = x[:, :, 0:8], x[:, :, 8:16]
                    cs, sn = (bc(v[:, t * 8:t * 8 + 8], [16, 8], 1) for v in (cosr, sinr))
                    r = [q3(rtmp[:, k * 128:(k + 1) * 128], 16) for k in range(4)]
                    V.tensor_tensor(r[0], x1, cs, ALU.mult)
                    V.tensor_tensor(r[1], x2, sn, ALU.mult)
                    V.tensor_tensor(r[2], x2, cs, ALU.mult)
                    V.tensor_tensor(r[3], x1, sn, ALU.mult)
                    dve.drain()
                    V.tensor_tensor(x1, r[0], r[1], ALU.subtract)
                    V.tensor_tensor(x2, r[2], r[3], ALU.add)
                    dve.drain()
                e_qk.set(dve.drain())

                e_xbcin.wait(dve, i)
                e_zero0.wait(dve, i)
                for c in range(8):
                    V.tensor_scalar(xc3[:, c, :], xbc3[:, c, 3:], convw3[:, 3, c:c + 1], p_convb[:, c:c + 1], ALU.mult, ALU.add)
                dve.drain()
                for j in range(3):
                    for c in range(8):
                        V.scalar_tensor_tensor(xc3[:, c, :], xbc3[:, c, j:j + S], convw3[:, j, c:c + 1], xc3[:, c, :], ALU.mult, ALU.add)
                    dve.drain()
                e_conv.set(dve.drain())

                lv = p_lam.rearrange("p (a b e) -> p a b e", a=2, b=2)
                V.tensor_tensor(q3(lamp, 2), lv[:, :, 0, :], lv[:, :, 1, :], ALU.mult)
                V.tensor_scalar(p_sub, p_sub, p_li[:, 1:2], None, ALU.mult)
                e_small.wait(dve, i)
                V.tensor_tensor(q3(dtx, NT), q3(dtx, NT), bc(p_dtb, [NT, SSD_H], 1), ALU.add)
                M.wait_filled(dve, "gate", i)
                for c in range(2):
                    last = V.tensor_scalar(gx[:, c * S:(c + 1) * S], M.buf("gate")[:, c * S:(c + 1) * S], p_bgate[:, c:c + 1], None, ALU.add)
                release(last, "gate")
                dve.drain()
                V.tensor_reduce(lam[:, 0:2], q3(lamp, 2), AX.X, ALU.add)
                V.tensor_scalar(dtl.bitcast(i32), dtx.bitcast(i32), 0x7FFFFFFF, None, ALU.bitwise_and)
                V.tensor_scalar(gax.bitcast(i32), gx.bitcast(i32), 0x7FFFFFFF, None, ALU.bitwise_and)
                e_abs.set(dve.drain())
                e_ln.wait(dve, i)
                V.scalar_tensor_tensor(gx, gx, 0.0, gax, ALU.min, ALU.subtract)
                V.scalar_tensor_tensor(dtx, dtx, 0.0, dtl, ALU.max, ALU.add)
                V.tensor_tensor(lam[:, 0:1], lam[:, 2:3], lam[:, 3:4], ALU.subtract)
                dve.drain()
                V.tensor_scalar(gx, gx, 1.0 / 16.0, None, ALU.mult)
                V.scalar_tensor_tensor(q3(dta, NT), q3(dtx, NT), -1.0, bc(aneg, [NT, SSD_H], 1), ALU.mult, ALU.mult)
                V.tensor_scalar(lam[:, 0:1], lam[:, 0:1], p_li[:, 0:1], None, ALU.add)
                e_dta.set(dve.drain())
                for c in range(8):
                    V.tensor_tensor_scan(gax[:, c * 64:(c + 1) * 64], ones[:, 0:64], gx[:, c * 64:(c + 1) * 64], 0.0, ALU.mult, ALU.add)
                dve.drain()
                b8 = q3(gax, 8)
                V.tensor_tensor(q3(gei, 8), b8[:, :, 63:64].to_broadcast([P, 8, 64]), b8, ALU.subtract)
                e_bc.set(dve.drain())

                def modulation_in(k):
                    M.wait_filled(dve, f"modT{k}", i)
                    src = M.buf(f"modT{k}")[:, 0:12].rearrange("p (c s) -> p c s", s=2)
                    M.release(V.tensor_tensor(mods4[:, bass.ds(i, 1), 6 * k:6 * k + 6, :].rearrange("p i c s -> p (i c) s"), src,
                                              bc(p_adab[:, 6 * k:6 * k + 6], [6, 2], 2), ALU.add), f"modT{k}")

                M.wait_filled(dve, "xsT", i)
                V.tensor_tensor(q3(xdt, 16), q3(M.buf("xsT"), 16), bc(dtx, [16, SSD_P], 2), ALU.mult)
                release(V.tensor_copy(xh, M.buf("xsT")), "xsT")
                M.wait_filled(dve, "bcum", i)
                b = M.buf("bcum")
                V.tensor_copy(bmT, b[:, 0:256])
                V.tensor_copy(cum, b[:, 512:528])
                dve.drain()
                release(V.tensor_tensor(dte, b[:, 528:536], cum[:, 0:8], ALU.subtract), "bcum")
                e_dtx.set(dve.drain())
                for t in range(NT):
                    e_ux.set(V.tensor_tensor(q3(big[:, t * 1024:(t + 1) * 1024], 8), bc(upper, [8, P], 1),
                                             bc(dta[:, t * 8:t * 8 + 8], [8, P], 2), ALU.mult))
                e_win.wait(dve, i)
                M.wait_filled(dve, "cb", i)
                release(V.tensor_tensor(q3(cbm, 4), q3(M.buf("cb")[:, 0:512], 4), bc(upper, [4, P], 1), ALU.mult), "cb")
                modulation_in(0)
                e_dte.wait(dve, i)
                e_xde.set(V.tensor_tensor(q3(xde, 8), q3(xdt[:, 0:512], 8), bc(dte, [8, SSD_P], 2), ALU.mult))

                e_gexp.wait(dve, i)
                e_gqk.wait(dve, i)
                e_zero1.wait(dve, i)
                gq, gk = gqk[:, 0:512], gqk[:, 512:1024]
                V.scalar_tensor_tensor(gqd, gq, GLA_K ** -0.5, geb, ALU.mult, ALU.mult)
                kz = kinvz.rearrange("p (a r n) -> p a r n", a=2, r=2)
                for r in range(2):
                    pr = slice(r * 64, r * 64 + 64)
                    V.tensor_tensor(kz[pr, :, r, :], q3(gk, 2)[pr], q3(gx, 2)[pr], ALU.mult)
                halves = lambda ap: ap.rearrange("p (n c l) -> p n c l", c=2, l=64)
                for c, dst in ((0, gkA), (1, gkB)):
                    V.tensor_tensor(halves(dst)[:, :, c, :], halves(gk)[:, :, c, :], halves(gei)[:, :, c, :], ALU.mult)
                dve.drain()
                for c, dst in ((0, gqA), (1, gqB)):
                    V.tensor_copy(halves(dst)[:, :, c, :], halves(gqd)[:, :, c, :])
                e_gops.set(dve.drain())

                def softmax(r):
                    name, n, keys, at = (("score0", 8, P, 0), ("score1", 4, 2 * P, 512), ("score2", 4, 2 * P, 1024))[r]
                    s3 = q3(sc, n)
                    M.wait_filled(dve, name, i)
                    mask = C["causal"][:, 2 * P - keys:2 * P]
                    release(V.tensor_tensor(s3, q3(M.buf(name), n), bc(mask, [n, keys], 1), ALU.add), name)
                    dve.drain()
                    V.tensor_reduce(mx[:, 0:n], s3, AX.X, ALU.max)
                    dve.drain()
                    V.tensor_tensor(s3, s3, bc(mx[:, 0:n], [n, keys], 2), ALU.subtract)
                    e_sub.set(dve.drain())
                    return s3, n, keys, at

                def softmax_end(r, s3, n, keys, at):
                    e_sexp.wait(dve, i, r + 1)
                    V.tensor_reduce(dsum[:, 0:n], s3, AX.X, ALU.add)
                    dve.drain()
                    V.reciprocal(wgt[:, 0:n], dsum[:, 0:n])
                    dve.drain()
                    odd = q3(wgt[:, 0:n], n // 2)[:, :, 1:2]
                    V.tensor_scalar(odd, odd, lam[:, 0:1], -1.0, ALU.mult, ALU.mult)
                    dve.drain()
                    V.tensor_tensor(s3, s3, bc(wgt[:, 0:n], [n, keys], 2), ALU.mult)
                    dve.drain()
                    s4 = s3.rearrange("p (a r) k -> p a r k", r=2)
                    V.tensor_tensor(q3(attn[:, at:at + n // 2 * keys], n // 2), s4[:, :, 0, :], s4[:, :, 1, :], ALU.add)
                    e_attn.set(dve.drain())

                def segment(t):
                    seg = big[:, t * 1024:(t + 1) * 1024]
                    M.wait_filled(dve, f"cumb{t}", i)
                    release(V.tensor_tensor(q3(seg, 8), q3(M.buf(f"cumb{t}"), 8), bc(cum[:, t * 8:t * 8 + 8], [8, P], 2), ALU.subtract), f"cumb{t}")
                    dve.drain()
                    e_seg.set(V.tensor_scalar(seg, seg, 0.0, None, ALU.min))

                def ssd_map(t):
                    seg = big[:, t * 1024:(t + 1) * 1024]
                    e_segx.wait(dve, i, t + 1)
                    s4 = seg.rearrange("p (g r l) -> p g r l", g=2, r=4)
                    e_mt.set(V.tensor_tensor(s4, s4, bc(q3(cbm[:, t * 256:(t + 1) * 256], 2), [2, 4, P], 2), ALU.mult))

                sm = softmax(0)
                segment(0)
                modulation_in(1)
                softmax_end(0, *sm)
                sm = softmax(1)
                segment(1)
                modulation_in(2)
                softmax_end(1, *sm)
                sm = softmax(2)
                modulation_in(3)
                ssd_map(0)
                ssd_map(1)
                softmax_end(2, *sm)

                M.wait_filled(dve, "gla_att", i)
                release(V.tensor_tensor(q3(gatT, 8), q3(M.buf("gla_att"), 8), bc(C["chunk_upper"], [8, P], 1), ALU.mult), "gla_att")
                e_gat.set(dve.drain())
                for c, (name, at) in enumerate((("gla_st0", 0), ("gla_st0", 512), ("gla_st1", 0))):
                    if c != 1:
                        M.wait_filled(dve, name, i)
                    for a in range(2):
                        for r in range(2):
                            pr = slice(r * 64, r * 64 + 64)
                            src = M.buf(name)[pr, at + a * 256 + r * P:at + a * 256 + (r + 1) * P]
                            if c == 0:
                                last = V.tensor_copy(Sz5[pr, c, a, r, :], src)
                            else:
                                end = a * S + c * 64 + 63
                                last = V.scalar_tensor_tensor(Sz5[pr, c, a, r, :], Sz5[pr, c - 1, a, r, :], geb[pr, end:end + 1],
                                                              src, ALU.mult, ALU.add)
                    if c > 0:
                        release(last, name)
                    dve.drain()
                e_S.set(dve.drain())

                def head_norm(x4, width, sq):
                    n = NT * x4.shape[2]
                    V.tensor_tensor(sq.rearrange("p (t a e) -> p t a e", t=NT, e=width), x4, x4, ALU.mult)
                    dve.drain()
                    group_rstd(dve, n_c[:, 0:n], sq, n, width)
                    V.tensor_tensor(x4, x4, bc(q3(n_c[:, 0:n], NT), list(x4.shape[1:]), 3), ALU.mult)
                    dve.drain()

                M.wait_filled(dve, "pv", i)
                o = mix3[:, :, 0:512]
                release(V.tensor_copy(o, q3(M.buf("pv"), NT)), "pv")
                dve.drain()
                o4 = o.rearrange("p t (a e) -> p t a e", e=DV)
                head_norm(o4, DV, sc)
                V.tensor_tensor(o4, o4, bc(p_sub, [NT, DA_H, DV], 1, 1), ALU.mult)
                e_mixed.set(dve.drain())

                y = mix3[:, :, 512:1024]
                y4 = y.rearrange("p t (a e) -> p t a e", e=SSD_P)
                V.tensor_tensor(y4, xh.rearrange("p (t a e) -> p t a e", t=NT, e=SSD_P),
                                bc(p_dskip, [NT, SSD_H, SSD_P], 1, 3), ALU.mult)
                dve.drain()
                M.wait_filled(dve, "ydiag", i)
                release(V.tensor_tensor(y, y, q3(M.buf("ydiag"), NT), ALU.add), "ydiag")
                M.wait_filled(dve, "yoff", i)
                release(V.tensor_tensor(q3(sc[:, 0:512], 8), q3(M.buf("yoff")[:, 0:512], 8), bc(ecum, [8, SSD_P], 2), ALU.mult), "yoff")
                dve.drain()
                V.tensor_tensor(y[:, 1, :], y[:, 1, :], sc[:, 0:512], ALU.add)
                dve.drain()
                e_sz.wait(dve, i)
                V.tensor_tensor(y, y, sz3, ALU.mult)
                dve.drain()
                head_norm(y.rearrange("p t (a e) -> p t a e", e=256), 256, sc)
                V.tensor_tensor(y, y, bc(p_ssdn, [NT, 512], 1), ALU.mult)
                e_mixed.set(dve.drain())

                M.wait_filled(dve, "gla_out", i)
                o = mix3[:, :, 1024:1536]
                release(V.tensor_copy(o, q3(M.buf("gla_out"), NT)), "gla_out")
                dve.drain()
                o4 = o.rearrange("p t (a e) -> p t a e", e=GLA_V)
                head_norm(o4, GLA_V, sc)
                V.tensor_tensor(o4, o4, bc(p_glan, [NT, GLA_H, GLA_V], 1, 1), ALU.mult)
                dve.drain()
                e_sg.wait(dve, i)
                V.tensor_tensor(o, o, sg3, ALU.mult)
                e_mixed.set(dve.drain())

                def add_to_h(names):
                    for t, name in enumerate(names):
                        GEMM.wait_filled(dve, name, i)
                        GEMM.release(V.tensor_tensor(h3[:, t, :], h3[:, t, :], GEMM.buf(name), ALU.add), name)
                    e_h.set(dve.drain())

                add_to_h(("wo_t0", "wo_t1"))
                norm_rows(2)
                columns_in(("norm1a", "norm1b"), p_ffn)
                for j in range(FC // 2):
                    name = f"gu{j}"
                    e_sgate.wait(dve, i, j + 1)
                    GEMM.release(V.tensor_tensor(gu[:, 2 * j * S:(2 * j + 2) * S], sgate[:, (j % 2) * 512:(j % 2) * 512 + 512],
                                                 GEMM.buf(name)[:, 512:1024], ALU.mult), name)
                    e_gu.set(dve.drain())
                add_to_h(("dn_t0", "dn_t1"))
                columns_in(("hT_a", "hT_b"), None)
                e_pp.wait(dve, i)
                for n in range(2):
                    e_psig.wait(dve, i, n + 1)
                    s3, hn = q3(psig, NT), h3[:, :, n * 512:(n + 1) * 512]
                    V.tensor_tensor(s3, s3, q3(pp, NT)[:, :, n * 512:(n + 1) * 512], ALU.mult)
                    dve.drain()
                    V.tensor_tensor(hn, hn, s3, ALU.add)
                    e_pused.set(dve.drain())
                e_h.set(dve.drain())
            second_dve(dve)


_INS = ["x", "p", "positions", "attn_norm", "w_in", "da_q_norm", "da_k_norm", "da_lambda_q1", "da_lambda_k1",
        "da_lambda_q2", "da_lambda_k2", "da_sub_norm", "ssd_conv_w", "ssd_conv_b", "ssd_dt_bias", "ssd_a_log", "ssd_d",
        "ssd_norm", "gla_w_gate2", "gla_b_gate", "gla_norm", "w_out", "ffn_norm", "w_ffn_gate", "w_ffn_up", "w_ffn_down",
        "ple_w_proj", "ple_w_gate", "c_2", "ctx_2", "c_ctx_2", "ada_w_2", "ada_b_2", "norm_pre_2", "norm_post_2",
        "hg_w_in_2", "hg_o_norm_2", "hg_w_out_2", "mla_w_in_2", "mla_qa_norm_2", "mla_w_qb_2", "mla_kva_norm_2",
        "mla_w_kvb_2", "mla_w_out_2"]


def kernel(**inputs):
    import concourse.bacc as bacc
    from concourse.bass_utils import run_bass_kernel_spmd

    nc = bacc.Bacc("TRN2", target_bir_lowering=False, num_devices=1)
    arrays = {name: np.ascontiguousarray(inputs[name]) for name in _INS}
    arrays["cst"], arrays["hmask"], arrays["lam"] = constants()
    d, feed = {}, {}
    for name, a in arrays.items():
        feed[f"in_{name}"] = a
        d[name] = nc.dram_tensor(f"in_{name}", a.shape, mybir.dt.from_np(a.dtype), kind="ExternalInput").ap()
    out = nc.dram_tensor("out_0", (1, S, D), mybir.dt.float32, kind="ExternalOutput").ap()
    program(nc, d, out)
    result = run_bass_kernel_spmd(nc, [feed], core_ids=[0])
    return result.results[0]["out_0"]
```

```python
import math
from contextlib import ExitStack

import numpy as np
import concourse.bass as bass
from concourse import mybir

P = 128
D = 1024
S = 256
CTX = 256
DEPTH = 2
EPS = 1e-6
NT = S // P
KC = D // P
PLE = 256
DA_H, DQK, DV = 4, 64, 128
HC = DA_H * 2
ROT = DQK // 4
SSD_H, SSD_P, SSD_N = 8, 64, 128
GLA_H, GLA_K, GLA_V, GLA_R = 4, 64, 128, 16
FF = -(-8 * D // (3 * 256)) * 256
FC = FF // P
MIX = 1536
MC = MIX // P
DI = 2 * D
NH = DI // P
PE_D = 64
QR, KVR = D // 4, D // 8
MLA_SCALE = (128 + 64) ** -0.5
C_DAQ, C_DAK, C_DAV, C_Z, C_XBC, C_DT = 0, 512, 1024, 1536, 2048, 3072
C_GQ, C_GV, C_GG, C_LR = 3080, 3592, 4104, 4616
NLEV = 7

CONST_COLS = dict(ident=128, upper=128, chunk_upper=128, causal=256, ones=128, inv_freq=8,
                  ax_cos=NT * 32, ax_sin=NT * 32)


def const_slices():
    at, where = 0, {}
    for name, n in CONST_COLS.items():
        where[name] = (at, at + n)
        at += n
    return where, at


def constants():
    where, width = const_slices()
    c = np.zeros((P, width), np.float32)

    def put(name, value):
        a, b = where[name]
        c[:, a:b] = value

    k, q = np.arange(P)[:, None], np.arange(P)[None, :]
    put("ident", k == q)
    put("upper", k <= q)
    put("chunk_upper", (k <= q) & (k // 64 == q // 64))
    put("causal", np.concatenate([np.zeros((P, P)), np.where(q <= k, 0.0, -1e30)], axis=1))
    put("ones", 1.0)
    put("inv_freq", np.float32(500000.0) ** (-np.arange(0, ROT, 2, dtype=np.float32) / np.float32(ROT)))
    init = [0.8 - 0.6 * math.exp(-0.3 * i) for i in range(DEPTH)]
    lam = np.array([[[v, 1.0 - v]] * P for v in init], np.float32)
    tok = np.arange(S)
    inv = np.float32(10000.0) ** (-np.arange(0, 32, 2, dtype=np.float32) / np.float32(32))
    ang = np.concatenate([(tok // 64).astype(np.float32)[:, None] * inv,
                          (tok % 64).astype(np.float32)[:, None] * inv], axis=1)
    fold = lambda t: t.reshape(NT, P, 32).transpose(1, 0, 2).reshape(P, NT * 32)
    put("ax_cos", fold(np.cos(ang)))
    put("ax_sin", fold(np.sin(ang)))
    m = np.zeros((P, NLEV + 1, P), np.float32)
    for lev in range(NLEV):
        h = 64 >> lev
        m[:, lev] = (k // (2 * h) == q // (2 * h)) & (k // h != q // h)
    m[:, NLEV] = k == q
    return c, m.reshape(P, -1), lam


class Turns:

    def __init__(self, area, filled, free, order):
        self.area, self.filled, self.free = area, filled, free
        self.at = {name: k for k, name in enumerate(order)}
        self.n = len(order)
        assert self.n % 2 == 0 and len(self.at) == self.n

    def buf(self, name):
        p = self.at[name] % 2
        return self.area[:, p * 1024:(p + 1) * 1024]

    def wait_free(self, eng, name, i=0):
        k = self.at[name]
        eng.wait_ge(self.free[k % 2], i * (self.n // 2) + k // 2 + 1)

    def wait_filled(self, eng, name, i=0):
        eng.wait_ge(self.filled, i * self.n + self.at[name] + 1)

    def done(self, ins):
        ins.then_inc(self.filled, 1)

    def release(self, ins, name):
        ins.then_inc(self.free[self.at[name] % 2], 1)


class Ring:

    def __init__(self, slots, ready, free, pieces):
        self.slots, self.ready, self.free = slots, ready, free
        self.names = [p[0] for p in pieces]
        self.at = {n: k for k, n in enumerate(self.names)}
        self.n, self.r = len(pieces), len(ready)
        assert self.n % self.r == 0
        self.dmas = [p[1] for p in pieces]
        self.total = [sum(self.dmas[s::self.r]) for s in range(self.r)]

    def slot(self, name):
        return self.slots[:, self.at[name] % self.r, :]

    def wait_free(self, eng, name, i=0):
        k, f = self.at[name], len(self.free)
        eng.wait_ge(self.free[k % f], i * (self.n // f) + k // f + 1)

    def all_free(self, eng, i=0):
        for f in self.free:
            eng.wait_ge(f, (self.r + i * self.n) // len(self.free))

    def loaded(self, dma, name):
        dma.then_inc(self.ready[self.at[name] % self.r], 16)

    def wait_ready(self, eng, name, i=0):
        k = self.at[name]
        s = k % self.r
        eng.wait_ge(self.ready[s], i * (16 * self.total[s]) + 16 * sum(self.dmas[s:k + 1:self.r]))

    def used(self, ins, name=None):
        ins.then_inc(self.free[self.at[name] % len(self.free) if name else 0], 1)


class Split:

    def __init__(self, high, low, high_ready, low_ready, free, pieces):
        self.high, self.low, self.high_ready, self.low_ready, self.free = high, low, high_ready, low_ready, free
        self.names = [n for n, _ in pieces]
        self.at = {n: k for k, n in enumerate(self.names)}
        self.by = dict(pieces)
        self.n, self.r = len(pieces), high.shape[1]
        assert self.n % self.r == 0
        self.turn = {n: sum(e == self.by[n] for _, e in pieces[:k + 1]) for k, (n, _) in enumerate(pieces)}
        self.per = {e: sum(e == x for _, x in pieces) for e in low_ready}

    def hi(self, name):
        return self.high[:, self.at[name] % self.r, :]

    def lo(self, name):
        return self.low[:, self.at[name] % self.r, :]

    def wait_free(self, eng, name, i=0):
        eng.wait_ge(self.free, i * self.n + self.at[name] + 1)

    def all_free(self, eng, i=0):
        eng.wait_ge(self.free, self.r + i * self.n)

    def high_done(self, ins):
        ins.then_inc(self.high_ready, 1)

    def wait_high(self, eng, name, i=0):
        eng.wait_ge(self.high_ready, i * self.n + self.at[name] + 1)

    def low_done(self, ins, name):
        ins.then_inc(self.low_ready[self.by[name]], 1)

    def wait_low(self, eng, name, i=0):
        eng.wait_ge(self.low_ready[self.by[name]], i * self.per[self.by[name]] + self.turn[name])

    def used(self, ins):
        ins.then_inc(self.free, 1)


def program(nc, d, out):
    f32, f32r, i32 = mybir.dt.float32, mybir.dt.float32r, mybir.dt.int32
    ALU, ACT, AX = mybir.AluOpType, mybir.ActivationFunctionType, mybir.AxisListType
    V, A, T, G = nc.vector, nc.scalar, nc.tensor, nc.gpsimd
    ctx = ExitStack()
    with ctx:
        def sb(name, cols, dt=f32):
            return ctx.enter_context(nc.sbuf_tensor(name, [P, cols], dt))

        sems = {}

        def sem(name):
            if name not in sems:
                sems[name] = ctx.enter_context(nc.semaphore(name))
            return sems[name]

        where, n_const = const_slices()
        cst = sb("cst", n_const)
        C = {n: cst[:, a:b] for n, (a, b) in where.items()}
        ident, upper, ones = C["ident"], C["upper"], C["ones"]
        h = sb("h", NT * D)
        h3 = h[:].rearrange("p (t n) -> p t n", t=NT)
        prm = sb("prm", 1712)
        prm2 = sb("prm2", 340)

        posi = sb("posi", NT, i32)
        with nc.sbuf_tensor("ring", [P, 4 * 4096], f32) as ring:
            pass
        ring_r = sb("ring_r", 4 * 4096, f32r)
        with nc.sbuf_tensor("work", [P, 31800], f32) as work:
            pass
        start = lambda ap: ap.offset % work.shape[1]
        views = []

        def float32r_views(parts):
            cuts = {0, work.shape[1]}
            for ap in parts:
                cuts |= {start(ap), start(ap) + ap.shape[1]}
            cuts = sorted(cuts)
            for a, b in zip(cuts, cuts[1:]):
                views.append((a, b, sb(f"work_r{a}", b - a, f32r)))

        def rounded(ap):
            for a, b, view in views:
                if a <= start(ap) and start(ap) + ap.shape[1] <= b:
                    return view[:, start(ap) - a:start(ap) - a + ap.shape[1]]
            raise AssertionError("no view")

        ring3 = ring[:].rearrange("p (s n) -> p s n", s=4)
        pg = ctx.enter_context(nc.psum_tensor("pg", [P, 2048], f32))
        pm = ctx.enter_context(nc.psum_tensor("pm", [P, 2048], f32))

        class Bump:
            def __init__(self, tile):
                self.tile, self.at = tile, 0

            def take(self, n):
                self.at += n
                assert self.at <= self.tile.shape[1], self.at
                return self.tile[:, self.at - n:self.at]

        bp = Bump(prm)
        p_qkg, p_lam, p_sub = bp.take(2 * DQK), bp.take(4 * DQK), bp.take(DV)
        p_ssdn, p_glan = bp.take(512), bp.take(GLA_V)
        p_dtb, p_alog, p_dskip = bp.take(8), bp.take(8), bp.take(8)
        p_attn, p_ffn = bp.take(KC), bp.take(KC)
        p_convw, p_convb, p_bgate = bp.take(32), bp.take(8), bp.take(2)
        p_wg2, p_li = bp.take(256), bp.take(2)
        convw3 = p_convw.rearrange("p (j c) -> p j c", j=4)

        b2 = Bump(prm2)
        scc, p_adab, mods = b2.take(2 * KC), b2.take(24), b2.take(DEPTH * 48)
        p_pre, p_post, p_qan, p_kvan = b2.take(DEPTH * KC), b2.take(DEPTH * KC), b2.take(QR // P), b2.take(1)
        g1, gtp = b2.take(2 * KC), b2.take(2 * KC)
        st_a, st_b, st_c, st_m = b2.take(8), b2.take(8), b2.take(8), b2.take(8)
        tot_f, tot_b = b2.take(8), b2.take(8)
        scc3 = scc.rearrange("p (c s) -> p c s", s=2)
        mods4 = mods.rearrange("p (i c s) -> p i c s", i=DEPTH, s=2)

        q3 = lambda ap, a: ap.rearrange("p (a b) -> p a b", a=a)
        w = Bump(work)
        xn, aT = w.take(2048), w.take(2048)
        gu = w.take(FC * S)
        qk, big, sc, at0T = gu[:, 0:2048], gu[:, 2048:4096], gu[:, 4096:5120], gu[:, 5120:5632]
        mixT = w.take(MC * S)
        qT, kTz = mixT[:, 0:1024], mixT[:, 1024:3072]
        dav = w.take(1024)
        sz_at = w.at
        sz, sg, gqk, gv = (w.take(1024) for _ in range(4))
        xbc = w.take(8 * 259)
        xc, mix = w.take(2048), w.take(NT * MIX)
        xde, st, bmT = w.take(512), w.take(512), w.take(256)
        gxa = w.take(1024)
        gx, gax, kendT = gxa[:, 0:512], gxa[:, 512:1024], gxa[:, 0:768]
        geb, gei, gqd, gqA, gqB, gkA, gkB = (w.take(512) for _ in range(7))
        pT = w.take(NT * PLE)
        kinvz, gatT, cbm, Sz = xn[:, 0:1024], xn[:, 1024:2048], aT[:, 0:512], aT[:, 512:2048]
        attn = qk[:, 0:1536]
        xh, xdt = xbc[:, 0:1024], xbc[:, 1024:2048]
        at1T, mod_rows = gqk, gqk[:, 0:768]
        ptok, junk = mix[:, 0:512], big
        gqA_to_gkB = work[:, w.at - 2560:w.at - 512]
        qk_jt = qk.rearrange("p (t j n) -> p t j n", t=NT, j=2)
        pp, psig = mix[:, 0:2048], mix[:, 2048:3072]
        sgate = dav
        ss, rstd = w.take(2), w.take(2)
        n_a, n_b, n_c = w.take(32), w.take(32), w.take(32)
        mx, dsum, wgt = w.take(16), w.take(16), w.take(16)
        lam, lamp = w.take(4), sc[:, 768:896]
        dtx, dtl, dta, cum = w.take(16), w.take(16), w.take(16), w.take(16)
        dte, ecum, aneg = w.take(8), w.take(8), w.take(8)
        lrT = sc[:, 512:768]
        cosr, sinr, rtmp = w.take(NT * 8), w.take(NT * 8), sc[:, 0:512]
        posf = w.take(2 * NT)

        low_a, low_f = mix[:, 1024:3072], xc
        low_mixT = gu[:, 0:MC * S]
        low_gu = work[:, sz_at:sz_at + FC * S]
        p_hi, p_lo = xde, st
        float32r_views([aT, gu, mixT, low_a, low_f, low_gu, p_hi, p_lo])
        hi_lo = lambda hi, lo, a: (q3(rounded(hi), a), q3(rounded(lo), a))
        A_IN, A_LATER = hi_lo(aT, low_a, KC), hi_lo(aT, low_f, KC)
        MIX_T, GU, P_T = hi_lo(mixT, low_mixT, MC), hi_lo(gu, low_gu, FC), hi_lo(p_hi, p_lo, PLE // P)
        xn3 = q3(xn, NT)
        mix3, dav3, gv3, sz3, sg3 = (q3(t, NT) for t in (mix, dav, gv, sz, sg))
        qk5 = qk.rearrange("p (t j c e) -> p t j c e", t=NT, j=2, c=HC)
        qT3, kTz4 = q3(qT, 4), kTz.rearrange("p (c r n) -> p c r n", c=4, r=2)
        xbc3, xc3 = q3(xbc, 8), q3(xc, 8)
        gqk3 = q3(gqk, 4)
        Sz5 = Sz.rearrange("p (c a r v) -> p c a r v", c=3, a=2, r=2)

        class Event:

            def __init__(self, name, n=1, start=0):
                self.sem, self.n, self.start = sem(name), n, start

            def wait(self, eng, i, k=None):
                eng.wait_ge(self.sem, i * self.n + ((self.n if k is None else k) + self.start))

            def set(self, ins):
                ins.then_inc(self.sem, 1)

        w_in_pieces = [f"{n}_{k}" for n in ("daq", "dak", "xbc0", "xbc1") for k in range(2)] + ["small"]
        w_in_pieces += [f"{n}_{k}" for n in ("gqk", "dav", "gv", "z", "gg") for k in range(2)]
        ada_pieces = [f"ada{a}" for a in range(12)]
        wo_pieces = [f"wo{j}" for j in range(MC // 2)]
        gu_pieces = [f"gu{j}_{k}" for j in range(FC // 2) for k in range(2)]
        dn_pieces = [f"dn{j}" for j in range(FC // 2)]
        ple_pieces = [f"plep{k}" for k in range(4)] + [f"pleg{n}_{k}" for n in range(2) for k in range(2)]
        ada_wo_pieces = ada_pieces[:3] + wo_pieces[:2] + ada_pieces[3:9] + wo_pieces[2:3] + ada_pieces[9:]
        layer_pieces = [(n, 2 if n in gu_pieces or n == "small" else 1) for n in
                        w_in_pieces + ada_wo_pieces + wo_pieces[3:] + gu_pieces + dn_pieces + ple_pieces]
        on_pool = w_in_pieces[:3] + w_in_pieces[6:] + wo_pieces + gu_pieces[:3] + ple_pieces
        split_pieces = [(n, "pool" if n in on_pool else "dve") for n, _ in layer_pieces if n not in ada_pieces]
        slots = lambda tile, at, n: tile[:, at:at + n * 2048].rearrange("p (s n) -> p s n", s=n)
        W = Ring(slots(ring, 0, 2), [sem(f"weights_ready{k}") for k in range(2)], [sem(f"weights_slot_free{k}") for k in range(2)], layer_pieces)
        SPLIT = Split(slots(ring_r, 2 * 2048, 3), slots(ring_r, 5 * 2048, 3), sem("weights_high_ready"),
                      dict(dve=sem("weights_low_ready_dve"), pool=sem("weights_low_ready_pool")), sem("split_slot_free"), split_pieces)

        piece_width = {n: KC * 24 if n == "small" else 2 * 256 if n.startswith("plep") else 2048 for n in SPLIT.at}

        def split_high(act, name, i):
            W.wait_ready(act, name, i)
            SPLIT.wait_free(act, name, i)
            n = piece_width[name]
            A.activation(SPLIT.hi(name)[:, 0:n], W.slot(name)[:, 0:n], ACT.Copy)
            SPLIT.high_done(act.drain())

        def split_low(eng, E, name, i):
            SPLIT.wait_high(eng, name, i)
            n = piece_width[name]
            W.used(E.tensor_tensor(SPLIT.lo(name)[:, 0:n], W.slot(name)[:, 0:n], SPLIT.hi(name)[:, 0:n].bitcast(f32), ALU.subtract), name)
            SPLIT.low_done(eng.drain(), name)

        GEMM = Turns(pg, sem("gemm_filled"), [sem("gemm_free0"), sem("gemm_free1")],
                     ["daq", "dak", "xbc0", "xbc1", "gqk", "dav", "gv", "z", "gg", "wo_t0", "wo_t1"]
                     + [f"gu{j}" for j in range(FC // 2)] + ["dn_t0", "dn_t1", "pp_t0", "pp_t1", "pleg0", "pleg1"])
        M = Turns(pm, sem("mixer_psum_filled"), [sem("mixer_psum_free0"), sem("mixer_psum_free1")],
                  ["norm0a", "norm0b", "small", "qT", "kT", "gate", "xsT", "score0", "bcum", "score1", "cumb0", "cumb1", "cb", "score2",
                   "state", "kendT", "mod0", "gla_att", "attT0", "modT0", "gla_st0", "gla_st1", "attT1", "pv", "mod1", "ydiag", "yoff", "modT1",
                   "mod2", "gla_out", "mix0", "modT2", "mod3", "mix1", "modT3", "mix2", "norm1a", "norm1b", "hT_a", "hT_b"])
        loaded_pos = sem("positions_loaded")
        loaded_const, loaded_h = sem("const_loaded"), sem("h_loaded")
        loaded_attn, loaded_prm, loaded_p = sem("attn_norm_loaded"), sem("params_loaded"), sem("p_loaded")
        N_PRM = 22
        tables_done = sem("rope_tables_done")
        sin_in, sin_out = sem("sin_arguments"), sem("sin_done")
        e_ss, e_xn, e_aT, e_h = Event("squares_summed", 2), Event("rows_normed", 2), Event("aT_ready", 6), Event("h_updated", 3, 1)
        e_zero0, e_zero1, e_win = Event("mixer_zeros", 2), Event("gla_zeros"), Event("w_in_done")
        e_qkin, e_qk, e_xbcin, e_conv, e_xs = Event("qk_in", 2), Event("qk_roped"), Event("xbc_in", 2), Event("conv_done"), Event("conv_silu")
        e_small, e_gqk, e_dav, e_gv, e_sz, e_sg = (Event(n) for n in ("small_in", "gqk_in", "dav_in", "gv_in", "silu_z", "silu_g"))
        e_qT, e_kT = Event("qT_in"), Event("kT_in")
        e_abs, e_ln, e_dta = Event("gate_arguments"), Event("softplus_logs"), Event("dta_ready")
        e_bc, e_gexp, e_gops = Event("gla_cumsums"), Event("gla_exps"), Event("gla_operands")
        e_xh, e_dtx, e_dte, e_xde, e_st = Event("bmT_in"), Event("ssd_decay_arguments"), Event("ssd_decay_exps"), Event("xde_ready"), Event("ssd_state_in")
        e_ux, e_seg, e_segx, e_mt = Event("dta_triangles", 2), Event("segments", 2), Event("segment_exps", 2), Event("ssd_maps", 2)
        e_cbm = Event("cb_masked")
        e_sub, e_sexp, e_attn = Event("scores_shifted", 3), Event("scores_exp", 3), Event("attn_ready", 3)
        e_kendT, e_gat, e_S = Event("kendT_in"), Event("gla_att_masked"), Event("gla_states")
        e_atT, e_mixed, e_mixT = Event("attT_in", 2), Event("mixer_out", 3), Event("mixT_high", 3)
        e_mixTlo = Event("mixT_low", 3)
        e_sgate, e_gu = Event("gate_silu", FC // 2), Event("gu_ready", FC // 2)
        e_pp, e_psig, e_pused = Event("p_proj_in", 2), Event("ple_sigmoid", 2), Event("ple_sigmoid_used", 2, 1)
        e_mrow = Event("modulation_rows", 4)
        steps_apart = sem("steps_apart")
        loaded_c, silu_c = sem("c_loaded"), sem("silu_c_done")
        out_done = sem("out_stored")

        ctx.enter_context(nc.allow_non_contiguous_dma(reason="vectors of parameters, one feature per partition"))
        block = ctx.enter_context(nc.Block())
        cols = lambda name, i: d[name][i].rearrange("(c p) -> p c", p=P)

        def rows(name, i):
            return d[name][i].rearrange("(o n) -> o n", o=1).to_broadcast([P, d[name].shape[1]])

        TOK = CTX + S
        TT = TOK // P
        GH = 2
        NG = NH // GH
        J = GH * TT
        w2 = Bump(work)
        hT = w2.take(KC * TOK)
        hT3 = q3(hT, KC)
        oT = w2.take(NH * TOK)
        oT3 = q3(oT, NH)
        raw = w2.take(2 * 5 * 1024)
        raw3 = raw.rearrange("p (b k n) -> p b k n", b=2, k=5)
        set0 = w2.take(6 * 1024)
        sixths = lambda ap: [ap[:, k * 1024:(k + 1) * 1024] for k in range(ap.shape[1] // 1024)]
        gate_sets = (sixths(set0), sixths(ring[:, 3 * 4096:]) + [raw3[:, 1, 4, :], prm[:, 512:1536]])
        maps = w2.take(1024)
        states = w2.take(3 * 2 * GH * P)
        states5 = states.rearrange("p (c d a v) -> p c d a v", c=3, d=2, a=GH)
        hmask = w2.take(1024 // 4).bitcast(mybir.dt.uint8)
        gate_tots = ((tot_f, tot_b), (p_lam[:, 32:40], p_lam[:, 40:48]))

        def gate_set(b):
            return gate_sets[b]

        def kend_transposed(b):
            return (set0, ring[:, 3 * 4096:])[b][:, 0:12 * P]

        x2n, xctx = raw[:, 0:4096], oT[:, 0:2048]
        x2n3, xctx3 = q3(x2n, TT), q3(xctx, NT)
        y2 = raw[:, 0:4096]
        y23 = q3(y2, TT)
        gtb = raw[:, 6144:8192]
        hT_split = [(rounded(hT[:, c * TOK:(c + 1) * TOK]), ring_r[:, 2 * 4096 + c * TOK:2 * 4096 + (c + 1) * TOK]) for c in range(KC)]
        thousands = lambda ap: ap.rearrange("p (s n) -> p s n", n=1024)

        w3 = Bump(work)
        w3.take(KC * TOK)
        qnT = q3(hT, NH)
        zT = w3.take(NH * S)
        zT3 = q3(zT, NH)
        knT = w3.take(NH * TOK)
        knT3 = q3(knT, NH)
        vv = w3.take(TT * DI)
        vv3 = q3(vv, TT)
        qpe = w3.take(NT * NH * PE_D)
        qpeT = w3.take(NH // 2 * S)
        kpeT2 = w3.take(2 * TOK)
        kvaT, qaT = w3.take(TOK), w3.take(2 * S)
        gtb2 = w3.take(D)
        qkv = vv[:, 2048:2048 + 2 * 448]
        kvc = vv[:, 4096:4096 + 2 * 192]
        kpe = vv[:, 5120:5120 + TT * P]
        rt = vv[:, 6144:8192]
        x3n, xctx_m = set0[:, 0:4096], vv[:, 0:2048]
        hq_tmp = qpeT
        n_a2, n_b2, n_c2 = p_lam[:, 0:8], p_lam[:, 8:16], p_lam[:, 16:24]
        pr_ = qpe
        prT = work[:, 29696:29696 + 1024]
        y3 = knT[:, 0:2048]

        HG_ORDER = ("gf", "gb", "v", "q", "z")
        HG_PIECES = ("gf0", "gf1", "gb0", "gb1", "v0", "v1", "q0", "q1", "z0", "z1")
        pair_pieces = [f"{n}_{b}" for b in range(2) for n in HG_PIECES]
        HW = Ring(thousands(oT[:, 6 * 1024:]), [sem(f"hg_weights_ready{k}") for k in range(2)], [sem("hg_slot_free")], [(n, 1) for n in pair_pieces])
        HS = Split(thousands(ring_r[:, 0:4096]), thousands(ring_r[:, 4096:8192]), sem("hg_high_ready"), dict(pool=sem("hg_low_ready")),
                   sem("hg_split_free"), [(n, "pool") for n in pair_pieces])
        PAIR = [f"{n}{b}" for b in range(2) for n in HG_ORDER]
        HGEMM = Turns(pg, sem("hg_gemm_filled"), [sem("hg_gemm_free0"), sem("hg_gemm_free1")], PAIR)
        HM = Turns(pm, sem("hg_psum_filled"), [sem("hg_psum_free0"), sem("hg_psum_free1")],
                   [f"lev{v}" for v in range(NLEV)] + ["keF", "keB", "stF", "stB", "diag", "o", "oT"])
        m_pieces = ([(f"hgo{k}", 1) for k in range(4)] + [("qkv", 1)] + [(f"z{k}", 1) for k in range(4)]
                    + [("qb0", 1), ("qb1", 1), ("kvb", 1)] + [(f"mo{k}", 1) for k in range(4)])
        MW = Ring(ring3, [sem(f"mla_weights_ready{s}") for s in range(4)], [sem("mla_slot_free")], m_pieces)
        MGEMM = Turns(pg, sem("mla_gemm_filled"), [sem("mla_gemm_free0"), sem("mla_gemm_free1")],
                      ["y0a", "y0b", "y1a", "y1b", "qkv_c", "qkv_l"] + [f"z{k}" for k in range(4)]
                      + ["qn0", "qn1", "qp0", "qn2", "qn3", "qp1"] + [f"kn{k}" for k in range(8)] + [f"v{k}" for k in range(8)]
                      + [f"s{k}" for k in range(NH)] + ["out_t0", "out_t1"])
        heads_order = [f"{n}{k}" for k in range(NH) for n in ("pT", "o")]
        MM = Turns(pm, sem("mla_psum_filled"), [sem("mla_psum_free0"), sem("mla_psum_free1")],
                   ["h0", "h1", "h2", "h3", "diag", "gt0", "gt1", "n0", "n1", "n2", "n3", "gt2", "qaT", "kvpe", "qpeT0", "qpeT1"] + heads_order)
        all_turns = [HGEMM, HM, MGEMM, MM]

        loaded_s2, loaded_ctx, loaded_on, loaded_mask = sem("second_params_loaded"), sem("ctx_loaded"), sem("second_gains_loaded"), sem("masks_loaded")
        s2_sq, s2_xn, s2_hT, s2_g = sem("hg_squares"), sem("hg_rows_normed"), sem("hg_input_ready"), sem("hg_done")
        h_q, h_g, h_v, h_z = Event("hg_q_in"), Event("hg_gates_in", 2), Event("hg_v_in"), Event("hg_z_in")
        h_abs, h_ln, h_karg, h_k = Event("hg_abs", 2), Event("hg_logs"), Event("hg_k_arguments"), Event("hg_k_ready")
        h_d, h_x, h_ops = Event("hg_differences", NLEV), Event("hg_exps", GH * NLEV), Event("hg_operands", GH * NLEV)
        h_iarg, h_iexp, h_iops, h_keT = Event("hg_state_arguments"), Event("hg_state_exps"), Event("hg_state_operands"), Event("hg_kendT_in", 2)
        h_S, h_map, h_og, h_oT = Event("hg_states"), Event("hg_maps"), Event("hg_out_normed"), Event("hg_oT_in")
        h_free, h_ks, h_logs = Event("hg_raw_used", 1, 1), Event("hg_k_summed"), Event("hg_log_gates")
        m_gt, m_gtb, m_y, m_ysq = sem("post_gains"), sem("post_gains_in"), sem("y_in"), sem("y_squares")
        m_x, m_xn, m_hT, m_sq = sem("ctx_updated"), sem("mla_rows_normed"), sem("mla_input_ready"), sem("mla_squares")
        m_qkv, m_qn, m_z = sem("qkv_in"), sem("latents_normed"), sem("mla_z_in")
        m_aT, m_kT = sem("qaT_in"), sem("kva_kpe_in")
        m_qp, m_qpr, m_qpT, m_kn, m_vv = sem("qpe_in"), sem("qpe_roped"), sem("qpeT_in"), sem("heads_in"), sem("mla_v_in")
        m_mx, m_p, m_pn, m_pT, m_o = sem("score_max"), sem("score_exp"), sem("probs_ready"), sem("probsT_in"), sem("mla_out")
        m_yfs, m_fin = sem("y_final_squares"), sem("out_ready")

        hg_w = d["hg_w_in_2"][0].rearrange("(c p) (k g n) -> k g p c n", p=P, k=5, g=NG)
        hg_order = {"q": 0, "v": 1, "gf": 2, "gb": 3, "z": 4}
        tok = lambda ap: ap.rearrange("(t p) n -> p t n", p=P)

        def pairs_loop(eng, body):
            with eng.Fori(0, NG // 2 - 1) as n:
                body(n, True)
            body(NG // 2 - 1, False)

        def second_sp(sp):
            for r in (HW, MW):
                sp.sem_inc(r.free[0], r.r)
            sp.sem_inc(HS.free, HS.r)
            for t in all_turns:
                for f in t.free:
                    sp.sem_inc(f, 1)
            W.all_free(sp, DEPTH)
            SPLIT.all_free(sp, DEPTH)
            with sp.Fori(0, NG // 2) as n:
                for b in range(2):
                    for name in HG_PIECES:
                        which, half = hg_order[name[:-1]], int(name[-1])
                        HW.wait_free(sp, f"{name}_{b}", n)
                        sp.sem_inc(steps_apart, 1)
                        rows, cols_ = (slice(4 * half, 4 * half + 4), slice(0, 256)) if name[0] in "vz" else (slice(0, KC), slice(P * half, P * half + P))
                        dst = HW.slot(f"{name}_{b}").rearrange("p (c n) -> p c n", n=256 if name[0] in "vz" else P)
                        HW.loaded(sp.dma_start(dst, hg_w[which, n * 2 + b, :, rows, cols_]), f"{name}_{b}")
            HW.all_free(sp, NG // 2)
            HS.all_free(sp, NG // 2)

            def piece(name, dst, src):
                MW.wait_free(sp, name)
                MW.loaded(sp.dma_start(dst, src), name)

            c8 = lambda s, n: s[:, 0:KC * n].rearrange("p (c n) -> p c n", c=KC)
            for n in range(2):
                if n == 1:
                    h_oT.wait(sp, NG - 1)
                for k in range(2):
                    name = f"hgo{2 * n + k}"
                    piece(name, c8(MW.slot(name), 512),
                          d["hg_w_out_2"][0, k * D:(k + 1) * D, n * 512:(n + 1) * 512].rearrange("(c p) n -> p c n", p=P))
            win = d["mla_w_in_2"][0].rearrange("(c p) n -> p c n", p=P)
            piece("qkv", c8(MW.slot("qkv"), 448), win[:, :, 0:448])
            for k in range(4):
                piece(f"z{k}", c8(MW.slot(f"z{k}"), 512), win[:, :, 448 + 512 * k:448 + 512 * (k + 1)])
            wqb = d["mla_w_qb_2"][0].rearrange("(c p) n -> p c n", p=P)
            for k in range(2):
                piece(f"qb{k}", MW.slot(f"qb{k}")[:, 0:2 * 1536].rearrange("p (c n) -> p c n", c=2), wqb[:, :, 1536 * k:1536 * (k + 1)])
            piece("kvb", MW.slot("kvb"), d["mla_w_kvb_2"][0])
            wo = d["mla_w_out_2"][0].rearrange("(c p) n -> p c n", p=P)
            for k in range(4):
                piece(f"mo{k}", MW.slot(f"mo{k}").rearrange("p (c n) -> p c n", c=4), wo[:, 4 * k:4 * k + 4, :])
            sp.wait_ge(m_fin, 1)
            sp.dma_start(tok(out[0]), h3).then_inc(out_done, 16)
            sp.wait_ge(out_done, 16)

        def second_pool_early(pool):
            for i in range(DEPTH):
                pool.dma_start(p_pre[:, i * KC:(i + 1) * KC], cols("norm_pre_2", i)).then_inc(loaded_s2, 16)
                pool.dma_start(p_post[:, i * KC:(i + 1) * KC], cols("norm_post_2", i)).then_inc(loaded_s2, 16)
            pool.dma_start(p_qan, cols("mla_qa_norm_2", 0)).then_inc(loaded_s2, 16)
            pool.dma_start(p_kvan, cols("mla_kva_norm_2", 0)).then_inc(loaded_s2, 16)

        def second_pool(pool):
            pool.wait_ge(e_h.sem, 3 * DEPTH)
            pool.dma_start(xctx3, tok(d["ctx_2"][0])).then_inc(loaded_ctx, 16)
            pool.wait_ge(e_h.sem, 3 * DEPTH + 1)
            pool.dma_start(p_sub, rows("hg_o_norm_2", 0)).then_inc(loaded_on, 16)
            pool.dma_start(oT[:, 2048:2048 + (NLEV + 1) * P], d["hmask"]).then_inc(loaded_mask, 16)
            with pool.Fori(0, NG // 2) as n:
                for b in range(2):
                    for piece in HG_PIECES:
                        if piece == "z0":
                            h_logs.wait(pool, n * 2 + b)
                            for k in range(2):
                                last = G.tensor_tensor(raw3[:, b, 1 + k, :], gate_set(b)[4 + k], raw3[:, b, 1 + k, :], ALU.subtract)
                            h_karg.set(pool.drain())
                        name = f"{piece}_{b}"
                        HS.wait_high(pool, name, n)
                        HW.used(G.tensor_tensor(HS.lo(name), HW.slot(name), HS.hi(name).bitcast(f32), ALU.subtract), name)
                        HS.low_done(pool.drain(), name)
            h_free.wait(pool, NG - 1)
            pool.dma_start(q3(xctx_m, NT), tok(d["ctx_2"][0])).then_inc(loaded_ctx, 16)

        def second_act(act):
            act.wait_ge(loaded_ctx, 16)
            for t in range(TT):
                src = xctx3[:, t, :] if t < NT else h3[:, t - NT, :]
                A.activation(oT[:, 3072 + t % NT * D:3072 + (t % NT + 1) * D], src, ACT.Square, accum_out=st_a[:, t:t + 1])
                if t % NT == NT - 1:
                    act.drain().then_inc(s2_sq, 1)
                if t == NT - 1:
                    act.wait_ge(e_h.sem, 3 * DEPTH + 1)

            EVAC = {"q": (0, ACT.Silu, h_q), "gf": (1, ACT.Copy, h_g), "gb": (2, ACT.Copy, h_g), "v": (3, ACT.Copy, h_v), "z": (4, ACT.Silu, h_z)}

            def evac(n, b, name):
                k, func, event = EVAC[name]
                HGEMM.wait_filled(act, f"{name}{b}", n)
                HGEMM.release(A.activation(raw3[:, b if name != "z" else 0, k, :], HGEMM.buf(f"{name}{b}"), func), f"{name}{b}")
                event.set(act.drain())

            def high(n, b, *names):
                for piece in names:
                    name = f"{piece}_{b}"
                    HW.wait_ready(act, name, n)
                    HS.wait_free(act, name, n)
                    A.activation(HS.hi(name), HW.slot(name), ACT.Copy)
                    HS.high_done(act.drain())

            def gate_exp(n, b, k):
                h_abs.wait(act, n * 2 + b, k + 1)
                d_ = gate_set(b)[2 + k]
                A.activation(d_, d_, ACT.Exp, scale=-1.0)

            def gate_ln(n, b):
                act.drain()
                for d_ in gate_set(b)[2:4]:
                    A.activation(d_, d_, ACT.Ln, bias=1.0)
                h_ln.set(act.drain())

            def k_exp(n, b):
                h_karg.wait(act, n * 2 + b)
                for k in (1, 2):
                    A.activation(raw3[:, b, k, :], raw3[:, b, k, :], ACT.Exp)
                h_k.set(act.drain())

            def level_exps(n, b, lev):
                h_d.wait(act, n * 2 + b, lev + 1)
                _, _, dF, dB, EQ, EK = gate_set(b)
                for a in range(GH):
                    v4 = lambda ap: ap[:, a * TOK:(a + 1) * TOK].rearrange("p (n h m) -> p n h m", h=2, m=64 >> lev)
                    A.activation(v4(EQ)[:, :, 0, :], v4(dB)[:, :, 0, :], ACT.Exp, scale=-1.0)
                    A.activation(v4(EQ)[:, :, 1, :], v4(dF)[:, :, 1, :], ACT.Exp)
                    A.activation(v4(EK)[:, :, 0, :], v4(dF)[:, :, 0, :], ACT.Exp, scale=-1.0)
                    A.activation(v4(EK)[:, :, 1, :], v4(dB)[:, :, 1, :], ACT.Exp)
                    h_x.set(act.drain())

            def group(n, b, nxt, after):
                g = n * 2 + b
                bF, cB, dF, dB, EQ, EK = gate_set(b)
                tF, tB = gate_tots[b]
                hkendT = kend_transposed(b)
                if nxt:
                    high(*nxt, "gb0", "gb1")
                for lev in range(NLEV):
                    if lev > 0:
                        HM.wait_filled(act, f"lev{lev - 1}", g)
                        level_exps(n, b, lev)
                    if nxt and lev == 1:
                        high(*nxt, "v0")
                        h_free.wait(act, g, 0)
                        evac(*nxt, "gf")
                    if nxt and lev == 2:
                        high(*nxt, "v1")
                        gate_exp(*nxt, 0)
                    if nxt and lev == 3:
                        high(*nxt, "q0")
                        evac(*nxt, "gb")
                    if nxt and lev == 4:
                        high(*nxt, "q1")
                        gate_exp(*nxt, 1)
                        gate_ln(*nxt)
                    if nxt and lev == 6:
                        k_exp(*nxt)
                        evac(*nxt, "v")
                        high(*nxt, "z0", "z1")
                h_iarg.wait(act, g)
                for dst, src in ((EQ, EQ), (EK, cB), (dF, bF), (dB, dB), (tF, tF), (tB, tB)):
                    A.activation(dst, src, ACT.Exp)
                h_iexp.set(act.drain())
                if nxt:
                    evac(*nxt, "q")
                for k, name in enumerate(("keF", "keB")):
                    HM.wait_filled(act, name, g)
                    HM.release(A.copy(hkendT[:, k * 768:(k + 1) * 768], HM.buf(name)[:, 0:768]), name)
                    h_keT.set(act.drain())
                if nxt:
                    HM.wait_filled(act, "diag", g)
                    level_exps(*nxt, 0)
                if after:
                    high(*after, "gf0", "gf1")
                HM.wait_filled(act, "oT", g)
                dst = oT.rearrange("p (g n) -> p g n", g=NG)
                dst = dst[:, g, :] if isinstance(n, int) else dst[:, bass.ds(g, 1), :].rearrange("p a n -> p (a n)")
                HM.release(A.copy(dst, HM.buf("oT")), "oT")
                h_oT.set(act.drain())
                if nxt:
                    evac(*nxt, "z")

            high(0, 0, *HG_PIECES[:4])
            evac(0, 0, "gf")
            high(0, 0, "v0")
            gate_exp(0, 0, 0)
            high(0, 0, "v1", "q0")
            evac(0, 0, "gb")
            high(0, 0, "q1")
            gate_exp(0, 0, 1)
            gate_ln(0, 0)
            k_exp(0, 0)
            evac(0, 0, "v")
            high(0, 0, "z0", "z1")
            evac(0, 0, "q")
            high(0, 1, "gf0", "gf1")
            MM.wait_filled(act, "diag")
            level_exps(0, 0, 0)
            evac(0, 0, "z")

            def body(n, more):
                group(n, 0, (n, 1), (n + 1, 0) if more else None)
                group(n, 1, (n + 1, 0) if more else None, (n + 1, 1) if more else None)

            pairs_loop(act, body)

            act.wait_ge(m_gt, 1)
            for s in range(2):
                MM.wait_filled(act, f"gt{s}")
                MM.release(A.copy(gtb[:, s * D:(s + 1) * D], MM.buf(f"gt{s}")), f"gt{s}")
                act.drain().then_inc(m_gtb, 1)
            def y_in(n, k):
                name = f"y{n}{'ab'[k]}"
                MGEMM.wait_filled(act, name)
                MGEMM.release(A.copy(y23[:, 2 * k:2 * k + 2, n * 512:(n + 1) * 512], q3(MGEMM.buf(name), 2)), name)

            def squares(x_t, t, junk_):
                A.activation(junk_[:, t % NT * D:(t % NT + 1) * D], x_t, ACT.Square, accum_out=st_a[:, t:t + 1])

            y_in(0, 0)
            y_in(0, 1)
            for s in range(2):
                y_in(1, s)
                act.drain()
                for t in range(s * NT, (s + 1) * NT):
                    squares(y23[:, t, :], t, vv[:, 4096:6144])
                act.drain().then_inc(m_ysq, 1)
                act.wait_ge(m_x, s + 1)
                for t in range(s * NT, (s + 1) * NT):
                    squares(q3(xctx_m, NT)[:, t, :] if s == 0 else h3[:, t - NT, :], t, vv[:, 4096:6144])
                act.drain().then_inc(m_sq, 1)
            for name, dst in (("qkv_c", q3(kvc, NT)), ("qkv_l", q3(qkv, NT))):
                MGEMM.wait_filled(act, name)
                MGEMM.release(A.copy(dst, q3(MGEMM.buf(name), NT)[:, :, 0:dst.shape[2]]), name)
                act.drain().then_inc(m_qkv, 1)
            MM.wait_filled(act, "gt2")
            MM.release(A.copy(gtb2, MM.buf("gt2")), "gt2")
            for k in range(4):
                MGEMM.wait_filled(act, f"z{k}")
                MGEMM.release(A.activation(zT[:, k * 1024:(k + 1) * 1024], MGEMM.buf(f"z{k}"), ACT.Silu), f"z{k}")
            act.drain().then_inc(m_z, 1)
            MM.wait_filled(act, "kvpe")
            b = MM.buf("kvpe")
            for r in range(2):
                pr = slice(r * 64, r * 64 + 64)
                last = A.copy(kpeT2[pr, r * TOK:(r + 1) * TOK], b[pr, 512:1024])
            MM.release(A.activation(kvaT, b[:, 0:512], ACT.Copy, scale=p_kvan), "kvpe")
            act.drain().then_inc(m_kT, 1)
            for k in range(2):
                for c in range(2):
                    name = f"qn{2 * k + c}"
                    MGEMM.wait_filled(act, name)
                    MGEMM.release(A.copy(hT[:, (2 * k + c) * 1024:(2 * k + c + 1) * 1024], MGEMM.buf(name)), name)
                name = f"qp{k}"
                MGEMM.wait_filled(act, name)
                MGEMM.release(A.copy(q3(qpe, NT)[:, :, k * 512:(k + 1) * 512], q3(MGEMM.buf(name), NT)), name)
                act.drain().then_inc(m_qp, 1)
            for k in range(8):
                MGEMM.wait_filled(act, f"kn{k}")
                MGEMM.release(A.copy(knT[:, k * 1024:(k + 1) * 1024], MGEMM.buf(f"kn{k}")), f"kn{k}")
            act.drain().then_inc(m_kn, 1)
            for k in range(8):
                MGEMM.wait_filled(act, f"v{k}")
                MGEMM.release(A.copy(vv3[:, k // 2, (k % 2) * 1024:(k % 2 + 1) * 1024], MGEMM.buf(f"v{k}")), f"v{k}")
            act.drain().then_inc(m_vv, 1)
            for k in range(2):
                MM.wait_filled(act, f"qpeT{k}")
                MM.release(A.copy(qpeT[:, k * 1024:(k + 1) * 1024], MM.buf(f"qpeT{k}")), f"qpeT{k}")
            act.drain().then_inc(m_qpT, 1)

            def probs(k):
                act.wait_ge(m_mx, k + 1)
                for t in range(NT):
                    last = A.activation(pr_[:, (k % 2) * 1024 + t * 512:(k % 2) * 1024 + (t + 1) * 512], MGEMM.buf(f"s{k}")[:, t * 512:(t + 1) * 512], ACT.Exp,
                                        bias=st_b[:, (k % 2) * 2 + t:(k % 2) * 2 + t + 1], scale=MLA_SCALE, accum_out=st_c[:, (k % 2) * 2 + t:(k % 2) * 2 + t + 1])
                MGEMM.release(act.drain(), f"s{k}")
                act.drain().then_inc(m_p, 1)

            probs(0)
            probs(1)
            for k in range(NH):
                MM.wait_filled(act, f"pT{k}")
                MM.release(A.copy(prT, MM.buf(f"pT{k}")), f"pT{k}")
                act.drain().then_inc(m_pT, 1)
                if k + 2 < NH:
                    probs(k + 2)
            for t in range(NT):
                MGEMM.wait_filled(act, f"out_t{t}")
                A.activation(vv[:, t * D:(t + 1) * D], MGEMM.buf(f"out_t{t}"), ACT.Square, accum_out=st_a[:, t:t + 1])
                act.drain().then_inc(m_yfs, 1)

        def second_pe(pe):
            def mm(out_, lhsT, rhs, first=True, last=True):
                return T.matmul(out_, lhsT, rhs, start=first, stop=last)

            def tr(out_, in_):
                return T.transpose(out_, in_, ident)

            def stream_transposes(names, src, normed, streams=range(2)):
                for a in (2 * s_ + f_ for s_ in streams for f_ in range(2)):
                    s, f, name = a // 2, a % 2, f"{names}{a}"
                    pe.wait_ge(normed, s + 1)
                    MM.wait_free(pe, name)
                    for c in range(4):
                        for t in range(NT):
                            last = tr(MM.buf(name)[:, c * S + t * P:c * S + (t + 1) * P], src[:, 2 * s + t, (4 * f + c) * P:(4 * f + c + 1) * P])
                    MM.done(last)

            def triple(out_, lhsT, rhs, first, last):
                (lh, ll), (rh, rl) = lhsT, rhs
                mm(out_, lh, rl, first, False)
                mm(out_, ll, rh, False, False)
                return mm(out_, lh, rh, False, last)

            stream_transposes("h", x2n3, s2_xn)
            pe.wait_ge(s2_hT, 1)

            def project(n, b, unit):
                name, half = HG_ORDER[unit // 2], unit % 2
                pieces = [f"{name}{k}_{b}" for k in range(2)]
                if half == 0:
                    HGEMM.wait_free(pe, f"{name}{b}", n)
                o_ = HGEMM.buf(f"{name}{b}")
                if name in ("v", "z"):
                    if half == 0:
                        for p_ in pieces:
                            HS.wait_low(pe, p_, n)
                    wt = [tuple(x.rearrange("p (c n) -> p c n", n=256) for x in (HS.hi(p_), HS.lo(p_))) for p_ in pieces]
                    for j in (2 * half, 2 * half + 1):
                        for c in range(KC):
                            last = triple(o_[:, j * 256:(j + 1) * 256], [x[:, j * P:(j + 1) * P] for x in hT_split[c]],
                                          [x[:, c % 4, :] for x in wt[c // 4]], c == 0, c == KC - 1)
                else:
                    HS.wait_low(pe, pieces[half], n)
                    wt = [x.rearrange("p (c n) -> p c n", n=P) for x in (HS.hi(pieces[half]), HS.lo(pieces[half]))]
                    for c in range(KC):
                        last = triple(o_[:, half * 512:(half + 1) * 512], [x[:, c, :] for x in wt], hT_split[c], c == 0, c == KC - 1)
                if half:
                    HGEMM.done(last)
                if name not in ("v", "z"):
                    HS.used(pe.drain())
                elif half:
                    pe.drain().then_inc(HS.free, 2)

            def level(n, b, lev):
                g = n * 2 + b
                name = f"lev{lev}"
                EQ, EK = gate_set(b)[4:6]
                HM.wait_free(pe, name, g)
                for j in range(J):
                    if j % TT == 0:
                        h_ops.wait(pe, g, GH * lev + j // TT + 1)
                    cs = slice(j * P, (j + 1) * P)
                    last = mm(HM.buf(name)[:, cs], EK[:, cs], EQ[:, cs])
                HM.done(last)

            def diagonal(n, b, turns, turn):
                h_ks.wait(pe, n * 2 + b)
                h_q.wait(pe, n * 2 + b)
                turns.wait_free(pe, "diag", turn)
                ks = gate_set(b)[5]
                for j in range(J):
                    cs = slice(j * P, (j + 1) * P)
                    last = mm(turns.buf("diag")[:, cs], ks[:, cs], raw3[:, b, 0, cs])
                turns.done(last)

            def out_head(n, hd, tiles=range(TT)):
                k, c = hd // KC, hd % KC
                name = f"hgo{2 * n + k}"
                if hd == 0:
                    for ab in sorted({"ab"[t // 2] for t in tiles}):
                        MGEMM.wait_free(pe, f"y{n}{ab}")
                if c == 0 and 0 in tiles:
                    MW.wait_ready(pe, name)
                wt = MW.slot(name).rearrange("p (c n) -> p c n", c=KC)
                for t in tiles:
                    y_ = f"y{n}{'ab'[t // 2]}"
                    last = mm(MGEMM.buf(y_)[:, (t % 2) * 512:(t % 2 + 1) * 512], oT3[:, hd, t * P:(t + 1) * P], wt[:, c, :], hd == 0, hd == NH - 1)
                    if hd == NH - 1 and t % 2:
                        MGEMM.done(last)
                if c == KC - 1 and TT - 1 in tiles:
                    MW.used(pe.drain())

            FWD, BWD = (0, 1, 2), (1, 0, 3)

            def group(n, b, nxt):
                g = n * 2 + b
                dF, dB, EQ, EK = gate_set(b)[2:6]
                hkendT = kend_transposed(b)
                heads_out = iter(range(NH - GH))

                def between(units, heads):
                    if nxt:
                        for unit in units:
                            project(*nxt, unit)
                    else:
                        for _ in range(heads):
                            out_head(0, next(heads_out))

                if not nxt:
                    h_z.wait(pe, NG - 1)
                    h_oT.wait(pe, NG - 2)
                for lev in range(NLEV):
                    between([lev] if lev < 6 else [], 1)
                    level(n, b, lev)
                between([6, 7], 4)
                v4 = raw3[:, b, 3, :].rearrange("p (t a v) -> p t a v", t=TT, a=GH)
                h_iops.wait(pe, g)
                for name, src, tiles in (("keF", EQ, FWD), ("keB", EK, BWD)):
                    HM.wait_free(pe, name, g)
                    for c, t in enumerate(tiles):
                        for a in range(GH):
                            last = tr(HM.buf(name)[:, (c * GH + a) * P:(c * GH + a + 1) * P], src[:, (a * TT + t) * P:(a * TT + t + 1) * P])
                    HM.done(last)
                h_v.wait(pe, g)
                for k, (name, tiles) in enumerate((("stF", FWD), ("stB", BWD))):
                    h_keT.wait(pe, g, k + 1)
                    HM.wait_free(pe, name, g)
                    for c, t in enumerate(tiles):
                        for a in range(GH):
                            at = (c * GH + a) * P
                            last = mm(HM.buf(name)[:, at:at + P], hkendT[:, k * 768 + at:k * 768 + at + P], v4[:, t, a, :])
                    HM.done(last)
                if nxt:
                    diagonal(*nxt, HM, g)
                else:
                    HM.wait_free(pe, "diag", g)
                    HM.done(tr(HM.buf("diag")[:, 0:P], ident))
                h_map.wait(pe, g)
                h_S.wait(pe, g)
                HM.wait_free(pe, "o", g)
                for t in range(TT):
                    for a in range(GH):
                        o_ = HM.buf("o")[:, (t * GH + a) * P:(t * GH + a + 1) * P]
                        cs = slice((a * TT + t) * P, (a * TT + t + 1) * P)
                        parts = [(maps[:, cs], v4[:, t, a, :])]
                        if t > 0:
                            parts.append((dF[:, cs], states5[:, t - 1, 0, a, :]))
                        if t != 1:
                            parts.append((dB[:, cs], states5[:, {0: 0, 3: 1, 2: 2}[t], 1, a, :]))
                        for k, (l_, r_) in enumerate(parts):
                            last = mm(o_, l_, r_, k == 0, k == len(parts) - 1)
                HM.done(last)
                between([8, 9], 3)
                h_og.wait(pe, g)
                HM.wait_free(pe, "oT", g)
                for a in range(GH):
                    for t in range(TT):
                        last = tr(HM.buf("oT")[:, (a * TT + t) * P:(a * TT + t + 1) * P], EQ[:, (t * GH + a) * P:(t * GH + a + 1) * P])
                HM.done(last)

            for unit in range(8):
                project(0, 0, unit)
            diagonal(0, 0, MM, 0)
            for unit in range(8, 10):
                project(0, 0, unit)

            def body(n, more):
                group(n, 0, (n, 1))
                group(n, 1, (n + 1, 0) if more else None)

            pairs_loop(pe, body)

            pe.wait_ge(m_gt, 1)
            dg = maps

            def spread(name):
                MM.wait_free(pe, name)
                for c in range(2):
                    last = mm(MM.buf(name)[:, c * 512:(c + 1) * 512], ones, dg[:, c * 512:(c + 1) * 512])
                MM.done(last)

            h_oT.wait(pe, NG - 1)
            spread("gt0")
            pe.wait_ge(m_gt, 2)
            spread("gt1")
            for hd in range(NH - GH, NH):
                out_head(0, hd)
            for s in range(2):
                for hd in range(NH):
                    out_head(1, hd, range(s * NT, (s + 1) * NT))

            MW.wait_ready(pe, "qkv")
            wt = MW.slot("qkv")[:, 0:KC * 448].rearrange("p (c n) -> p c n", c=KC)
            for s, (name, t0, lo) in enumerate((("qkv_c", 0, QR), ("qkv_l", NT, 0))):
                stream_transposes("n", q3(x3n, TT), m_xn, (s,))
                pe.wait_ge(m_hT, s + 1)
                MGEMM.wait_free(pe, name)
                for t in range(NT):
                    for c in range(KC):
                        last = mm(MGEMM.buf(name)[:, t * 512:t * 512 + 448 - lo], hT3[:, c, (t0 + t) * P:(t0 + t + 1) * P], wt[:, c, lo:448],
                                  c == 0, c == KC - 1)
                MGEMM.done(last)
            MW.used(pe.drain())
            pe.wait_ge(m_gt, 3)
            spread("gt2")
            for k in range(4):
                name = f"z{k}"
                MW.wait_ready(pe, name)
                MGEMM.wait_free(pe, name)
                wt = MW.slot(name).rearrange("p (c n) -> p c n", c=KC)
                for f in range(4):
                    for c in range(KC):
                        last = mm(MGEMM.buf(name)[:, f * S:(f + 1) * S], wt[:, c, f * P:(f + 1) * P], hT3[:, c, CTX:TOK], c == 0, c == KC - 1)
                MGEMM.done(last)
                MW.used(pe.drain())
            pe.wait_ge(m_qn, 1)
            MM.wait_free(pe, "qaT")
            for c in range(2):
                for t in range(NT):
                    last = tr(MM.buf("qaT")[:, c * S + t * P:c * S + (t + 1) * P], q3(qkv, NT)[:, t, c * P:(c + 1) * P])
            MM.done(last)
            MM.wait_free(pe, "kvpe")
            b = MM.buf("kvpe")
            for t in range(TT):
                src = q3(kvc, NT)[:, t, 0:KVR] if t < NT else q3(qkv, NT)[:, t - NT, QR:QR + KVR]
                tr(b[:, t * P:(t + 1) * P], src)
            for t in range(TT):
                last = tr(b[:, 512 + t * P:512 + (t + 1) * P], q3(kpe, TT)[:, t, :])
            MM.done(last)
            pe.wait_ge(m_aT, 1)
            qa3 = q3(qaT, 2)
            for k in range(2):
                MW.wait_ready(pe, f"qb{k}")
                wt = MW.slot(f"qb{k}")[:, 0:3072].rearrange("p (c h n) -> p c h n", c=2, h=8)
                for q4 in range(2):
                    name = f"qn{2 * k + q4}"
                    MGEMM.wait_free(pe, name)
                    for a in range(4):
                        for c in range(2):
                            last = mm(MGEMM.buf(name)[:, a * S:(a + 1) * S], wt[:, c, 4 * q4 + a, 0:P], qa3[:, c, :], c == 0, c == 1)
                    MGEMM.done(last)
                name = f"qp{k}"
                MGEMM.wait_free(pe, name)
                for t in range(NT):
                    for c in range(2):
                        last = mm(MGEMM.buf(name)[:, t * 512:(t + 1) * 512], qa3[:, c, t * P:(t + 1) * P], wt[:, c, :, P:P + PE_D], c == 0, c == 1)
                MGEMM.done(last)
                MW.used(pe.drain())
            pe.wait_ge(m_kT, 1)
            MW.wait_ready(pe, "kvb")
            wt = MW.slot("kvb").rearrange("p (h n) -> p h n", h=NH)
            for k in range(8):
                MGEMM.wait_free(pe, f"kn{k}")
                for a in range(2):
                    last = mm(MGEMM.buf(f"kn{k}")[:, a * 512:(a + 1) * 512], wt[:, 2 * k + a, 0:P], kvaT)
                MGEMM.done(last)
            for k in range(8):
                MGEMM.wait_free(pe, f"v{k}")
                for a in range(2):
                    h0 = (k % 2) * 8 + a * 4
                    last = mm(MGEMM.buf(f"v{k}")[:, a * 512:(a + 1) * 512], kvaT[:, (k // 2) * P:(k // 2 + 1) * P], wt[:, h0:h0 + 4, P:2 * P])
                MGEMM.done(last)
            MW.used(pe.drain())
            pe.wait_ge(m_qpr, 1)
            for k in range(2):
                MM.wait_free(pe, f"qpeT{k}")
                for c in range(4):
                    for t in range(NT):
                        last = tr(MM.buf(f"qpeT{k}")[:, c * S + t * P:c * S + (t + 1) * P], q3(qpe, NT)[:, t, (4 * k + c) * P:(4 * k + c + 1) * P])
                MM.done(last)
            pe.wait_ge(m_qpT, 1)
            pe.wait_ge(m_kn, 1)

            def scores(k):
                MGEMM.wait_free(pe, f"s{k}")
                for t in range(NT):
                    o_ = MGEMM.buf(f"s{k}")[:, t * 512:(t + 1) * 512]
                    mm(o_, qnT[:, k, t * P:(t + 1) * P], knT3[:, k, :], True, False)
                    last = mm(o_, qpeT[:, (k // 2) * S + t * P:(k // 2) * S + (t + 1) * P], kpeT2[:, (k % 2) * TOK:(k % 2 + 1) * TOK], False, True)
                MGEMM.done(last)

            pe.wait_ge(m_vv, 1)
            scores(0)
            scores(1)
            for k in range(NH):
                pe.wait_ge(m_pn, k + 1)
                MM.wait_free(pe, f"pT{k}")
                p3 = pr_[:, (k % 2) * 1024:(k % 2 + 1) * 1024].rearrange("p (t n) -> p t n", t=NT)
                for c in range(TT):
                    for t in range(NT):
                        last = tr(MM.buf(f"pT{k}")[:, c * S + t * P:c * S + (t + 1) * P], p3[:, t, c * P:(c + 1) * P])
                MM.done(last)
                if k + 2 < NH:
                    scores(k + 2)
                pe.wait_ge(m_pT, k + 1)
                MM.wait_free(pe, f"o{k}")
                for c in range(TT):
                    last = mm(MM.buf(f"o{k}")[:, 0:S], vv3[:, c, k * P:(k + 1) * P], prT[:, c * S:(c + 1) * S], c == 0, c == TT - 1)
                MM.done(last)
            pe.wait_ge(m_o, NH)
            for t in range(NT):
                MGEMM.wait_free(pe, f"out_t{t}")
            for k in range(4):
                MW.wait_ready(pe, f"mo{k}")
                wt = MW.slot(f"mo{k}").rearrange("p (c n) -> p c n", c=4)
                for c in range(4):
                    hd = 4 * k + c
                    for t in range(NT):
                        for e in range(2):
                            last = mm(MGEMM.buf(f"out_t{t}")[:, e * 512:(e + 1) * 512], zT3[:, hd, t * P:(t + 1) * P], wt[:, c, e * 512:(e + 1) * 512],
                                      hd == 0, hd == NH - 1)
                        if hd == NH - 1:
                            MGEMM.done(last)
                MW.used(pe.drain())

        def second_dve(dve):
            dve.wait_ge(loaded_s2, 16 * (2 * DEPTH + 2))
            dve.wait_ge(loaded_ctx, 16)
            ctx_lat = (1, 0)

            def mod_gains(i):
                V.tensor_scalar(g1, mods4[:, i, 8:16, :].rearrange("p c s -> p (c s)"), 1.0, None, ALU.add)
                dve.drain()
                V.tensor_tensor(g1.rearrange("p (c s) -> p c s", s=2), g1.rearrange("p (c s) -> p c s", s=2),
                                bc(p_pre[:, i * KC:(i + 1) * KC], [KC, 2], 2), ALU.mult)
                V.tensor_tensor(gtp.rearrange("p (c s) -> p c s", s=2), mods4[:, i, 16:24, :],
                                bc(p_post[:, i * KC:(i + 1) * KC], [KC, 2], 2), ALU.mult)
                dve.drain()

            def stream_norm(xc_, dst, sq, sig, streams=range(2)):
                for s in streams:
                    dve.wait_ge(sq, s + 1)
                    c = slice(s * NT, (s + 1) * NT)
                    V.tensor_scalar(st_b[:, c], st_a[:, c], 1.0 / D, EPS, ALU.mult, ALU.add)
                    dve.drain()
                    rsqrt(dve, st_c[:, c], st_b[:, c], st_m[:, c])
                    for t in range(s * NT, (s + 1) * NT):
                        src = xc_[:, t, :] if t < NT else h3[:, t - NT, :]
                        V.tensor_scalar(dst[:, t, :], src, st_c[:, t:t + 1], None, ALU.mult)
                    dve.drain().then_inc(sig, 1)

            def stream_in(names, i, sig, split=False, streams=range(2)):
                for a in (2 * s_ + f_ for s_ in streams for f_ in range(2)):
                    s, f, name = a // 2, a % 2, f"{names}{a}"
                    m_ = ctx_lat[s]
                    MM.wait_filled(dve, name)
                    for c in range(4):
                        k, cs = 4 * f + c, slice(s * S, (s + 1) * S)
                        dst = hT_split[k][0][:, cs] if split else hT3[:, k, cs]
                        last = V.tensor_scalar(dst, MM.buf(name)[:, c * S:(c + 1) * S], g1[:, 2 * k + m_:2 * k + m_ + 1],
                                               mods4[:, i, k, m_:m_ + 1], ALU.mult, ALU.add)
                    if split:
                        y_ = raw[:, 6144:7168]
                        for c in range(4):
                            k = 4 * f + c
                            V.tensor_scalar(y_[:, c * S:(c + 1) * S], MM.buf(name)[:, c * S:(c + 1) * S], g1[:, 2 * k + m_:2 * k + m_ + 1],
                                            mods4[:, i, k, m_:m_ + 1], ALU.mult, ALU.add)
                        dve.drain()
                        for c in range(4):
                            hi, lo = (x[:, s * S:(s + 1) * S] for x in hT_split[4 * f + c])
                            last = V.tensor_tensor(lo, y_[:, c * S:(c + 1) * S], hi.bitcast(f32), ALU.subtract)
                        dve.drain()
                    MM.release(last, name)
                dve.drain().then_inc(sig, 1)

            mod_gains(0)
            stream_norm(xctx3, x2n3, s2_sq, s2_xn)
            stream_in("h", 0, s2_hT, True)
            dve.wait_ge(loaded_mask, 16)
            dve.wait_ge(loaded_on, 16)
            V.tensor_copy(hmask, oT[:, 2048:2048 + (NLEV + 1) * P])
            dve.drain()
            mask3 = hmask.rearrange("p (l n) -> p l n", l=NLEV + 1)
            maps3 = q3(maps, J)

            j3 = lambda ap: q3(ap, J)

            def gate_abs(n, b, k):
                h_g.wait(dve, n * 2 + b, k + 1)
                V.tensor_scalar(gate_set(b)[2 + k].bitcast(i32), raw3[:, b, 1 + k, :].bitcast(i32), 0x7FFFFFFF, None, ALU.bitwise_and)
                h_abs.set(dve.drain())

            def gate_logs(n, b):
                h_ln.wait(dve, n * 2 + b)
                for k in range(2):
                    V.scalar_tensor_tensor(gate_set(b)[4 + k], raw3[:, b, 1 + k, :], 0.0, gate_set(b)[2 + k], ALU.min, ALU.subtract)
                h_logs.set(dve.drain())

            def running_decays(b):
                bF, cB, _, _, EQ, EK = gate_set(b)
                for src, dst in ((EQ, bF), (EK, cB)):
                    for j in range(J):
                        cs = slice(j * P, (j + 1) * P)
                        V.tensor_tensor_scan(dst[:, cs], ones, src[:, cs], 0.0, ALU.mult, ALU.add)
                dve.drain()
                V.tensor_copy(gate_tots[b][0], j3(bF)[:, :, P - 1])
                V.tensor_copy(gate_tots[b][1], j3(cB)[:, :, P - 1])
                dve.drain()
                V.tensor_tensor(cB, cB, EK, ALU.subtract)
                dve.drain()

            def k_sum(n, b):
                h_k.wait(dve, n * 2 + b)
                V.tensor_tensor(gate_set(b)[5], raw3[:, b, 1, :], raw3[:, b, 2, :], ALU.add)
                h_ks.set(dve.drain())

            def differences(b, lev):
                bF, cB, dF, dB, _, _ = gate_set(b)
                m = 64 >> lev
                v4 = lambda ap: ap.rearrange("p (n h m) -> p n h m", h=2, m=m)
                v3 = lambda ap: ap.rearrange("p (n k) -> p n k", k=2 * m)
                nb = 1024 // (2 * m)
                V.tensor_tensor(v3(dF), v3(bF), v4(bF)[:, :, 0, m - 1:m].to_broadcast([P, nb, 2 * m]), ALU.subtract)
                V.tensor_tensor(v3(dB), v3(cB), v4(cB)[:, :, 1, 0:1].to_broadcast([P, nb, 2 * m]), ALU.subtract)
                h_d.set(dve.drain())

            def keep(lev, turns, name, turn):
                turns.wait_filled(dve, name, turn)
                dve.sem_inc(steps_apart, 1)
                turns.release(V.copy_predicated(maps3, bc(mask3[:, lev, :], [J, P], 1), j3(turns.buf(name))), name)

            def group(n, b, nxt):
                g = n * 2 + b
                q_, kf, kb = (raw3[:, b, k, :] for k in range(3))
                z_ = raw3[:, 0, 4, :]
                bF, cB, dF, dB, EQ, EK = gate_set(b)
                tF, tB = gate_tots[b]
                h_q.wait(dve, g)
                for lev in range(NLEV):
                    for a in range(GH):
                        ha = lambda ap: ap[:, a * TOK:(a + 1) * TOK]
                        v4 = lambda ap: ha(ap).rearrange("p (n h m) -> p n h m", h=2, m=64 >> lev)
                        h_x.wait(dve, g, GH * lev + a + 1)
                        V.tensor_tensor(ha(EQ), ha(EQ), ha(q_), ALU.mult)
                        V.tensor_tensor(v4(EK)[:, :, 0, :], v4(EK)[:, :, 0, :], v4(kf)[:, :, 0, :], ALU.mult)
                        V.tensor_tensor(v4(EK)[:, :, 1, :], v4(EK)[:, :, 1, :], v4(kb)[:, :, 1, :], ALU.mult)
                        h_ops.set(dve.drain())
                    if lev + 1 < NLEV:
                        differences(b, lev + 1)
                    keep(lev, HM, f"lev{lev}", g)
                    if nxt and lev == 1:
                        gate_abs(*nxt, 0)
                    if nxt and lev == 3:
                        gate_abs(*nxt, 1)
                    if nxt and lev == 4:
                        gate_logs(*nxt)
                h_map.set(dve.drain())
                V.tensor_tensor(j3(EQ), bc(tF, [J, P], 2), j3(bF), ALU.subtract)
                V.tensor_tensor(j3(dB), bc(tB, [J, P], 2), j3(cB), ALU.subtract)
                h_iarg.set(dve.drain())
                if nxt:
                    running_decays(nxt[1])
                h_iexp.wait(dve, g)
                V.tensor_tensor(EQ, EQ, kf, ALU.mult)
                V.tensor_tensor(EK, EK, kb, ALU.mult)
                h_iops.set(dve.drain())
                if nxt:
                    k_sum(*nxt)
                for k, (name, tiles, tot) in enumerate((("stF", (0, 1, 2), tF), ("stB", (1, 0, 3), tB))):
                    HM.wait_filled(dve, name, g)
                    src = HM.buf(name)[:, 0:768].rearrange("p (c a v) -> p c a v", c=3, a=GH)
                    V.tensor_copy(states5[:, 0, k, :, :], src[:, 0])
                    dve.drain()
                    for c in (1, 2):
                        for a in range(GH):
                            j = a * TT + tiles[c]
                            last = V.scalar_tensor_tensor(states5[:, c, k, a, :], states5[:, c - 1, k, a, :], tot[:, j:j + 1], src[:, c, a, :],
                                                          ALU.mult, ALU.add)
                        if c == 1:
                            dve.drain()
                    HM.release(last, name)
                V.tensor_tensor(dF, dF, q_, ALU.mult)
                V.tensor_tensor(dB, dB, q_, ALU.mult)
                h_S.set(dve.drain())
                if nxt:
                    differences(nxt[1], 0)
                HM.wait_filled(dve, "o", g)
                HM.release(V.tensor_copy(EQ, HM.buf("o")), "o")
                if nxt:
                    keep(NLEV, HM, "diag", g)
                else:
                    HM.wait_filled(dve, "diag", g)
                    HM.release(dve.drain(), "diag")
                dve.drain()
                V.tensor_tensor(EK, EQ, EQ, ALU.mult)
                dve.drain()
                V.tensor_reduce(st_a[:, 0:J], j3(EK), AX.X, ALU.add)
                dve.drain()
                V.tensor_scalar(st_b[:, 0:J], st_a[:, 0:J], 1.0 / P, EPS, ALU.mult, ALU.add)
                dve.drain()
                rsqrt(dve, st_c[:, 0:J], st_b[:, 0:J], st_m[:, 0:J])
                V.tensor_tensor(j3(EQ), j3(EQ), bc(st_c, [J, P], 2), ALU.mult)
                dve.drain()
                V.tensor_tensor(j3(EQ), j3(EQ), bc(p_sub, [J, P], 1), ALU.mult)
                dve.drain()
                h_z.wait(dve, g)
                V.tensor_tensor(EQ, EQ, z_, ALU.mult)
                h_og.set(dve.drain())
                h_free.set(dve.drain())

            gate_abs(0, 0, 0)
            gate_abs(0, 0, 1)
            gate_logs(0, 0)
            running_decays(0)
            k_sum(0, 0)
            differences(0, 0)
            keep(NLEV, MM, "diag", 0)

            def body(n, more):
                group(n, 0, (n, 1))
                group(n, 1, (n + 1, 0) if more else None)

            pairs_loop(dve, body)

            mod_gains_post = gtp.rearrange("p (c s) -> p c s", s=2)

            def diag(s, count):
                V.tensor_tensor(q3(maps, KC), bc(ident, [KC, P], 1), bc(mod_gains_post[:, :, s], [KC, P], 2), ALU.mult)
                dve.drain().then_inc(m_gt, 1)

            diag(ctx_lat[0], 1)
            dve.wait_ge(m_gtb, 1)
            diag(ctx_lat[1], 2)
            dve.wait_ge(m_gtb, 2)

            def post(y_t, rstd_col, gain, x_t):
                V.scalar_tensor_tensor(y_t, y_t, rstd_col, gain, ALU.mult, ALU.mult)
                dve.drain()
                V.tensor_tensor(x_t, x_t, y_t, ALU.add)

            mod_gains(1)
            dve.wait_ge(loaded_ctx, 32)
            for s in range(2):
                dve.wait_ge(m_ysq, s + 1)
                c = slice(s * NT, (s + 1) * NT)
                V.tensor_scalar(st_b[:, c], st_a[:, c], 1.0 / D, EPS, ALU.mult, ALU.add)
                dve.drain()
                rsqrt(dve, st_c[:, c], st_b[:, c], st_m[:, c])
                for t in range(s * NT, (s + 1) * NT):
                    post(y23[:, t, :], st_c[:, t:t + 1], gtb[:, s * D:(s + 1) * D], q3(xctx_m, NT)[:, t, :] if s == 0 else h3[:, t - NT, :])
                dve.drain().then_inc(m_x, 1)
                stream_norm(q3(xctx_m, NT), q3(x3n, TT), m_sq, m_xn, (s,))
                stream_in("n", 1, m_hT, streams=(s,))
            diag(ctx_lat[1], 3)
            dve.wait_ge(m_qkv, 2)
            q_l, kv_c = q3(qkv, NT), q3(kvc, NT)
            parts = [(q_l[:, t, 0:QR], QR) for t in range(NT)] + [(kv_c[:, t, 0:KVR], KVR) for t in range(NT)] + [(q_l[:, t, QR:QR + KVR], KVR) for t in range(NT)]
            for k, (x, n) in enumerate(parts):
                V.tensor_tensor(rt[:, k * 256:k * 256 + n], x, x, ALU.mult)
            dve.drain()
            for k, (x, n) in enumerate(parts):
                V.tensor_reduce(n_a2[:, k:k + 1], rt[:, k * 256:k * 256 + n], AX.X, ALU.add)
            dve.drain()
            for k0, k1, n in ((0, 2, QR), (2, 6, KVR)):
                V.tensor_scalar(n_b2[:, k0:k1], n_a2[:, k0:k1], 1.0 / n, EPS, ALU.mult, ALU.add)
            dve.drain()
            rsqrt(dve, n_c2[:, 0:6], n_b2[:, 0:6], n_a2[:, 0:6])
            for k, (x, n) in enumerate(parts):
                V.tensor_scalar(x, x, n_c2[:, k:k + 1], None, ALU.mult)
            kpe4 = kpe.rearrange("p (t r e) -> p t r e", t=TT, r=2)
            cos3, sin3 = q3(C["ax_cos"], NT), q3(C["ax_sin"], NT)
            for r in range(2):
                V.tensor_copy(kpe4[:, 0:NT, r, :], kv_c[:, :, KVR:KVR + PE_D])
            x1, x2 = q_l[:, :, QR + KVR:QR + KVR + 32], q_l[:, :, QR + KVR + 32:QR + KVR + 64]
            r4 = [q3(rt[:, 1536 + k * 64:1536 + (k + 1) * 64], NT) for k in range(4)]
            for dst, x, cs in ((r4[0], x1, cos3), (r4[1], x2, sin3), (r4[2], x1, sin3), (r4[3], x2, cos3)):
                V.tensor_tensor(dst, x, cs, ALU.mult)
            dve.drain()
            for r in range(2):
                V.tensor_tensor(kpe4[:, NT:TT, r, 0:32], r4[0], r4[1], ALU.subtract)
                V.tensor_tensor(kpe4[:, NT:TT, r, 32:64], r4[2], r4[3], ALU.add)
            MM.wait_filled(dve, "gt2")
            V.memset(kpeT2, 0.0)
            dve.drain().then_inc(m_qn, 1)
            MM.wait_filled(dve, "qaT")
            for c in range(2):
                last = V.tensor_scalar(qaT[:, c * S:(c + 1) * S], MM.buf("qaT")[:, c * S:(c + 1) * S], p_qan[:, c:c + 1], None, ALU.mult)
            MM.release(last, "qaT")
            dve.drain().then_inc(m_aT, 1)
            dve.wait_ge(m_qp, 2)
            for t in range(NT):
                x = qpe[:, t * 1024:(t + 1) * 1024].rearrange("p (a e) -> p a e", a=NH)
                x1, x2 = x[:, :, 0:32], x[:, :, 32:64]
                cs, sn = (bc(v[:, t, :], [NH, 32], 1) for v in (cos3, sin3))
                r4 = [q3(hq_tmp[:, k * 512:(k + 1) * 512], NH) for k in range(4)]
                for dst, x_, c_ in ((r4[0], x1, cs), (r4[1], x2, sn), (r4[2], x1, sn), (r4[3], x2, cs)):
                    V.tensor_tensor(dst, x_, c_, ALU.mult)
                dve.drain()
                V.tensor_tensor(x1, r4[0], r4[1], ALU.subtract)
                V.tensor_tensor(x2, r4[2], r4[3], ALU.add)
                dve.drain()
            dve.drain().then_inc(m_qpr, 1)

            def score_max(k):
                MGEMM.wait_filled(dve, f"s{k}")
                cs = slice((k % 2) * 2, (k % 2) * 2 + 2)
                V.tensor_reduce(st_m[:, cs], q3(MGEMM.buf(f"s{k}"), NT), AX.X, ALU.max)
                dve.drain()
                V.tensor_scalar(st_b[:, cs], st_m[:, cs], -MLA_SCALE, None, ALU.mult)
                dve.drain().then_inc(m_mx, 1)

            def normalise(k):
                dve.wait_ge(m_p, k + 1)
                cs = slice((k % 2) * 2, (k % 2) * 2 + 2)
                V.reciprocal(st_a[:, cs], st_c[:, cs])
                dve.drain()
                for t in range(NT):
                    x = pr_[:, (k % 2) * 1024 + t * 512:(k % 2) * 1024 + (t + 1) * 512]
                    V.tensor_scalar(x, x, st_a[:, (k % 2) * 2 + t:(k % 2) * 2 + t + 1], None, ALU.mult)
                dve.drain().then_inc(m_pn, 1)

            dve.wait_ge(m_z, 1)
            for k in range(2):
                score_max(k)
            for k in range(2):
                normalise(k)
            for k in range(NH):
                if k + 2 < NH:
                    score_max(k + 2)
                MM.wait_filled(dve, f"o{k}")
                MM.release(V.tensor_tensor(zT3[:, k, :], zT3[:, k, :], MM.buf(f"o{k}")[:, 0:S], ALU.mult), f"o{k}")
                dve.drain().then_inc(m_o, 1)
                if k + 2 < NH:
                    normalise(k + 2)
            for t in range(NT):
                dve.wait_ge(m_yfs, t + 1)
                V.tensor_scalar(st_b[:, t:t + 1], st_a[:, t:t + 1], 1.0 / D, EPS, ALU.mult, ALU.add)
                dve.drain()
                rsqrt(dve, st_c[:, t:t + 1], st_b[:, t:t + 1], st_m[:, t:t + 1])
                y_t = y3[:, t * D:(t + 1) * D]
                V.scalar_tensor_tensor(y_t, MGEMM.buf(f"out_t{t}"), st_c[:, t:t + 1], gtb2, ALU.mult, ALU.mult)
                dve.drain()
                V.tensor_tensor(h3[:, t, :], h3[:, t, :], y_t, ALU.add)
            dve.drain().then_inc(m_fin, 1)


        @block.sync
        def _(sp):
            for f in W.free:
                sp.sem_inc(f, 1)
            sp.sem_inc(SPLIT.free, SPLIT.r)
            for s in GEMM.free + M.free:
                sp.sem_inc(s, 1)
            for e in (e_h, e_pused, h_free):
                sp.sem_inc(e.sem, e.start)
            sp.dma_start(cst[:], d["cst"]).then_inc(loaded_const, 16)
            sp.dma_start(h3, d["x"][0].rearrange("(t p) n -> p t n", p=P)).then_inc(loaded_h, 16)

            def piece(name, i, *parts):
                W.wait_free(sp, name, i)
                for dst, src in parts:
                    W.loaded(sp.dma_start(dst(W.slot(name)), src), name)

            def layer_parameters(i):
                small_loads = [
                    (p_convb, cols("ssd_conv_b", i)),
                    (p_qkg[:, 0:DQK], rows("da_q_norm", i)), (p_qkg[:, DQK:], rows("da_k_norm", i)),
                    (p_bgate, cols("gla_b_gate", i)), (p_wg2[0:GLA_R, :], d["gla_w_gate2"][i]),
                    (p_dtb, rows("ssd_dt_bias", i)), (p_alog, rows("ssd_a_log", i)),
                    (p_lam[:, 0:64], rows("da_lambda_q1", i)), (p_lam[:, 64:128], rows("da_lambda_k1", i)),
                    (p_lam[:, 128:192], rows("da_lambda_q2", i)), (p_lam[:, 192:256], rows("da_lambda_k2", i)),
                    (p_dskip, rows("ssd_d", i)), (p_ssdn, rows("ssd_norm", i)), (p_glan, rows("gla_norm", i)),
                    (p_sub, rows("da_sub_norm", i)),
                    (p_ffn, cols("ffn_norm", i)), (p_li, d["lam"][i]),
                    (p_adab, d["ada_b_2"][i].rearrange("(c p) -> p c", p=P)),
                ]
                for j in range(4):
                    small_loads.insert(1 + j, (convw3[:, j, :], d["ssd_conv_w"][i, j].rearrange("(c p) -> p c", p=P)))
                for dst, src in small_loads:
                    sp.dma_start(dst, src).then_inc(loaded_prm, 16)
                assert len(small_loads) == N_PRM

            whole8 = lambda s: s.rearrange("p (c n) -> p c n", c=KC)
            whole2 = lambda s: s.rearrange("p (c n) -> p c n", c=2)
            small8 = lambda s: s[:, 0:KC * 24].rearrange("p (c n) -> p c n", c=KC)
            with sp.Fori(0, DEPTH) as i:
                win = d["w_in"][i].rearrange("(c p) n -> p c n", p=P)
                at = dict(daq=C_DAQ, dak=C_DAK, xbc0=C_XBC, xbc1=C_XBC + 512, gqk=C_GQ, dav=C_DAV, gv=C_GV, z=C_Z, gg=C_GG)
                for name in w_in_pieces:
                    if name == "xbc0_0":
                        e_h.wait(sp, i, 0)
                        sp.sem_inc(steps_apart, 1)
                        layer_parameters(i)
                    if name == "small":
                        piece(name, i, (lambda s: small8(s)[:, :, 0:16], win[:, :, C_LR:C_LR + 16]),
                              (lambda s: small8(s)[:, :, 16:24], win[:, :, C_DT:C_DT + 8]))
                    else:
                        c0 = at[name[:-2]] + 256 * int(name[-1])
                        piece(name, i, (whole8, win[:, :, c0:c0 + 256]))
                wa = d["ada_w_2"][i].rearrange("(c p) n -> p c n", p=P)
                wo = d["w_out"][i].rearrange("(c p) n -> p c n", p=P)
                for name in ada_wo_pieces + wo_pieces[3:]:
                    if name in ada_pieces:
                        a = ada_pieces.index(name)
                        piece(name, i, (whole8, wa[:, :, 256 * a:256 * a + 256]))
                    else:
                        j = wo_pieces.index(name)
                        piece(name, i, (whole2, wo[:, 2 * j:2 * j + 2, :]))
                wg = d["w_ffn_gate"][i].rearrange("(c p) n -> p c n", p=P)
                wu = d["w_ffn_up"][i].rearrange("(c p) n -> p c n", p=P)
                for j, name in enumerate(gu_pieces):
                    piece(name, i, (lambda s: whole8(s)[:, :, 0:P], wg[:, :, P * j:P * j + P]),
                          (lambda s: whole8(s)[:, :, P:2 * P], wu[:, :, P * j:P * j + P]))
                wd = d["w_ffn_down"][i].rearrange("(c p) n -> p c n", p=P)
                for j, name in enumerate(dn_pieces):
                    piece(name, i, (whole2, wd[:, 2 * j:2 * j + 2, :]))
                wp = d["ple_w_proj"][i].rearrange("(c p) n -> p c n", p=P)
                wpg = d["ple_w_gate"][i].rearrange("(c p) n -> p c n", p=P)
                for k, name in enumerate(ple_pieces):
                    if k < 4:
                        piece(name, i, (lambda s: whole2(s[:, 0:512]), wp[:, :, 256 * k:256 * k + 256]))
                    else:
                        piece(name, i, (whole8, wpg[:, :, 256 * (k - 4):256 * (k - 4) + 256]))
            second_sp(sp)

        @block.gpsimd
        def _(pool):
            pool.dma_start(posi[:], d["positions"][0].rearrange("(t p) -> p t", p=P)).then_inc(loaded_pos, 16)
            pool.dma_start(scc3[:, :, 0], d["c_2"][0].rearrange("(c p) -> p c", p=P)).then_inc(loaded_c, 16)
            pool.dma_start(scc3[:, :, 1], d["c_ctx_2"].rearrange("(c p) -> p c", p=P)).then_inc(loaded_c, 16)
            second_pool_early(pool)
            with pool.Fori(0, DEPTH) as i:
                pool.dma_start(p_attn, cols("attn_norm", i)).then_inc(loaded_attn, 16)
                for name in w_in_pieces[:3]:
                    split_low(pool, G, name, i)
                e_h.wait(pool, i, 0)
                pool.sem_inc(steps_apart, 1)
                G.memset(gqA_to_gkB, 0.0)
                G.memset(kTz, 0.0)
                e_zero0.set(G.memset(xbc3[:, :, 0:3], 0.0))
                pool.dma_start(q3(ptok, NT), d["p"][i, 0].rearrange("(t p) n -> p t n", p=P)).then_inc(loaded_p, 16)
                e_aT.wait(pool, i, 2)
                pool.sem_inc(steps_apart, 1)
                e_zero0.set(G.memset(kinvz, 0.0))
                for name in w_in_pieces[6:]:
                    split_low(pool, G, name, i)
                e_win.wait(pool, i)
                pool.sem_inc(steps_apart, 1)
                e_zero1.set(G.memset(Sz, 0.0))
                for name in wo_pieces + gu_pieces[:3] + ple_pieces:
                    split_low(pool, G, name, i)
            second_pool(pool)

        @block.scalar
        def _(act):
            act.wait_ge(sin_in, 1)
            A.activation(sinr, sinr, ACT.Sin)
            A.activation(cosr, cosr, ACT.Sin).then_inc(sin_out, 1)
            act.wait_ge(loaded_c, 32)
            A.activation(scc, scc, ACT.Silu).then_inc(silu_c, 1)
            act.wait_ge(loaded_h, 16)
            with act.Fori(0, DEPTH) as i:
                def squares(k, turn):
                    e_h.wait(act, i, turn)
                    for t in range(NT):
                        A.activation(junk[:, t * D:(t + 1) * D], h3[:, t, :], ACT.Square, accum_out=ss[:, t:t + 1])
                    e_ss.set(act.drain())

                def gemm_copy(name, dst, event, func=ACT.Copy):
                    GEMM.wait_filled(act, name, i)
                    GEMM.release(A.activation(dst, GEMM.buf(name).rearrange("p (t n) -> p t n", t=dst.shape[1]), func), name)
                    event.set(act.drain())

                squares(0, 0)
                for name in w_in_pieces[:3]:
                    split_high(act, name, i)
                def q_and_k():
                    M.wait_filled(act, "qT", i)
                    M.release(A.copy(qT, M.buf("qT")), "qT")
                    e_qT.set(act.drain())
                    M.wait_filled(act, "kT", i)
                    e_zero0.wait(act, i, 1)
                    kTb = M.buf("kT").rearrange("p (c n) -> p c n", c=4)
                    A.copy(kTz4[0:64, :, 0, :], kTb[0:64])
                    M.release(A.copy(kTz4[64:128, :, 1, :], kTb[64:128]), "kT")
                    e_kT.set(act.drain())

                def modulation_rows(k):
                    M.wait_filled(act, f"mod{k}", i)
                    M.release(A.copy(mod_rows[0:2, :], M.buf(f"mod{k}")[0:2, 0:768]), f"mod{k}")
                    e_mrow.set(act.drain())

                def silu_conv():
                    e_conv.wait(act, i)
                    e_xs.set(A.activation(xc, xc, ACT.Silu))

                def gate_logs():
                    e_abs.wait(act, i)
                    A.activation(gax, gax, ACT.Exp, scale=-1.0)
                    A.activation(dtl, dtl, ACT.Exp, scale=-1.0)
                    A.activation(aneg, p_alog, ACT.Exp)
                    A.activation(lam[:, 2:4], lam[:, 0:2], ACT.Exp)
                    act.drain()
                    A.activation(gax, gax, ACT.Ln, bias=1.0)
                    A.activation(dtl, dtl, ACT.Ln, bias=1.0)
                    e_ln.set(act.drain())

                def gla_exps():
                    e_bc.wait(act, i)
                    A.activation(geb, gax, ACT.Exp)
                    A.activation(gx, gax, ACT.Exp, scale=-1.0)
                    A.activation(gei, gei, ACT.Exp)
                    e_gexp.set(act.drain())

                def ssd_exps():
                    e_dtx.wait(act, i)
                    A.activation(dte, dte, ACT.Exp)
                    A.activation(ecum, cum[:, 8:16], ACT.Exp)
                    e_dte.set(act.drain())

                def score_exp(r):
                    e_sub.wait(act, i, r + 1)
                    e_sexp.set(A.activation(sc, sc, ACT.Exp, scale=DQK ** -0.5))

                def segment_exp(t):
                    e_seg.wait(act, i, t + 1)
                    seg = big[:, t * 1024:(t + 1) * 1024]
                    e_segx.set(A.activation(seg, seg, ACT.Exp))

                def segment_exps():
                    segment_exp(0)
                    segment_exp(1)

                behind = dict(gqk_1=q_and_k, dav_0=silu_conv, dav_1=gate_logs, gv_0=gla_exps, gv_1=lambda: score_exp(0), z_0=ssd_exps,
                              gg_0=lambda: score_exp(1), gg_1=segment_exps)
                evacuations = dict(daq_1=("daq", qk_jt[:, :, 0, :], e_qkin), dak_1=("dak", qk_jt[:, :, 1, :], e_qkin),
                                   xbc0_1=("xbc0", xbc3[:, 0:4, 3:], e_xbcin), xbc1_1=("xbc1", xbc3[:, 4:8, 3:], e_xbcin),
                                   gqk_1=("gqk", gqk3, e_gqk), dav_1=("dav", dav3, e_dav), gv_1=("gv", gv3, e_gv),
                                   z_1=("z", sz3, e_sz, ACT.Silu), gg_1=("gg", sg3, e_sg, ACT.Silu))
                for k, name in enumerate(w_in_pieces):
                    if name in evacuations:
                        gemm_copy(*evacuations[name])
                    if name == "small":
                        M.wait_filled(act, "small", i)
                        b = M.buf("small")
                        A.copy(dtx, b[:, 0:16])
                        A.copy(lrT[0:GLA_R, :], b[0:GLA_R, 256:512])
                        M.release(A.copy(pT, b[:, 512:1024]), "small")
                        e_small.set(act.drain())
                    if k + 3 < len(w_in_pieces):
                        split_high(act, w_in_pieces[k + 3], i)
                    if name in behind:
                        behind[name]()
                score_exp(2)
                M.wait_filled(act, "state", i)
                M.release(A.copy(st, M.buf("state")[:, 0:512]), "state")
                e_st.set(act.drain())
                M.wait_filled(act, "kendT", i)
                M.release(A.copy(kendT, M.buf("kendT")[:, 0:768]), "kendT")
                e_kendT.set(act.drain())
                modulation_rows(0)
                M.wait_filled(act, "attT0", i)
                M.release(A.copy(at0T, M.buf("attT0")[:, 0:512]), "attT0")
                e_atT.set(act.drain())
                for name in wo_pieces[:2]:
                    split_high(act, name, i)
                M.wait_filled(act, "attT1", i)
                M.release(A.copy(at1T, M.buf("attT1")), "attT1")
                e_atT.set(act.drain())

                def mixed_high(k):
                    M.wait_filled(act, f"mix{k}", i)
                    A.copy(rounded(mixT[:, k * 1024:(k + 1) * 1024]), M.buf(f"mix{k}"))
                    e_mixT.set(act.drain())

                modulation_rows(1)
                modulation_rows(2)
                split_high(act, wo_pieces[2], i)
                mixed_high(0)
                modulation_rows(3)
                mixed_high(1)
                mixed_high(2)
                for name in wo_pieces[3:] + gu_pieces[:2]:
                    split_high(act, name, i)
                squares(1, 1)
                split_high(act, gu_pieces[2], i)
                later = gu_pieces + dn_pieces + ple_pieces
                for k in range(3, len(gu_pieces) + 3):
                    j = (k - 3) // 2
                    if k % 2 == 0:
                        GEMM.wait_filled(act, f"gu{j}", i)
                        e_sgate.set(A.activation(sgate[:, (j % 2) * 512:(j % 2) * 512 + 512], GEMM.buf(f"gu{j}")[:, 0:512], ACT.Silu))
                    split_high(act, later[k], i)
                for k in range(len(gu_pieces) + 3, len(later)):
                    if later[k] == "pleg0_0":
                        for t in range(NT):
                            GEMM.wait_filled(act, f"pp_t{t}", i)
                            GEMM.release(A.copy(pp[:, t * 1024:(t + 1) * 1024], GEMM.buf(f"pp_t{t}")), f"pp_t{t}")
                            e_pp.set(act.drain())
                    split_high(act, later[k], i)
                for n in range(2):
                    GEMM.wait_filled(act, f"pleg{n}", i)
                    e_pused.wait(act, i, n)
                    GEMM.release(A.activation(psig, GEMM.buf(f"pleg{n}"), ACT.Sigmoid), f"pleg{n}")
                    e_psig.set(act.drain())
            second_act(act)

        @block.tensor
        def _(pe):
            pe.wait_ge(loaded_const, 16)
            pe.wait_ge(loaded_h, 16)
            pe.wait_ge(silu_c, 1)
            with pe.Fori(0, DEPTH) as i:
                def mm(out_, lhsT, rhs, first=True, last=True):
                    return T.matmul(out_, lhsT, rhs, start=first, stop=last)

                def tr(out_, in_):
                    return T.transpose(out_, in_, ident)

                def norm_transposes(names, src):
                    for a, name in enumerate(names):
                        M.wait_free(pe, name, i)
                        for c in range(4):
                            for t in range(NT):
                                last = tr(M.buf(name)[:, c * S + t * P:c * S + (t + 1) * P],
                                          src[:, t, (4 * a + c) * P:(4 * a + c + 1) * P])
                        M.done(last)

                def triple(out_, lhsT, rhs, first, last):
                    (lh, ll), (rh, rl) = lhsT, rhs
                    mm(out_, lh, rl, first, False)
                    mm(out_, ll, rh, False, False)
                    return mm(out_, lh, rh, False, last)

                def part(pair, *at):
                    return tuple(x[at] for x in pair)

                def weights(name, chunks, width):
                    SPLIT.wait_low(pe, name, i)
                    return tuple(x[:, 0:chunks * width].rearrange("p (c n) -> p c n", c=chunks) for x in (SPLIT.hi(name), SPLIT.lo(name)))

                def weights_used():
                    SPLIT.used(pe.drain())

                every = slice(None)

                def halves(turn):
                    for half in range(2 if turn is not None else 1):
                        if turn is not None:
                            e_aT.wait(pe, i, 2 * turn + half + 1)
                        yield range(KC) if turn is None else range(half * KC // 2, (half + 1) * KC // 2)

                def tokens_by_columns(name, a_T, turn=None):
                    for hf in range(2):
                        wt = weights(f"{name}_{hf}", KC, 256)
                        if hf == 0:
                            GEMM.wait_free(pe, name, i)
                        for chunks in halves(turn if hf == 0 else None):
                            for t in range(NT):
                                for c in chunks:
                                    last = triple(GEMM.buf(name)[:, t * 512 + hf * 256:t * 512 + (hf + 1) * 256],
                                                  part(a_T, every, c, slice(t * P, (t + 1) * P)), part(wt, every, c), c == 0, c == KC - 1)
                        if hf:
                            GEMM.done(last)
                        weights_used()

                def columns_by_tokens(name, a_T, places, turn=None):
                    for hf in range(2):
                        wt = weights(f"{name}_{hf}", KC, 256)
                        if hf == 0:
                            GEMM.wait_free(pe, name, i)
                        for chunks in halves(turn if hf == 0 else None):
                            for f in range(2):
                                at = places[2 * hf + f]
                                for c in chunks:
                                    last = triple(GEMM.buf(name)[:, at * S:(at + 1) * S], part(wt, every, c, slice(f * P, (f + 1) * P)),
                                                  part(a_T, every, c), c == 0, c == KC - 1)
                        if hf:
                            GEMM.done(last)
                        weights_used()

                def rows_to_width(turns, pieces, lhs):
                    for name in turns:
                        GEMM.wait_free(pe, name, i)
                    k = 0
                    for name in pieces:
                        wt = weights(name, 2, D)
                        for c in range(2):
                            for t in range(NT):
                                for b in range(2):
                                    last = triple(GEMM.buf(turns[t])[:, b * 512:(b + 1) * 512], part(lhs, every, k, slice(t * P, (t + 1) * P)),
                                                  part(wt, every, c, slice(b * 512, (b + 1) * 512)), k == 0, k == 2 * len(pieces) - 1)
                                if k == 2 * len(pieces) - 1:
                                    GEMM.done(last)
                            k += 1
                        weights_used()

                e_xn.wait(pe, i, 1)
                norm_transposes(("norm0a", "norm0b"), xn3)
                tokens_by_columns("daq", A_IN, 0)
                tokens_by_columns("dak", A_IN)
                columns_by_tokens("xbc0", A_IN, range(4))
                columns_by_tokens("xbc1", A_IN, range(4))
                M.wait_free(pe, "small", i)
                pe.wait_ge(loaded_p, 16 * i + 16)
                wt = weights("small", KC, 24)
                b = M.buf("small")
                for t in range(NT):
                    for c in range(KC):
                        triple(b[:, t * 8:t * 8 + 8], part(A_IN, every, c, slice(t * P, (t + 1) * P)), part(wt, every, c, slice(16, 24)), c == 0, c == KC - 1)
                for c in range(KC):
                    triple(b[0:GLA_R, 256:512], part(wt, every, c, slice(0, GLA_R)), part(A_IN, every, c), c == 0, c == KC - 1)
                weights_used()
                for c in range(2):
                    for t in range(NT):
                        last = tr(b[:, 512 + c * S + t * P:512 + c * S + (t + 1) * P], q3(ptok, NT)[:, t, c * P:(c + 1) * P])
                M.done(last)
                def modulation(k):
                    M.wait_free(pe, f"mod{k}", i)
                    for a in range(3 * k, 3 * k + 3):
                        W.wait_ready(pe, f"ada{a}", i)
                        wt = W.slot(f"ada{a}").rearrange("p (c n) -> p c n", c=KC)
                        for c in range(KC):
                            last = mm(M.buf(f"mod{k}")[0:2, (a % 3) * 256:(a % 3 + 1) * 256], scc3[:, c, :], wt[:, c, :], c == 0, c == KC - 1)
                        if a % 3 == 2:
                            M.done(last)
                        W.used(pe.drain(), f"ada{a}")

                def modulation_columns(k):
                    e_mrow.wait(pe, i, k + 1)
                    M.wait_free(pe, f"modT{k}", i)
                    for c in range(6):
                        last = mm(M.buf(f"modT{k}")[:, 2 * c:2 * c + 2], mod_rows[0:2, c * P:(c + 1) * P], ident[0:2, 0:2])
                    M.done(last)

                def scores(name, maps, t):
                    M.wait_free(pe, name, i)
                    keys = (t + 1) * P
                    for k, m_ in enumerate(maps):
                        last = mm(M.buf(name)[:, k * keys:(k + 1) * keys], qT3[:, m_ // 2, t * P:(t + 1) * P],
                                  kTz4[:, m_ // 2, m_ % 2, 0:keys])
                    M.done(last)

                def running_rows(t):
                    e_ux.wait(pe, i, t + 1)
                    M.wait_free(pe, f"cumb{t}", i)
                    for b_ in range(2):
                        last = mm(M.buf(f"cumb{t}")[:, b_ * 512:(b_ + 1) * 512], ones, big[:, t * 1024 + b_ * 512:t * 1024 + (b_ + 1) * 512])
                    M.done(last)

                columns_by_tokens("gqk", A_IN, range(4))
                e_qk.wait(pe, i)
                for name, j in (("qT", 0), ("kT", 1)):
                    M.wait_free(pe, name, i)
                    for c in range(4):
                        for t in range(NT):
                            last = tr(M.buf(name)[:, c * S + t * P:c * S + (t + 1) * P], qk_jt[:, t, j, c * P:(c + 1) * P])
                    M.done(last)
                M.wait_free(pe, "gate", i)
                e_small.wait(pe, i)
                pe.wait_ge(loaded_prm, 16 * N_PRM * i + 16 * N_PRM)
                for c in range(2):
                    last = mm(M.buf("gate")[:, c * S:(c + 1) * S], p_wg2[0:GLA_R, c * P:(c + 1) * P], lrT[0:GLA_R, :])
                M.done(last)
                tokens_by_columns("dav", A_IN)
                e_xs.wait(pe, i)
                M.wait_free(pe, "xsT", i)
                for t in range(NT):
                    for c in range(4):
                        last = tr(M.buf("xsT")[:, t * 512 + c * P:t * 512 + (c + 1) * P], xc3[:, c, t * P:(t + 1) * P])
                M.done(last)
                e_qT.wait(pe, i)
                e_kT.wait(pe, i)
                scores("score0", range(HC), 0)
                tokens_by_columns("gv", A_IN)
                e_dta.wait(pe, i)
                M.wait_free(pe, "bcum", i)
                b = M.buf("bcum")
                for g in range(2):
                    tr(b[:, g * P:(g + 1) * P], xc3[:, 4 + g, 0:P])
                for t in range(NT):
                    mm(b[:, 512 + t * 8:520 + t * 8], upper, dta[:, t * 8:t * 8 + 8])
                M.done(mm(b[:, 528:536], ones, dta[:, 0:8]))
                scores("score1", range(0, HC // 2), 1)
                tokens_by_columns("z", A_IN)
                running_rows(0)
                running_rows(1)
                tokens_by_columns("gg", A_IN)
                e_win.set(pe.drain())

                M.wait_free(pe, "cb", i)
                for t in range(NT):
                    for g in range(2):
                        last = mm(M.buf("cb")[:, (2 * t + g) * P:(2 * t + g + 1) * P], xc3[:, 4 + g, t * P:(t + 1) * P],
                                  xc3[:, 6 + g, t * P:(t + 1) * P])
                M.done(last)
                scores("score2", range(HC // 2, HC), 1)
                e_xde.wait(pe, i)
                M.wait_free(pe, "state", i)
                for g in range(2):
                    last = mm(M.buf("state")[:, g * 256:(g + 1) * 256], bmT[:, g * P:(g + 1) * P], xde[:, g * 256:(g + 1) * 256])
                M.done(last)
                e_gops.wait(pe, i)
                M.wait_free(pe, "kendT", i)
                for c, (src, t) in enumerate(((gkA, 0), (gkB, 0), (gkA, 1))):
                    for f in range(2):
                        last = tr(M.buf("kendT")[:, c * 256 + f * P:c * 256 + (f + 1) * P], src[:, f * S + t * P:f * S + (t + 1) * P])
                M.done(last)
                modulation(0)
                M.wait_free(pe, "gla_att", i)
                for t in range(NT):
                    for hd in range(GLA_H):
                        last = mm(M.buf("gla_att")[:, (t * 4 + hd) * P:(t * 4 + hd + 1) * P],
                                  kinvz[:, hd * S + t * P:hd * S + (t + 1) * P], gqd[:, (hd // 2) * S + t * P:(hd // 2) * S + (t + 1) * P])
                M.done(last)
                e_attn.wait(pe, i, 1)
                M.wait_free(pe, "attT0", i)
                for hd in range(DA_H):
                    last = tr(M.buf("attT0")[:, hd * P:(hd + 1) * P], attn[:, hd * P:(hd + 1) * P])
                M.done(last)
                modulation_columns(0)
                e_kendT.wait(pe, i)
                e_gv.wait(pe, i)
                for name, chunks in (("gla_st0", (0, 1)), ("gla_st1", (2,))):
                    M.wait_free(pe, name, i)
                    for k, c in enumerate(chunks):
                        for f in range(2):
                            last = mm(M.buf(name)[:, k * 512 + f * 256:k * 512 + (f + 1) * 256], kendT[:, c * 256 + f * P:c * 256 + (f + 1) * P],
                                      gv3[:, c // 2, f * 256:(f + 1) * 256])
                    M.done(last)
                e_attn.wait(pe, i, 3)
                M.wait_free(pe, "attT1", i)
                for hd in range(DA_H):
                    for kt in range(NT):
                        last = tr(M.buf("attT1")[:, kt * 512 + hd * P:kt * 512 + (hd + 1) * P],
                                  attn[:, 512 + hd * 256 + kt * P:512 + hd * 256 + (kt + 1) * P])
                M.done(last)
                e_atT.wait(pe, i)
                e_dav.wait(pe, i)
                M.wait_free(pe, "pv", i)
                b = M.buf("pv")
                for hd in range(DA_H):
                    mm(b[:, hd * DV:(hd + 1) * DV], at0T[:, hd * P:(hd + 1) * P], dav3[:, 0, hd * DV:(hd + 1) * DV])
                for hd in range(DA_H):
                    for kt in range(NT):
                        last = mm(b[:, 512 + hd * DV:512 + (hd + 1) * DV], at1T[:, kt * 512 + hd * P:kt * 512 + (hd + 1) * P],
                                  dav3[:, kt, hd * DV:(hd + 1) * DV], kt == 0, kt == NT - 1)
                M.done(last)
                modulation(1)
                e_mt.wait(pe, i)
                M.wait_free(pe, "ydiag", i)
                for t in range(NT):
                    for hd in range(SSD_H):
                        last = mm(M.buf("ydiag")[:, t * 512 + hd * 64:t * 512 + (hd + 1) * 64], big[:, t * 1024 + hd * P:t * 1024 + (hd + 1) * P],
                                  xdt[:, t * 512 + hd * 64:t * 512 + (hd + 1) * 64])
                M.done(last)
                e_st.wait(pe, i)
                M.wait_free(pe, "yoff", i)
                for g in range(2):
                    last = mm(M.buf("yoff")[:, g * 256:(g + 1) * 256], xc3[:, 6 + g, P:2 * P], st[:, g * 256:(g + 1) * 256])
                M.done(last)
                modulation_columns(1)
                modulation(2)
                e_gat.wait(pe, i)
                e_S.wait(pe, i)
                M.wait_free(pe, "gla_out", i)
                for t in range(NT):
                    for hd in range(GLA_H):
                        o_ = M.buf("gla_out")[:, t * 512 + hd * P:t * 512 + (hd + 1) * P]
                        at = (hd // 2) * S + t * P
                        mm(o_, gatT[:, (t * 4 + hd) * P:(t * 4 + hd + 1) * P], gv3[:, t, hd * P:(hd + 1) * P], True, False)
                        if t > 0:
                            mm(o_, gqA[:, at:at + P], Sz5[:, 2 * t - 1, hd // 2, hd % 2, :], False, False)
                        last = mm(o_, gqB[:, at:at + P], Sz5[:, 2 * t, hd // 2, hd % 2, :], False, True)
                M.done(last)

                def mixed_transposes(k):
                    e_mixed.wait(pe, i, k + 1)
                    M.wait_free(pe, f"mix{k}", i)
                    for c in range(4):
                        for t in range(NT):
                            last = tr(M.buf(f"mix{k}")[:, c * S + t * P:c * S + (t + 1) * P], mix3[:, t, k * 512 + c * P:k * 512 + (c + 1) * P])
                    M.done(last)

                mixed_transposes(0)
                modulation_columns(2)
                modulation(3)
                mixed_transposes(1)
                modulation_columns(3)
                mixed_transposes(2)
                e_mixTlo.wait(pe, i)
                rows_to_width(("wo_t0", "wo_t1"), wo_pieces, MIX_T)

                e_xn.wait(pe, i, 2)
                norm_transposes(("norm1a", "norm1b"), xn3)
                for j in range(FC // 2):
                    columns_by_tokens(f"gu{j}", A_LATER, (0, 2, 1, 3), None if j else 1)
                e_gu.wait(pe, i)
                rows_to_width(("dn_t0", "dn_t1"), dn_pieces, GU)

                for t in range(NT):
                    GEMM.wait_free(pe, f"pp_t{t}", i)
                for k in range(4):
                    wt = weights(f"plep{k}", 2, 256)
                    for t in range(NT):
                        for c in range(2):
                            last = triple(GEMM.buf(f"pp_t{t}")[:, k * 256:(k + 1) * 256], part(P_T, every, c, slice(t * P, (t + 1) * P)),
                                          part(wt, every, c), c == 0, c == 1)
                        if k == 3:
                            GEMM.done(last)
                    weights_used()
                e_h.wait(pe, i, 2)
                norm_transposes(("hT_a", "hT_b"), h3)
                tokens_by_columns("pleg0", A_LATER, 2)
                tokens_by_columns("pleg1", A_LATER)
            second_pe(pe)

        def bc(ap, shape, *axes):
            for a in axes:
                ap = ap.unsqueeze(a)
            return ap.to_broadcast([P, *shape])

        def rsqrt(dve, y, x, tmp):
            V.tensor_scalar(tmp.bitcast(i32), x.bitcast(i32), 1, None, ALU.logical_shift_right)
            dve.drain()
            V.tensor_scalar(y.bitcast(i32), tmp.bitcast(i32), -1.0, float(0x5F3759DF), ALU.mult, ALU.add)
            dve.drain()
            for _ in range(3):
                V.tensor_tensor(tmp, y, y, ALU.mult)
                dve.drain()
                V.scalar_tensor_tensor(tmp, tmp, -0.5, x, ALU.mult, ALU.mult)
                dve.drain()
                V.scalar_tensor_tensor(y, tmp, 1.5, y, ALU.add, ALU.mult)
                dve.drain()

        def group_rstd(dve, y, sq, groups, width, x=None):
            V.tensor_reduce(n_a[:, 0:groups], sq.rearrange("p (g e) -> p g e", g=groups), AX.X, ALU.add)
            dve.drain()
            V.tensor_scalar(n_b[:, 0:groups], n_a[:, 0:groups], 1.0 / width, EPS, ALU.mult, ALU.add)
            dve.drain()
            rsqrt(dve, y, n_b[:, 0:groups], n_a[:, 0:groups])

        @block.vector
        def _(dve):
            dve.wait_ge(loaded_const, 16)
            dve.wait_ge(loaded_pos, 16)
            V.tensor_copy(posf[:, 0:NT], posi[:])
            dve.drain()
            ang, turns_ = rtmp[:, 0:16], rtmp[:, 16:32]
            for t in range(NT):
                V.tensor_scalar(ang[:, t * 8:t * 8 + 8], C["inv_freq"], posf[:, t:t + 1], None, ALU.mult)
            dve.drain()
            big_ = 1.5 * 2.0 ** 23
            V.tensor_scalar(turns_, ang, 1.0 / (2 * math.pi), big_, ALU.mult, ALU.add)
            dve.drain()
            V.tensor_scalar(turns_, turns_, big_, None, ALU.subtract)
            dve.drain()
            c1 = 6.28125
            c2 = round((2 * math.pi - c1) * 2.0 ** 20) / 2.0 ** 20
            c3 = 2 * math.pi - c1 - c2
            for c_ in (c1, c2, c3):
                V.scalar_tensor_tensor(ang, turns_, -c_, ang, ALU.mult, ALU.add)
                dve.drain()
            lim = 3.1415925
            V.tensor_scalar(sinr, ang, lim, -lim, ALU.min, ALU.max)
            V.tensor_scalar(ang, ang, math.pi / 2, None, ALU.add)
            dve.drain()
            V.tensor_scalar(turns_, ang, math.pi, -2 * math.pi, ALU.is_gt, ALU.mult)
            dve.drain()
            V.tensor_tensor(ang, ang, turns_, ALU.add)
            dve.drain()
            V.tensor_scalar(cosr, ang, lim, -lim, ALU.min, ALU.max).then_inc(sin_in, 1)
            dve.wait_ge(sin_out, 1)
            dve.wait_ge(loaded_h, 16)

            with dve.Fori(0, DEPTH) as i:
                def release(ins, name):
                    M.release(ins, name)

                def norm_rows(turn):
                    e_ss.wait(dve, i, turn)
                    V.tensor_scalar(n_b[:, 0:NT], ss, 1.0 / D, EPS, ALU.mult, ALU.add)
                    dve.drain()
                    rsqrt(dve, rstd, n_b[:, 0:NT], n_a[:, 0:NT])
                    for t in range(NT):
                        V.tensor_scalar(xn3[:, t, :], h3[:, t, :], rstd[:, t:t + 1], None, ALU.mult)
                    e_xn.set(dve.drain())

                def columns_in(names, gain, a_T):
                    hi, lo = a_T
                    for a, name in enumerate(names):
                        M.wait_filled(dve, name, i)
                        src = q3(M.buf(name), 4)
                        for c in range(4):
                            k = 4 * a + c
                            if gain is None:
                                V.tensor_copy(hi[:, k, :], src[:, c, :])
                            else:
                                V.tensor_scalar(hi[:, k, :], src[:, c, :], gain[:, k:k + 1], None, ALU.mult)
                        dve.drain()
                        for c in range(4):
                            k = 4 * a + c
                            last = V.scalar_tensor_tensor(lo[:, k, :], src[:, c, :], 1.0 if gain is None else gain[:, k:k + 1],
                                                          hi[:, k, :].bitcast(f32), ALU.mult, ALU.subtract)
                        release(last, name)
                        e_aT.set(dve.drain())

                norm_rows(1)
                dve.wait_ge(loaded_attn, 16 * i + 16)
                columns_in(("norm0a", "norm0b"), p_attn, A_IN)
                for name in w_in_pieces[3:6]:
                    split_low(dve, V, name, i)

                e_qkin.wait(dve, i)
                dve.wait_ge(loaded_prm, 16 * N_PRM * i + 16 * N_PRM)
                V.tensor_tensor(big, qk, qk, ALU.mult)
                dve.drain()
                group_rstd(dve, n_c, big, 32, DQK)
                V.tensor_tensor(q3(qk, 32), q3(qk, 32), bc(n_c, [32, DQK], 2), ALU.mult)
                dve.drain()
                for t in range(NT):
                    V.tensor_tensor(qk5[:, t], qk5[:, t], bc(q3(p_qkg, 2), [2, HC, DQK], 2), ALU.mult)
                dve.drain()
                for t in range(NT):
                    x = qk5[:, t].rearrange("p j c e -> p (j c) e")
                    x1, x2 = x[:, :, 0:8], x[:, :, 8:16]
                    cs, sn = (bc(v[:, t * 8:t * 8 + 8], [16, 8], 1) for v in (cosr, sinr))
                    r = [q3(rtmp[:, k * 128:(k + 1) * 128], 16) for k in range(4)]
                    V.tensor_tensor(r[0], x1, cs, ALU.mult)
                    V.tensor_tensor(r[1], x2, sn, ALU.mult)
                    V.tensor_tensor(r[2], x2, cs, ALU.mult)
                    V.tensor_tensor(r[3], x1, sn, ALU.mult)
                    dve.drain()
                    V.tensor_tensor(x1, r[0], r[1], ALU.subtract)
                    V.tensor_tensor(x2, r[2], r[3], ALU.add)
                    dve.drain()
                e_qk.set(dve.drain())

                e_xbcin.wait(dve, i)
                e_zero0.wait(dve, i, 1)
                for c in range(8):
                    V.tensor_scalar(xc3[:, c, :], xbc3[:, c, 3:], convw3[:, 3, c:c + 1], p_convb[:, c:c + 1], ALU.mult, ALU.add)
                dve.drain()
                for j in range(3):
                    for c in range(8):
                        V.scalar_tensor_tensor(xc3[:, c, :], xbc3[:, c, j:j + S], convw3[:, j, c:c + 1], xc3[:, c, :], ALU.mult, ALU.add)
                    dve.drain()
                e_conv.set(dve.drain())

                lv = p_lam.rearrange("p (a b e) -> p a b e", a=2, b=2)
                V.tensor_tensor(q3(lamp, 2), lv[:, :, 0, :], lv[:, :, 1, :], ALU.mult)
                V.tensor_scalar(p_sub, p_sub, p_li[:, 1:2], None, ALU.mult)
                e_small.wait(dve, i)
                V.tensor_tensor(q3(dtx, NT), q3(dtx, NT), bc(p_dtb, [NT, SSD_H], 1), ALU.add)
                M.wait_filled(dve, "gate", i)
                for c in range(2):
                    last = V.tensor_scalar(gx[:, c * S:(c + 1) * S], M.buf("gate")[:, c * S:(c + 1) * S], p_bgate[:, c:c + 1], None, ALU.add)
                release(last, "gate")
                dve.drain()
                V.tensor_reduce(lam[:, 0:2], q3(lamp, 2), AX.X, ALU.add)
                V.tensor_scalar(dtl.bitcast(i32), dtx.bitcast(i32), 0x7FFFFFFF, None, ALU.bitwise_and)
                V.tensor_scalar(gax.bitcast(i32), gx.bitcast(i32), 0x7FFFFFFF, None, ALU.bitwise_and)
                e_abs.set(dve.drain())
                e_ln.wait(dve, i)
                V.scalar_tensor_tensor(gx, gx, 0.0, gax, ALU.min, ALU.subtract)
                V.scalar_tensor_tensor(dtx, dtx, 0.0, dtl, ALU.max, ALU.add)
                V.tensor_tensor(lam[:, 0:1], lam[:, 2:3], lam[:, 3:4], ALU.subtract)
                dve.drain()
                V.tensor_scalar(gx, gx, 1.0 / 16.0, None, ALU.mult)
                V.scalar_tensor_tensor(q3(dta, NT), q3(dtx, NT), -1.0, bc(aneg, [NT, SSD_H], 1), ALU.mult, ALU.mult)
                V.tensor_scalar(lam[:, 0:1], lam[:, 0:1], p_li[:, 0:1], None, ALU.add)
                e_dta.set(dve.drain())
                for c in range(8):
                    V.tensor_tensor_scan(gax[:, c * 64:(c + 1) * 64], ones[:, 0:64], gx[:, c * 64:(c + 1) * 64], 0.0, ALU.mult, ALU.add)
                dve.drain()
                b8 = q3(gax, 8)
                V.tensor_tensor(q3(gei, 8), b8[:, :, 63:64].to_broadcast([P, 8, 64]), b8, ALU.subtract)
                e_bc.set(dve.drain())

                def modulation_in(k):
                    M.wait_filled(dve, f"modT{k}", i)
                    src = M.buf(f"modT{k}")[:, 0:12].rearrange("p (c s) -> p c s", s=2)
                    M.release(V.tensor_tensor(mods4[:, bass.ds(i, 1), 6 * k:6 * k + 6, :].rearrange("p i c s -> p (i c) s"), src,
                                              bc(p_adab[:, 6 * k:6 * k + 6], [6, 2], 2), ALU.add), f"modT{k}")

                def softmax(r):
                    name, n, keys, at = (("score0", 8, P, 0), ("score1", 4, 2 * P, 512), ("score2", 4, 2 * P, 1024))[r]
                    s3 = q3(sc, n)
                    M.wait_filled(dve, name, i)
                    mask = C["causal"][:, 2 * P - keys:2 * P]
                    release(V.tensor_tensor(s3, q3(M.buf(name), n), bc(mask, [n, keys], 1), ALU.add), name)
                    dve.drain()
                    V.tensor_reduce(mx[:, 0:n], s3, AX.X, ALU.max)
                    dve.drain()
                    V.tensor_tensor(s3, s3, bc(mx[:, 0:n], [n, keys], 2), ALU.subtract)
                    e_sub.set(dve.drain())
                    return s3, n, keys, at

                def softmax_end(r, s3, n, keys, at):
                    e_sexp.wait(dve, i, r + 1)
                    V.tensor_reduce(dsum[:, 0:n], s3, AX.X, ALU.add)
                    dve.drain()
                    V.reciprocal(wgt[:, 0:n], dsum[:, 0:n])
                    dve.drain()
                    odd = q3(wgt[:, 0:n], n // 2)[:, :, 1:2]
                    V.tensor_scalar(odd, odd, lam[:, 0:1], -1.0, ALU.mult, ALU.mult)
                    dve.drain()
                    V.tensor_tensor(s3, s3, bc(wgt[:, 0:n], [n, keys], 2), ALU.mult)
                    dve.drain()
                    s4 = s3.rearrange("p (a r) k -> p a r k", r=2)
                    V.tensor_tensor(q3(attn[:, at:at + n // 2 * keys], n // 2), s4[:, :, 0, :], s4[:, :, 1, :], ALU.add)
                    e_attn.set(dve.drain())

                def segment(t):
                    seg = big[:, t * 1024:(t + 1) * 1024]
                    M.wait_filled(dve, f"cumb{t}", i)
                    release(V.tensor_tensor(q3(seg, 8), q3(M.buf(f"cumb{t}"), 8), bc(cum[:, t * 8:t * 8 + 8], [8, P], 2), ALU.subtract), f"cumb{t}")
                    dve.drain()
                    e_seg.set(V.tensor_scalar(seg, seg, 0.0, None, ALU.min))

                def ssd_map(t):
                    seg = big[:, t * 1024:(t + 1) * 1024]
                    e_segx.wait(dve, i, t + 1)
                    s4 = seg.rearrange("p (g r l) -> p g r l", g=2, r=4)
                    e_mt.set(V.tensor_tensor(s4, s4, bc(q3(cbm[:, t * 256:(t + 1) * 256], 2), [2, 4, P], 2), ALU.mult))

                M.wait_filled(dve, "xsT", i)
                V.tensor_tensor(q3(xdt, 16), q3(M.buf("xsT"), 16), bc(dtx, [16, SSD_P], 2), ALU.mult)
                release(V.tensor_copy(xh, M.buf("xsT")), "xsT")
                sm = softmax(0)
                M.wait_filled(dve, "bcum", i)
                b = M.buf("bcum")
                V.tensor_copy(bmT, b[:, 0:256])
                V.tensor_copy(cum, b[:, 512:528])
                dve.drain()
                release(V.tensor_tensor(dte, b[:, 528:536], cum[:, 0:8], ALU.subtract), "bcum")
                e_dtx.set(dve.drain())
                for t in range(NT):
                    e_ux.set(V.tensor_tensor(q3(big[:, t * 1024:(t + 1) * 1024], 8), bc(upper, [8, P], 1),
                                             bc(dta[:, t * 8:t * 8 + 8], [8, P], 2), ALU.mult))
                softmax_end(0, *sm)
                sm = softmax(1)
                e_dte.wait(dve, i)
                e_xde.set(V.tensor_tensor(q3(xde, 8), q3(xdt[:, 0:512], 8), bc(dte, [8, SSD_P], 2), ALU.mult))

                e_gexp.wait(dve, i)
                e_gqk.wait(dve, i)
                e_zero0.wait(dve, i, 2)
                gq, gk = gqk[:, 0:512], gqk[:, 512:1024]
                V.scalar_tensor_tensor(gqd, gq, GLA_K ** -0.5, geb, ALU.mult, ALU.mult)
                kz = kinvz.rearrange("p (a r n) -> p a r n", a=2, r=2)
                for r in range(2):
                    pr = slice(r * 64, r * 64 + 64)
                    V.tensor_tensor(kz[pr, :, r, :], q3(gk, 2)[pr], q3(gx, 2)[pr], ALU.mult)
                halves = lambda ap: ap.rearrange("p (n c l) -> p n c l", c=2, l=64)
                for c, dst in ((0, gkA), (1, gkB)):
                    V.tensor_tensor(halves(dst)[:, :, c, :], halves(gk)[:, :, c, :], halves(gei)[:, :, c, :], ALU.mult)
                dve.drain()
                for c, dst in ((0, gqA), (1, gqB)):
                    V.tensor_copy(halves(dst)[:, :, c, :], halves(gqd)[:, :, c, :])
                e_gops.set(dve.drain())

                segment(0)
                segment(1)
                softmax_end(1, *sm)
                e_win.wait(dve, i)
                M.wait_filled(dve, "cb", i)
                release(V.tensor_tensor(q3(cbm, 4), q3(M.buf("cb")[:, 0:512], 4), bc(upper, [4, P], 1), ALU.mult), "cb")
                sm = softmax(2)
                ssd_map(0)
                ssd_map(1)
                softmax_end(2, *sm)

                M.wait_filled(dve, "gla_att", i)
                release(V.tensor_tensor(q3(gatT, 8), q3(M.buf("gla_att"), 8), bc(C["chunk_upper"], [8, P], 1), ALU.mult), "gla_att")
                e_gat.set(dve.drain())
                modulation_in(0)
                e_zero1.wait(dve, i)
                for c, (name, at) in enumerate((("gla_st0", 0), ("gla_st0", 512), ("gla_st1", 0))):
                    if c != 1:
                        M.wait_filled(dve, name, i)
                    for a in range(2):
                        for r in range(2):
                            pr = slice(r * 64, r * 64 + 64)
                            src = M.buf(name)[pr, at + a * 256 + r * P:at + a * 256 + (r + 1) * P]
                            if c == 0:
                                last = V.tensor_copy(Sz5[pr, c, a, r, :], src)
                            else:
                                end = a * S + c * 64 + 63
                                last = V.scalar_tensor_tensor(Sz5[pr, c, a, r, :], Sz5[pr, c - 1, a, r, :], geb[pr, end:end + 1],
                                                              src, ALU.mult, ALU.add)
                    if c > 0:
                        release(last, name)
                    dve.drain()
                e_S.set(dve.drain())

                def head_norm(x4, width, sq):
                    n = NT * x4.shape[2]
                    V.tensor_tensor(sq.rearrange("p (t a e) -> p t a e", t=NT, e=width), x4, x4, ALU.mult)
                    dve.drain()
                    group_rstd(dve, n_c[:, 0:n], sq, n, width)
                    V.tensor_tensor(x4, x4, bc(q3(n_c[:, 0:n], NT), list(x4.shape[1:]), 3), ALU.mult)
                    dve.drain()

                M.wait_filled(dve, "pv", i)
                o = mix3[:, :, 0:512]
                release(V.tensor_copy(o, q3(M.buf("pv"), NT)), "pv")
                dve.drain()
                o4 = o.rearrange("p t (a e) -> p t a e", e=DV)
                head_norm(o4, DV, sc)
                V.tensor_tensor(o4, o4, bc(p_sub, [NT, DA_H, DV], 1, 1), ALU.mult)
                e_mixed.set(dve.drain())

                y = mix3[:, :, 512:1024]
                y4 = y.rearrange("p t (a e) -> p t a e", e=SSD_P)
                V.tensor_tensor(y4, xh.rearrange("p (t a e) -> p t a e", t=NT, e=SSD_P),
                                bc(p_dskip, [NT, SSD_H, SSD_P], 1, 3), ALU.mult)
                dve.drain()
                M.wait_filled(dve, "ydiag", i)
                release(V.tensor_tensor(y, y, q3(M.buf("ydiag"), NT), ALU.add), "ydiag")
                M.wait_filled(dve, "yoff", i)
                release(V.tensor_tensor(q3(sc[:, 0:512], 8), q3(M.buf("yoff")[:, 0:512], 8), bc(ecum, [8, SSD_P], 2), ALU.mult), "yoff")
                dve.drain()
                modulation_in(1)
                V.tensor_tensor(y[:, 1, :], y[:, 1, :], sc[:, 0:512], ALU.add)
                dve.drain()
                e_sz.wait(dve, i)
                V.tensor_tensor(y, y, sz3, ALU.mult)
                dve.drain()
                head_norm(y.rearrange("p t (a e) -> p t a e", e=256), 256, sc)
                V.tensor_tensor(y, y, bc(p_ssdn, [NT, 512], 1), ALU.mult)
                e_mixed.set(dve.drain())

                def low_mixed(k):
                    e_mixT.wait(dve, i, k + 1)
                    cs = slice(k * 1024, (k + 1) * 1024)
                    release(V.tensor_tensor(rounded(low_mixT[:, cs]), M.buf(f"mix{k}"), rounded(mixT[:, cs]).bitcast(f32), ALU.subtract), f"mix{k}")
                    e_mixTlo.set(dve.drain())

                M.wait_filled(dve, "gla_out", i)
                o = mix3[:, :, 1024:1536]
                release(V.tensor_copy(o, q3(M.buf("gla_out"), NT)), "gla_out")
                dve.drain()
                low_mixed(0)
                modulation_in(2)
                o4 = o.rearrange("p t (a e) -> p t a e", e=GLA_V)
                head_norm(o4, GLA_V, sc)
                V.tensor_tensor(o4, o4, bc(p_glan, [NT, GLA_H, GLA_V], 1, 1), ALU.mult)
                dve.drain()
                e_sg.wait(dve, i)
                V.tensor_tensor(o, o, sg3, ALU.mult)
                e_mixed.set(dve.drain())

                low_mixed(1)
                modulation_in(3)
                low_mixed(2)

                def add_to_h(names):
                    for t, name in enumerate(names):
                        GEMM.wait_filled(dve, name, i)
                        GEMM.release(V.tensor_tensor(h3[:, t, :], h3[:, t, :], GEMM.buf(name), ALU.add), name)
                    e_h.set(dve.drain())

                add_to_h(("wo_t0", "wo_t1"))
                norm_rows(2)
                columns_in(("norm1a", "norm1b"), p_ffn, A_LATER)
                V.tensor_copy(rounded(p_hi), pT)
                dve.drain()
                V.tensor_tensor(rounded(p_lo), pT, rounded(p_hi).bitcast(f32), ALU.subtract)
                dve.drain()
                later = gu_pieces + dn_pieces + ple_pieces
                for k in range(3, len(gu_pieces) + 3):
                    j = (k - 3) // 2
                    if k % 2 == 0:
                        name = f"gu{j}"
                        act_up = sgate[:, (j % 2) * 512:(j % 2) * 512 + 512]
                        cs = slice(2 * j * S, (2 * j + 2) * S)
                        e_sgate.wait(dve, i, j + 1)
                        V.tensor_tensor(act_up, act_up, GEMM.buf(name)[:, 512:1024], ALU.mult)
                        dve.drain()
                        V.tensor_copy(rounded(gu[:, cs]), act_up)
                        dve.drain()
                        GEMM.release(V.tensor_tensor(rounded(low_gu[:, cs]), act_up, rounded(gu[:, cs]).bitcast(f32), ALU.subtract), name)
                        e_gu.set(dve.drain())
                    split_low(dve, V, later[k], i)
                for name in dn_pieces[3:]:
                    split_low(dve, V, name, i)
                add_to_h(("dn_t0", "dn_t1"))
                columns_in(("hT_a", "hT_b"), None, A_LATER)
                e_pp.wait(dve, i)
                for n in range(2):
                    e_psig.wait(dve, i, n + 1)
                    s3, hn = q3(psig, NT), h3[:, :, n * 512:(n + 1) * 512]
                    V.tensor_tensor(s3, s3, q3(pp, NT)[:, :, n * 512:(n + 1) * 512], ALU.mult)
                    dve.drain()
                    V.tensor_tensor(hn, hn, s3, ALU.add)
                    e_pused.set(dve.drain())
                e_h.set(dve.drain())
            second_dve(dve)


_INS = ["x", "p", "positions", "attn_norm", "w_in", "da_q_norm", "da_k_norm", "da_lambda_q1", "da_lambda_k1",
        "da_lambda_q2", "da_lambda_k2", "da_sub_norm", "ssd_conv_w", "ssd_conv_b", "ssd_dt_bias", "ssd_a_log", "ssd_d",
        "ssd_norm", "gla_w_gate2", "gla_b_gate", "gla_norm", "w_out", "ffn_norm", "w_ffn_gate", "w_ffn_up", "w_ffn_down",
        "ple_w_proj", "ple_w_gate", "c_2", "ctx_2", "c_ctx_2", "ada_w_2", "ada_b_2", "norm_pre_2", "norm_post_2",
        "hg_w_in_2", "hg_o_norm_2", "hg_w_out_2", "mla_w_in_2", "mla_qa_norm_2", "mla_w_qb_2", "mla_kva_norm_2",
        "mla_w_kvb_2", "mla_w_out_2"]


def kernel(**inputs):
    import concourse.bacc as bacc
    from concourse.bass_utils import run_bass_kernel_spmd

    nc = bacc.Bacc("TRN2", target_bir_lowering=False, num_devices=1)
    arrays = {name: np.ascontiguousarray(inputs[name]) for name in _INS}
    arrays["cst"], arrays["hmask"], arrays["lam"] = constants()
    d, feed = {}, {}
    for name, a in arrays.items():
        feed[f"in_{name}"] = a
        d[name] = nc.dram_tensor(f"in_{name}", a.shape, mybir.dt.from_np(a.dtype), kind="ExternalInput").ap()
    out = nc.dram_tensor("out_0", (1, S, D), mybir.dt.float32, kind="ExternalOutput").ap()
    program(nc, d, out)
    result = run_bass_kernel_spmd(nc, [feed], core_ids=[0])
    return result.results[0]["out_0"]
```
